# Optimizing a Trainium2 kernel written in Bass

```python
import jax, jax.numpy as jnp
from jax import lax
import numpy as np

D_MODEL = 1024
BATCH = 1
SEQ = 1024
DEPTH = 1

N_MIXERS = 2
N_MEM = 256
MIX_WIDTH = 3 * D_MODEL // 4
MEM_HEADS = 4
MEM_HEAD_DIM = D_MODEL // 16
MEM_WIDTH = MEM_HEADS * MEM_HEAD_DIM
CHUNK = 64
GLA_HEADS = 4
GLA_KEY_WIDTH = D_MODEL // 2
GLA_DK = GLA_KEY_WIDTH // GLA_HEADS
GLA_DV = MIX_WIDTH // GLA_HEADS
GLA_GATE_RANK = 16
GLA_GATE_NORMALIZER = 16.0
GLA_IN_WIDTH = 2 * GLA_KEY_WIDTH + 2 * MIX_WIDTH + GLA_GATE_RANK + MEM_WIDTH
HG_EXPAND = 128
HG_HEADS = MIX_WIDTH // HG_EXPAND
HG_DK = HG_EXPAND
HG_DV = MIX_WIDTH // HG_HEADS
HG_IN_WIDTH = 4 * MIX_WIDTH + MEM_WIDTH
N_GROUPS = 4
EXPERTS_PER_GROUP = 4
N_EXPERTS = N_GROUPS * EXPERTS_PER_GROUP
EXPERT_FF = 256
TOP_K_IN_GROUP = 2
NORM_EPS = 1e-6

kernel_name = 'hybrid_gla_hgrn2_memxattn_hmoe'

def rms_norm(x, gain):
    xf = x.astype(jnp.float32)
    y = xf * lax.rsqrt(jnp.mean(xf * xf, axis=-1, keepdims=True) + NORM_EPS)
    return (y * gain.astype(jnp.float32)).astype(x.dtype)

def split_cols(a, sizes):
    offsets, acc = [], 0
    for s in sizes[:-1]:
        acc += s
        offsets.append(acc)
    return jnp.split(a, offsets, axis=-1)

def chunk_gated_linear_attention(q, k, v, log_decay):
    B, T, H, K = q.shape
    V = v.shape[-1]
    n_chunks = T // CHUNK

    def to_chunks(a):
        return a.astype(jnp.float32).reshape(B, n_chunks, CHUNK, H, a.shape[-1]).transpose(1, 0, 3, 2, 4)

    qc, kc, vc, gc = to_chunks(q), to_chunks(k), to_chunks(v), to_chunks(log_decay)
    bc = jnp.cumsum(gc, axis=-2)
    causal = jnp.tril(jnp.ones((CHUNK, CHUNK), dtype=bool))[:, :, None]

    def step(state, inp):
        q_, k_, v_, b_ = inp
        diff = b_[..., :, None, :] - b_[..., None, :, :]
        decay = jnp.exp(jnp.where(causal, diff, -jnp.inf))
        scores = jnp.sum(q_[..., :, None, :] * k_[..., None, :, :] * decay, axis=-1)
        out = scores @ v_ + (q_ * jnp.exp(b_)) @ state
        b_last = b_[..., -1:, :]
        state = state * jnp.exp(b_last).swapaxes(-1, -2) + (k_ * jnp.exp(b_last - b_)).swapaxes(-1, -2) @ v_
        return state, out

    state0 = jnp.zeros((B, H, K, V), jnp.float32)
    _, out = lax.scan(step, state0, (qc, kc, vc, bc))
    return out.transpose(1, 0, 3, 2, 4).reshape(B, T, H, V).astype(v.dtype)

def gla_mixer(u, w_in, w_gate_up, b_gate, out_gain):
    B, T, _ = u.shape
    proj = u @ w_in
    q, k, v, g, r, mq = split_cols(proj, [GLA_KEY_WIDTH, GLA_KEY_WIDTH, MIX_WIDTH, MIX_WIDTH, GLA_GATE_RANK, MEM_WIDTH])
    q = q.reshape(B, T, GLA_HEADS, GLA_DK) * (GLA_DK ** -0.5)
    k = k.reshape(B, T, GLA_HEADS, GLA_DK)
    v = v.reshape(B, T, GLA_HEADS, GLA_DV)
    gate_logit = (r @ w_gate_up + b_gate).astype(jnp.float32)
    log_decay = (jax.nn.log_sigmoid(gate_logit) / GLA_GATE_NORMALIZER).reshape(B, T, GLA_HEADS, GLA_DK)
    o = chunk_gated_linear_attention(q, k, v, log_decay)
    o = rms_norm(o, out_gain) * jax.nn.silu(g.reshape(B, T, GLA_HEADS, GLA_DV))
    return o.reshape(B, T, MIX_WIDTH), mq

def hgrn2_mixer(u, w_in, lower_bound, out_gain):
    B, T, _ = u.shape
    proj = u @ w_in
    q, f, i, g, mq = split_cols(proj, [MIX_WIDTH, MIX_WIDTH, MIX_WIDTH, MIX_WIDTH, MEM_WIDTH])
    q = jax.nn.silu(q).reshape(B, T, HG_HEADS, HG_DK)
    z = f.astype(jnp.float32).reshape(B, T, HG_HEADS, HG_DK)
    lb = lower_bound.reshape(HG_HEADS, HG_DK)
    log_f = jnp.logaddexp(jnp.log(lb), jnp.log1p(-lb) + jax.nn.log_sigmoid(z))
    one_minus_f = (1.0 - lb) * jax.nn.sigmoid(-z)
    i = i.reshape(B, T, HG_HEADS, HG_DV)
    o = chunk_gated_linear_attention(q, one_minus_f, i, log_f)
    o = rms_norm(o, out_gain) * jax.nn.silu(g.reshape(B, T, HG_HEADS, HG_DV))
    return o.reshape(B, T, MIX_WIDTH), mq

def memory_cross_attention(mq, mem_n, w_mem_kv):
    B, T, _ = mq.shape
    kv = mem_n @ w_mem_kv
    k, v = split_cols(kv, [MEM_WIDTH, MEM_WIDTH])
    k = k.reshape(B, N_MEM, MEM_HEADS, MEM_HEAD_DIM)
    v = v.reshape(B, N_MEM, MEM_HEADS, MEM_HEAD_DIM)
    q = mq.reshape(B, T, MEM_HEADS, MEM_HEAD_DIM)
    s = jnp.einsum('bthd,bmhd->bhtm', q, k).astype(jnp.float32) * (MEM_HEAD_DIM ** -0.5)
    p = jax.nn.softmax(s, axis=-1).astype(v.dtype)
    o = jnp.einsum('bhtm,bmhd->bthd', p, v)
    return o.reshape(B, T, MEM_WIDTH)

def hierarchical_moe(u, w_group, b_group, w_router, b_router, w_up, w_down):
    B, T, D = u.shape
    t = u.reshape(B * T, D)
    n_tok = t.shape[0]
    g_logits = (t @ w_group + b_group).astype(jnp.float32)
    g_prob = jax.nn.softmax(g_logits, axis=-1)
    g_idx = jnp.argmax(g_logits, axis=-1)
    g_w = jnp.take_along_axis(g_prob, g_idx[:, None], axis=-1)
    e_logits = (t @ w_router + b_router).astype(jnp.float32).reshape(n_tok, N_GROUPS, EXPERTS_PER_GROUP)
    e_in_group = jnp.take_along_axis(e_logits, g_idx[:, None, None], axis=1)[:, 0]
    top_v, top_i = lax.top_k(e_in_group, TOP_K_IN_GROUP)
    top_w = jax.nn.softmax(top_v, axis=-1) * g_w
    expert_id = g_idx[:, None] * EXPERTS_PER_GROUP + top_i
    gates = jnp.einsum('nk,nke->ne', top_w, jax.nn.one_hot(expert_id, N_EXPERTS, dtype=jnp.float32))
    h = jnp.einsum('nd,edf->nef', t, w_up)
    a, b = split_cols(h, [EXPERT_FF, EXPERT_FF])
    h = jax.nn.silu(a) * b * gates[..., None].astype(h.dtype)
    y = jnp.einsum('nef,efd->nd', h, w_down)
    return y.reshape(B, T, D)

def setup_inputs(seed: int = 0) -> dict:
    key = jax.random.key(seed)
    ks = jax.random.split(key, 24)
    n_gla = (DEPTH + N_MIXERS - 1) // N_MIXERS
    n_hg = DEPTH // N_MIXERS

    def nrm(k, shape, scale):
        return jax.random.normal(k, shape, jnp.float32) * scale

    def gain(k, shape):
        return 1.0 + 0.02 * jax.random.normal(k, shape, jnp.float32)

    return {
        'x': nrm(ks[0], (BATCH, SEQ, D_MODEL), 1.0),
        'mem': nrm(ks[1], (BATCH, N_MEM, D_MODEL), 1.0),
        'mix_norm': gain(ks[2], (DEPTH, D_MODEL)),
        'ffn_norm': gain(ks[3], (DEPTH, D_MODEL)),
        'mem_norm': gain(ks[4], (DEPTH, D_MODEL)),
        'final_norm': gain(ks[5], (D_MODEL,)),
        'gla_w_in': nrm(ks[6], (n_gla, D_MODEL, GLA_IN_WIDTH), D_MODEL ** -0.5),
        'gla_w_gate_up': nrm(ks[7], (n_gla, GLA_GATE_RANK, GLA_KEY_WIDTH), GLA_GATE_RANK ** -0.5),
        'gla_b_gate': nrm(ks[8], (n_gla, GLA_KEY_WIDTH), 0.1),
        'gla_out_norm': gain(ks[9], (n_gla, GLA_DV)),
        'hg_w_in': nrm(ks[10], (n_hg, D_MODEL, HG_IN_WIDTH), D_MODEL ** -0.5),
        'hg_lower_bounds': nrm(ks[11], (DEPTH, MIX_WIDTH), 0.1),
        'hg_out_norm': gain(ks[12], (n_hg, HG_DV)),
        'w_mem_kv': nrm(ks[13], (DEPTH, D_MODEL, 2 * MEM_WIDTH), D_MODEL ** -0.5),
        'w_out': nrm(ks[14], (DEPTH, MIX_WIDTH + MEM_WIDTH, D_MODEL), (MIX_WIDTH + MEM_WIDTH) ** -0.5),
        'w_group': nrm(ks[15], (DEPTH, D_MODEL, N_GROUPS), D_MODEL ** -0.5),
        'b_group': nrm(ks[16], (DEPTH, N_GROUPS), 0.01),
        'w_router': nrm(ks[17], (DEPTH, D_MODEL, N_EXPERTS), D_MODEL ** -0.5),
        'b_router': nrm(ks[18], (DEPTH, N_EXPERTS), 0.01),
        'w_up': nrm(ks[19], (DEPTH, N_EXPERTS, D_MODEL, 2 * EXPERT_FF), D_MODEL ** -0.5),
        'w_down': nrm(ks[20], (DEPTH, N_EXPERTS, EXPERT_FF, D_MODEL), EXPERT_FF ** -0.5),
    }

def reference(x, mem, mix_norm, ffn_norm, mem_norm, final_norm, gla_w_in, gla_w_gate_up, gla_b_gate,
              gla_out_norm, hg_w_in, hg_lower_bounds, hg_out_norm, w_mem_kv, w_out, w_group, b_group,
              w_router, b_router, w_up, w_down):
    lb_prob = jax.nn.softmax(hg_lower_bounds.astype(jnp.float32), axis=0)
    lower_bounds = jnp.cumsum(lb_prob, axis=0) - lb_prob[0]
    h = x
    for layer in range(DEPTH):
        u = rms_norm(h, mix_norm[layer])
        j = layer // N_MIXERS
        if layer % N_MIXERS == 0:
            mix, mq = gla_mixer(u, gla_w_in[j], gla_w_gate_up[j], gla_b_gate[j], gla_out_norm[j])
        else:
            mix, mq = hgrn2_mixer(u, hg_w_in[j], lower_bounds[layer], hg_out_norm[j])
        mem_o = memory_cross_attention(mq, rms_norm(mem, mem_norm[layer]), w_mem_kv[layer])
        h = h + jnp.concatenate([mix, mem_o], axis=-1) @ w_out[layer]
        h = h + hierarchical_moe(rms_norm(h, ffn_norm[layer]), w_group[layer], b_group[layer],
                                 w_router[layer], b_router[layer], w_up[layer], w_down[layer])
    return rms_norm(h, final_norm)


_drawn_inputs = setup_inputs


def setup_inputs(seed=0):
    import zlib

    import numpy as np

    out = dict(_drawn_inputs(seed))
    spreads = {}
    factors = {'mem_norm': 8.0,
     'final_norm': 7.313,
     'gla_out_norm': 16.558,
     'b_group': 36.59,
     'b_router': 51.831,
     'ffn_norm': 7.44,
     'gla_b_gate': 2.939}
    for name, (base, spread) in spreads.items():
        noise = np.random.default_rng([zlib.crc32(name.encode()), seed]).standard_normal(out[name].shape)
        drawn = base * np.exp(spread * noise) if base else spread * noise
        out[name] = __import__('jax').numpy.asarray(drawn.astype(out[name].dtype))
    for name, factor in factors.items():
        out[name] = (out[name] * factor).astype(out[name].dtype)
    return out
```

```python
from contextlib import ExitStack

import concourse.bass as bass
from concourse import mybir

P = 128


class Chain:

    def __init__(self, eng, sem):
        self.eng, self.sem, self.base, self.n, self.turn, self.per = eng, sem, 0, 0, 0, 0

    def link(self, ins):
        ins.then_inc(self.sem, 1)
        self.n += 1
        self.eng.wait_ge(self.sem, self.turn * self.per + (self.base + self.n))

    def enter(self, turn, per):
        self.turn, self.per = turn, per

    def leave(self, turns):
        assert self.n - self.start == self.per, (self.n - self.start, self.per)
        self.base += self.per * (turns - 1)
        self.turn = 0

    def mark(self):
        self.start = self.n


def hybrid_layer(nc, x, mem, mix_norm, ffn_norm, mem_norm, final_norm, gla_w_in, gla_w_gate_up,
                 gla_b_gate, gla_out_norm, w_mem_kv, w_out, w_group, b_group, w_router, b_router,
                 w_up, w_down, out):
    f32, f16 = mybir.dt.float32, mybir.dt.float16
    i32, u8 = mybir.dt.int32, mybir.dt.uint8
    ALU, ACT, AX = mybir.AluOpType, mybir.ActivationFunctionType, mybir.AxisListType
    ds = bass.ds

    T, D = x.shape[1], x.shape[2]
    N_MEM = mem.shape[1]
    TILES, KD = T // P, D // P
    HEADS = 4
    KEY = gla_w_gate_up.shape[2]
    RANK = gla_w_gate_up.shape[1]
    DV = gla_out_norm.shape[1]
    MIX = HEADS * DV
    DK = KEY // HEADS
    MEMW = w_mem_kv.shape[2] // 2
    MHEADS = 4
    MHD = MEMW // MHEADS
    MTILES = N_MEM // P
    GROUPS = w_group.shape[2]
    EXPERTS = w_router.shape[2]
    PER = EXPERTS // GROUPS
    FF = w_down.shape[2]
    KF = FF // P
    EPS = 1e-6
    GATE_SCALE = 1.0 / 16.0
    Q_SCALE = DK ** -0.5
    M_SCALE = MHD ** -0.5
    LEVELS = 7
    CHOICES = 2
    BLOCKS = (T * CHOICES + EXPERTS * (P - 1)) // P
    EXTRA = BLOCKS - EXPERTS
    assert DK == P and KD == 8 and T % 512 == 0 and D == 1024

    w_in = gla_w_in[0].rearrange("(k p) n -> p k n", p=P)
    w_kv = w_mem_kv[0].rearrange("(k p) n -> p k n", p=P)
    w_o = w_out[0].rearrange("(k p) n -> p k n", p=P)
    up_rows = w_up[0].rearrange("e (k p) n -> e p k n", p=P)
    down_rows = w_down[0].rearrange("e (k p) n -> e p k n", p=P)
    h_dram = nc.dram_tensor("h_rows", [T, D], f32, kind="Internal").ap()
    u_dram = nc.dram_tensor("u_rows", [T, D], f32, kind="Internal").ap()
    y_dram = nc.dram_tensor("y_rows", [BLOCKS * P, D], f32, kind="Internal").ap()

    with ExitStack() as ctx:
        def sb(name, shape, dt=f32):
            return ctx.enter_context(nc.sbuf_tensor(name, shape, dt))

        def sem(name):
            return ctx.enter_context(nc.semaphore(name))

        def sems(name, n):
            return [sem(f"{name}{i}") for i in range(n)]

        region_a = sb("region_a", [P, KD * T])
        ring = sb("weight_ring", [P, 2, KD, 512])
        acts = sb("activations", [P, 24576])
        mqT = sb("mqT", [P, 2, T])
        fac = sb("fac", [P, 3, 512])
        qk = sb("qk", [P, 2, HEADS, P])
        scoresT = sb("scoresT", [P, HEADS, P])
        q_decayed = sb("q_decayed", [P, HEADS, P])
        k_decayed = sb("k_decayed", [P, HEADS, P])
        k_decayedT = sb("k_decayedT", [P, HEADS, P])
        mq_tile = sb("mq_tile", [P, 2, P])
        state = sb("state", [P, HEADS, DV])
        mix = sb("mix", [P, HEADS, DV])
        gate = sb("gate", [P, HEADS, DV])
        out_gain = sb("out_gain", [P, 1, DV])
        mem_kT = sb("mem_kT", [P, 2, N_MEM])
        mem_v = sb("mem_v", [P, MTILES, MEMW])
        masks = sb("masks", [P, LEVELS + 1, P], u8)
        ident = sb("ident", [P, P])
        w_route = sb("w_route", [P, KD, GROUPS + EXPERTS])
        b_route = sb("b_route", [P, GROUPS + EXPERTS])
        logits = sb("logits", [P, TILES, GROUPS + EXPERTS])
        b_gate = sb("b_gate", [P, HEADS])
        stat = sb("stat", [P, 48])
        minus_half = sb("minus_half", [P, 4])
        eps = sb("eps", [P, 4])
        spare = sb("spare", [P, 2])
        sumsq, meansq, rstd = stat[:, 0:2], stat[:, 2:4], stat[:, 4:6]
        neg_max, row_sum, row_inv = stat[:, 8:12], stat[:, 12:16], stat[:, 16:20]
        o_sumsq, o_meansq, o_rstd = stat[:, 20:24], stat[:, 24:28], stat[:, 28:32]
        h_sumsq, h_meansq, h_rstd = stat[:, 32:33], stat[:, 33:34], stat[:, 34:35]
        decay_all = stat[:, 36:40]

        xT = region_a[:, :].rearrange("p (k t) -> p k t", k=KD)
        qT = acts[:, 0:4096].rearrange("p (h t) -> p h t", h=HEADS)
        kT = acts[:, 4096:8192].rearrange("p (h t) -> p h t", h=HEADS)
        vg = acts[:, 8192:20480].rearrange("p (t n) -> p t n", t=TILES)
        bT = acts[:, 20480:24576].rearrange("p (h t) -> p h t", h=HEADS)
        x_in = acts[:, 8192:10240].rearrange("p (u n) -> p u n", u=2)
        x_norm = acts[:, 10240:12288].rearrange("p (u n) -> p u n", u=2)
        junk = acts[:, 12288:14336].rearrange("p (u n) -> p u n", u=2)
        mix_gain = acts[:, 14336:15360]
        mem_gain = acts[:, 15360:16384]
        memT = acts[:, 20480:22528].rearrange("p (k t) -> p k t", k=KD)
        rT = fac[0:RANK, 0:2, :].rearrange("p u t -> p (u t)")
        w_gate = fac[0:RANK, 2, :]
        log_term = [qk[:, u, :, :].rearrange("p h t -> p (h t)") for u in range(2)]
        min_term = [q_decayed[:, :, :].rearrange("p h t -> p (h t)"),
                    k_decayed[:, :, :].rearrange("p h t -> p (h t)")]
        h_tile, u_tile = region_a[:, 0:1024], region_a[:, 1024:2048]
        uT = region_a[:, 2048:3072].rearrange("p (k t) -> p k t", k=KD)
        catT = region_a[:, 3072:4096].rearrange("p (k t) -> p k t", k=KD)
        probs = region_a[:, 4096:5120].rearrange("p (h m) -> p h m", h=MHEADS)
        probsT = region_a[:, 5120:6144].rearrange("p (h m t) -> p h m t", h=MHEADS, m=MTILES)
        ffn_gain = region_a[:, 6144:7168]
        o_sq = region_a[:, 7168:7168 + MIX].rearrange("p (h d) -> p h d", h=HEADS)

        psum = [ctx.enter_context(nc.psum_tensor(f"bank{b}", [P, 512], f32)) for b in range(8)]

        def heads_of(bank):
            return psum[bank][:, :].rearrange("p (h t) -> p h t", h=HEADS)

        def cols(bank, n, parts):
            return psum[bank][:, 0:n].rearrange("p (a b) -> p a b", a=parts)

        small_loaded, gains_loaded = sem("small_loaded"), sem("gains_loaded")
        out_gain_loaded, ffn_gain_loaded = sem("out_gain_loaded"), sem("ffn_gain_loaded")
        pool_step, dve_step = sem("pool_step"), sem("dve_step")
        ident_built, half_built, state_zero = sem("ident_built"), sem("half_built"), sem("state_zero")
        masks_built = sem("masks_built")
        x_loaded, sumsq_ready, rstd_ready = sems("x_loaded", 2), sems("sumsq_ready", 2), sems("rstd_ready", 2)
        norm_ready, x_transposed = sems("norm_ready", 2), sems("x_transposed", 2)
        xT_low, xT_high = sems("xT_low", 2), sems("xT_high", 2)
        chunk_loaded = sems("chunk_loaded", 2)
        job_filled, job_drained = sems("job_filled", 4), sems("job_drained", 4)
        gate_filled, gate_log, gate_min = sems("gate_filled", 2), sems("gate_log", 2), sems("gate_min", 2)
        gate_summed = sems("gate_summed", 2)
        filled, drained = sems("bank_filled", 8), sems("bank_drained", 8)
        arg_ready, exp_ready, fac_used = sem("arg_ready"), sem("exp_ready"), sems("fac_used", 3)
        kd_ready, mq_ready, decay_ready = sem("kd_ready"), sem("mq_ready"), sem("decay_ready")
        negmax_ready, probs_ready = sem("negmax_ready"), sem("probs_ready")
        tanh_ready, o_sq_ready, o_sumsq_ready = sem("tanh_ready"), sem("o_sq_ready"), sem("o_sumsq_ready")
        o_rstd_ready, mix_ready = sem("o_rstd_ready"), sem("mix_ready")
        x_tile_loaded, h_sumsq_ready, h_rstd_ready = sem("x_tile_loaded"), sem("h_sumsq_ready"), sem("h_rstd_ready")
        u_ready, h_stored, u_stored = sem("u_ready"), sem("h_stored"), sem("u_stored")
        exp_arg, exp_done, ones_built = sem("exp_arg"), sem("exp_done"), sem("ones_built")
        member_ready, rank_filled, hot_ready = sem("member_ready"), sem("rank_filled"), sem("hot_ready")
        hot_used, table_filled, tables_ready = sem("hot_used"), sem("table_filled"), sem("tables_ready")
        w_loaded, y_stored, gathered = sems("w_loaded", 3), sems("y_stored", 3), sems("gathered", 3)
        idx_ready = sem("idx_ready")
        rows_filled, rowsT_low, rowsT_high = sem("rows_filled"), sem("rowsT_low"), sem("rowsT_high")
        up_filled, silu_ready, hid_ready = sem("up_filled"), sem("silu_ready"), sem("hid_ready")
        hidT_filled, hidT_ready, down_filled = sem("hidT_filled"), sem("hidT_ready"), sem("down_filled")
        y_low, y_high = sem("y_low"), sem("y_high")
        final_gain_loaded = sem("final_gain_loaded")
        ya_loaded, yb_loaded, h_loaded = sems("ya_loaded", 2), sems("yb_loaded", 2), sems("h_loaded", 2)
        slot_copied = sem("slot_copied")
        sum_ready, f_sumsq, f_rstd = sem("sum_ready"), sem("f_sumsq"), sem("f_rstd")
        out_ready, out_stored = sem("out_ready"), sems("out_stored", 2)

        CHUNKS = [(w_kv, 0, 512), (w_in, 2 * KEY + 2 * MIX, RANK + MEMW), (w_in, KEY, 512), (w_in, 0, 512),
                  (w_in, 2 * KEY, 512), (w_in, 2 * KEY + 512, 512), (w_in, 2 * KEY + 1024, 512),
                  (w_o, 0, 512), (w_o, 512, 512)]
        JOBS = ([(0, "mem_k", g, 0) for g in range(2)] + [(0, "mem_v", m, 0) for m in range(MTILES)]
                + [(1, "rank", 0, s) for s in range(2)] + [(1, "mem_q", g, s) for g in range(2) for s in range(2)]
                + [(2, "k", h, s) for h in range(HEADS) for s in range(2)]
                + [(3, "q", h, s) for h in range(HEADS) for s in range(2)]
                + [(4 + n, "vg", n, t) for n in range(3) for t in range(TILES)])
        GATES_BEFORE = next(n for n, j in enumerate(JOBS) if j[1] == "q")
        GATE_JOBS = [(h, s) for h in range(HEADS) for s in range(2)]

        def last_job(chunk):
            return max(n for n, j in enumerate(JOBS) if j[0] == chunk)

        w_out_half = [ring[:, 1, :, :], ring[:, 0, :, :]]

        USES = [4, 4, 2, 2, 3, 3, 4, 3]

        rt = region_a

        def small(at, *dims):
            n = 1
            for d in dims:
                n *= d
            v = rt[:, at:at + n]
            if len(dims) == 2:
                return v.rearrange("p (a b) -> p a b", a=dims[0])
            if len(dims) == 3:
                return v.rearrange("p (a b c) -> p a b c", a=dims[0], b=dims[1])
            return v

        W_SLOT = KD * 2 * FF + KF * D
        w_slots = [acts[:, u * W_SLOT:(u + 1) * W_SLOT] for u in range(3)]
        up_w = [w[:, 0:KD * 2 * FF].rearrange("p (k n) -> p k n", k=KD) for w in w_slots]
        down_w = [w[:, KD * 2 * FF:W_SLOT].rearrange("p (k n) -> p k n", k=KF) for w in w_slots]
        at = 3 * W_SLOT
        rows = acts[:, at:at + 3 * D].rearrange("p (u n) -> p u n", u=3)
        rowsT = acts[:, at + 3 * D:at + 6 * D].rearrange("p (u k t) -> p u k t", u=3, k=KD)
        ring_flat = ring[:, :, :, :].rearrange("p u k n -> p (u k n)")
        y_rows = ring_flat[:, 0:3 * D].rearrange("p (u n) -> p u n", u=3)
        silu = ring_flat[:, 3 * D:3 * D + 3 * FF].rearrange("p (u n) -> p u n", u=3)
        hid = ring_flat[:, 3 * D + 3 * FF:3 * D + 6 * FF].rearrange("p (u n) -> p u n", u=3)
        hidT = ring_flat[:, 3 * D + 6 * FF:3 * D + 9 * FF].rearrange("p (u k t) -> p u k t", u=3, k=KF)
        final_gain = ring_flat[:, 6144:7168]
        y_a = acts[:, 0:2 * D].rearrange("p (u n) -> p u n", u=2)
        y_b = acts[:, 2 * D:4 * D].rearrange("p (u n) -> p u n", u=2)
        h_in = acts[:, 4 * D:6 * D].rearrange("p (u n) -> p u n", u=2)
        o_out = acts[:, 6 * D:8 * D].rearrange("p (u n) -> p u n", u=2)
        f_junk = acts[:, 8 * D:10 * D].rearrange("p (u n) -> p u n", u=2)

        G, E, TG, TE = GROUPS, EXPERTS, TILES * GROUPS, TILES * EXPERTS
        g_max, e_top, e_second = small(0, TILES), small(8, TILES), small(16, TILES)
        g_prob, w_first, w_sec, seen = small(24, TILES), small(32, TILES), small(40, TILES), small(48, TILES)
        g_exp, g_hot = small(64, TILES, G), small(96, TILES, G)
        e_in, e_rest = small(128, TILES, PER), small(160, TILES, PER)
        a_hot, b_hot, equal = small(192, TILES, PER), small(224, TILES, PER), small(256, TILES, PER)
        picked = small(320, TILES, G, PER)
        a_all, b_all = small(448, TILES, G, PER), small(576, TILES, G, PER)
        member = small(704, TILES, E)
        carry = small(832, TILES + 1, E)
        rank, code, prod = small(1024, TILES, E), small(1152, TILES, E), small(1280, TILES, E)
        extra, extra_upto, code_low, code_high = small(1408, E), small(1424, E), small(1440, E), small(1456, E)
        slot_f, row_f, block_f = small(1488, 2, TILES), small(1504, 2, TILES), small(1520, 2, TILES)
        token_id = small(1536, TILES)
        weight = small(1552, 2, TILES)
        upto_cmp = small(1600, EXTRA, E)
        block_iota, row_iota = small(1856, BLOCKS), small(1920, P)
        tri = small(2048, P)
        ones = small(2176, P)
        expert_f = small(2304, BLOCKS)
        one_minus = small(2368, E)
        expert_base = small(2384, E)
        ints = rt[:, 2560:3200].bitcast(i32)
        slot_i, row_i, block_i = ints[:, 0:16], ints[:, 16:32], ints[:, 32:48]
        token_table = ints[:, 64:64 + BLOCKS]
        expert_table = ints[:, 128:128 + BLOCKS]
        iota_i = ints[:, 256:256 + P]
        idx_tile = ints[:, 400:403]
        slot_tile = ints[:, 410:414]
        halves = rt[:, 3200:3200 + 1024].bitcast(f16)
        row_hot = [halves[:, u * P:(u + 1) * P] for u in range(2)]
        block_hot = [halves[:, 512 + u * 64:512 + u * 64 + BLOCKS] for u in range(2)]

        def job_result(job, n):
            _, kind, g, s = job
            bank = psum[4 + n % 4]
            half = slice(s * 512, s * 512 + 512)
            if kind == "mem_k":
                return mem_kT[:, g, :], bank[:, 0:N_MEM], 1.0
            if kind == "mem_v":
                return mem_v[:, g, :], bank[:, 0:MEMW], 1.0
            if kind == "rank":
                return rT[:, half], bank[0:RANK, :], 1.0
            if kind == "mem_q":
                return mqT[:, g, half], bank[:, :], 1.0
            if kind == "k":
                return kT[:, g, half], bank[:, :], 1.0
            if kind == "q":
                return qT[:, g, half], bank[:, :], Q_SCALE
            return vg[:, s, g * 512:(g + 1) * 512], bank[:, :], 1.0

        block = ctx.enter_context(nc.Block())

        @block.sync
        def _(sp):
            sp.dma_start(mix_gain, mix_norm[0:1, :].partition_broadcast(P).rearrange("p a n -> p (a n)")).then_inc(gains_loaded, 16)
            sp.dma_start(mem_gain, mem_norm[0:1, :].partition_broadcast(P).rearrange("p a n -> p (a n)")).then_inc(gains_loaded, 16)

            def chunk(c):
                src, at, n = CHUNKS[c]
                if c >= 2:
                    j = last_job(c - 2)
                    sp.wait_ge(job_filled[j % 4], j // 4 + 1)
                sp.dma_start(ring[:, c % 2, :, 0:n], src[:, :, at:at + n]).then_inc(chunk_loaded[c % 2], 16)

            with sp.Fori(0, TILES // 2) as i:
                for u in range(2):
                    sp.wait_ge(norm_ready[u], i)
                    sp.dma_start(x_in[:, u, :], x[0, ds((i * 2 + u) * P, P), :]).then_inc(x_loaded[u], 16)
            for u in range(2):
                sp.wait_ge(norm_ready[u], TILES // 2)
                sp.dma_start(x_in[:, u, :], mem[0, u * P:(u + 1) * P, :]).then_inc(x_loaded[u], 16)
            for c in range(len(CHUNKS)):
                chunk(c)

            sp.wait_ge(job_filled[(len(JOBS) - 1) % 4], (len(JOBS) - 1) // 4 + 1)
            sp.dma_start(ffn_gain, ffn_norm[0:1, :].partition_broadcast(P).rearrange("p a n -> p (a n)")).then_inc(ffn_gain_loaded, 16)
            with sp.Fori(0, TILES) as t:
                sp.wait_ge(h_stored, t * 16)
                sp.wait_ge(u_ready, t)
                sp.dma_start(h_tile, x[0, ds(t * P, P), :]).then_inc(x_tile_loaded, 16)
                sp.wait_ge(drained[2], t * 2 + 2)
                sp.wait_ge(drained[3], t * 2 + 2)
                sp.dma_start(h_dram[ds(t * P, P), :], h_tile).then_inc(h_stored, 16)
                sp.wait_ge(u_ready, t + 1)
                sp.dma_start(u_dram[ds(t * P, P), :], u_tile).then_inc(u_stored, 16)

            sp.wait_ge(tables_ready, 1)

            def load_expert(j, u):
                sp.wait_ge(tables_ready, 1)
                e = sp.value_load(expert_table[0:1, ds(j, 1)], min_val=0, max_val=EXPERTS - 1)
                sp.dma_start(up_w[u], up_rows[ds(e, 1), :, :, :].rearrange("e p k n -> p (e k) n")).then_inc(w_loaded[u], 16)
                sp.dma_start(down_w[u], down_rows[ds(e, 1), :, :, :].rearrange("e p k n -> p (e k) n")).then_inc(w_loaded[u], 16)

            def store_y(j, u):
                sp.wait_ge(y_low, j + 1)
                sp.wait_ge(y_high, j + 1)
                sp.dma_start(y_dram[ds(j * P, P), :], y_rows[:, u, :]).then_inc(y_stored[u], 16)

            for u in range(3):
                load_expert(u, u)
            with sp.Fori(0, (BLOCKS - 4) // 3) as i:
                for u in range(3):
                    sp.wait_ge(down_filled, i * 3 + (u + 1))
                    load_expert(i * 3 + (u + 3), u)
                    store_y(i * 3 + u, u)
            sp.wait_ge(down_filled, BLOCKS - 3)
            load_expert(BLOCKS - 1, 0)
            for j in range(BLOCKS - 4, BLOCKS):
                store_y(j, j % 3)

            for u in range(3):
                sp.wait_ge(y_stored[u], 16 * len(range(u, BLOCKS, 3)))
            sp.dma_start(final_gain, final_norm.rearrange("(a n) -> a n", a=1).partition_broadcast(P).rearrange("p a n -> p (a n)")).then_inc(final_gain_loaded, 16)
            with sp.Fori(0, TILES // 2) as i:
                for u in range(2):
                    sp.wait_ge(out_ready, i * 2)
                    sp.dma_start(h_in[:, u, :], h_dram[ds((i * 2 + u) * P, P), :]).then_inc(h_loaded[u], 16)
                for u in range(2):
                    sp.wait_ge(out_ready, i * 2 + (u + 1))
                    sp.dma_start(out[0, ds((i * 2 + u) * P, P), :], o_out[:, u, :]).then_inc(out_stored[u], 16)
            for u in range(2):
                sp.wait_ge(out_stored[u], 16 * (TILES // 2))

        @block.gpsimd
        def _(pool):
            c = Chain(pool, pool_step)
            pool.dma_start(b_gate[:, :], gla_b_gate[0].rearrange("(h p) -> p h", p=P), allow_slow_non_contiguous=True).then_inc(small_loaded, 16)
            pool.dma_start(w_gate, gla_w_gate_up[0]).then_inc(small_loaded, 16)
            pool.dma_start(out_gain[:, :, :], gla_out_norm[0:1, :].partition_broadcast(P)).then_inc(out_gain_loaded, 16)
            pool.dma_start(w_route[:, :, 0:G], w_group[0].rearrange("(k p) n -> p k n", p=P), allow_slow_non_contiguous=True).then_inc(small_loaded, 16)
            pool.dma_start(w_route[:, :, G:G + E], w_router[0].rearrange("(k p) n -> p k n", p=P), allow_slow_non_contiguous=True).then_inc(small_loaded, 16)
            pool.dma_start(b_route[:, 0:G], b_group[0:1, :].partition_broadcast(P).rearrange("p a n -> p (a n)")).then_inc(small_loaded, 16)
            pool.dma_start(b_route[:, G:G + E], b_router[0:1, :].partition_broadcast(P).rearrange("p a n -> p (a n)")).then_inc(small_loaded, 16)
            mask_rows = acts[:, 16384:16384 + 3 * P].bitcast(i32)
            pool.iota(mask_rows[:, 0:P], [[1, P]], base=0, channel_multiplier=0)
            pool.iota(mask_rows[:, P:2 * P], [[0, P]], base=0, channel_multiplier=1).then_inc(masks_built, 1)
            pool.memset(eps[:, :], EPS)
            pool.memset(minus_half[:, :], -0.5).then_inc(half_built, 1)
            c.link(pool.memset(ident[:, :], 0.0))
            pool.affine_select(out=ident[:, :], in_=ident[:, :], compare_op=ALU.not_equal, fill=1.0, base=0,
                               pattern=[[-1, P]], channel_multiplier=1).then_inc(ident_built, 1)
            pool.wait_ge(half_built, 1)

            def wait_apart(*waits):
                for s, v in waits:
                    pool.wait_ge(s, v)
                pool.tensor_tensor(spare[:, 0:1], minus_half[:, 0:1], minus_half[:, 0:1], ALU.mult)

            def rms(dst, mean, src, width):
                c.link(pool.tensor_tensor(mean, src, eps[:, 0:width], ALU.add))
                return pool.tensor_tensor(dst, mean, minus_half[:, 0:width], ALU.pow)

            def tile_norm(i, u):
                pool.wait_ge(sumsq_ready[u], i + 1)
                rms(rstd[:, u:u + 1], meansq[:, u:u + 1], sumsq[:, u:u + 1], 1).then_inc(rstd_ready[u], 1)

            with pool.Fori(0, TILES // 2) as i:
                c.enter(i, 2)
                c.mark()
                for u in range(2):
                    tile_norm(i, u)
            c.leave(TILES // 2)
            for u in range(2):
                tile_norm(TILES // 2, u)

            for u in range(2):
                pool.wait_ge(gate_summed[u], len(GATE_JOBS) // 2)
            pool.wait_ge(out_gain_loaded, 16)
            c.link(pool.tensor_scalar(out_gain[:, :, :], out_gain[:, :, :], 0.5, None, ALU.mult))
            for b in range(4):
                pool.wait_ge(job_drained[b], len(range(b, len(JOBS), 4)))
            with pool.Fori(0, TILES) as t:
                c.enter(t, 5)
                c.mark()
                bt = bT[:, :, ds(t * P, P)]
                pool.wait_ge(fac_used[0], t * 3)
                f0 = fac[:, 0, :].rearrange("p (h t) -> p h t", h=HEADS)
                pool.tensor_tensor(f0, bt[:, :, P - 1:P].to_broadcast([P, HEADS, P]), bt, ALU.subtract).then_inc(arg_ready, 1)
                for lvl in range(LEVELS):
                    f, s = lvl + 2, (P // 2) >> lvl
                    pool.wait_ge(fac_used[f % 3], t * 3 + f // 3)
                    fh = fac[:, f % 3, :].rearrange("p (h b a s) -> p h b a s", h=HEADS, a=2, s=s)
                    bh = bt.rearrange("p h (b a s) -> p h b a s", a=2, s=s)
                    nb = P // (2 * s)
                    mid = bh[:, :, :, 1, 0:1].to_broadcast([P, HEADS, nb, s])
                    pool.tensor_tensor(fh[:, :, :, 0, :], mid, bh[:, :, :, 0, :], ALU.subtract)
                    pool.tensor_tensor(fh[:, :, :, 1, :], bh[:, :, :, 1, :], mid, ALU.subtract).then_inc(arg_ready, 1)
                g_t = vg[:, ds(t, 1), MIX:2 * MIX].rearrange("p a (h d) -> p (a h) d", h=HEADS)
                wait_apart((tanh_ready, t + 1))
                c.link(pool.tensor_tensor(gate[:, :, :], gate[:, :, :], g_t, ALU.mult))
                wait_apart()
                c.link(pool.tensor_tensor(gate[:, :, :], gate[:, :, :], g_t, ALU.add))
                c.link(pool.tensor_tensor(gate[:, :, :], gate[:, :, :], out_gain[:, :, :].to_broadcast([P, HEADS, DV]), ALU.mult))
                pool.wait_ge(o_sumsq_ready, t + 1)
                rms(o_rstd, o_meansq, o_sumsq, 4).then_inc(o_rstd_ready, 1)
                pool.wait_ge(drained[2], t * 2 + 1)
                pool.wait_ge(drained[3], t * 2 + 1)
                pool.tensor_tensor(mix[:, :, :], mix[:, :, :], gate[:, :, :], ALU.mult).then_inc(mix_ready, 1)
                pool.wait_ge(h_sumsq_ready, t + 1)
                rms(h_rstd, h_meansq, h_sumsq, 1).then_inc(h_rstd_ready, 1)
            c.leave(TILES)

            pool.wait_ge(filled[7], TILES * USES[7])
            pool.wait_ge(u_stored, 16 * TILES)
            pool.wait_ge(h_stored, 16 * TILES)
            c.link(pool.memset(ones, 1.0))
            c.link(pool.affine_select(out=tri, in_=ones, compare_op=ALU.is_gt, fill=0.0, base=0,
                                      pattern=[[1, P]], channel_multiplier=-1))
            c.link(pool.iota(iota_i[:, 0:P], [[1, P]], base=0, channel_multiplier=0))
            c.link(pool.tensor_copy(row_iota, iota_i[:, 0:P]))
            c.link(pool.tensor_copy(block_iota, iota_i[:, 0:BLOCKS]))
            c.link(pool.tensor_scalar(expert_base, iota_i[:, 0:E], float(P), None, ALU.mult))
            c.link(pool.iota(iota_i[:, 0:TILES], [[P, TILES]], base=0, channel_multiplier=1))
            pool.tensor_copy(token_id, iota_i[:, 0:TILES]).then_inc(ones_built, 1)

            pool.wait_ge(tables_ready, 1)

            def gather(j, u):
                pool.tensor_copy(idx_tile[:, u:u + 1], token_table[:, ds(j, 1)]).then_inc(idx_ready, 1)
                wait_apart((idx_ready, j + 1))
                pool.indirect_dma_start(rows[:, u, :], None, u_dram, bass.IndirectOffsetOnAxis(idx_tile[:, u:u + 1], 0)).then_inc(gathered[u], 16)

            for u in range(3):
                gather(u, u)
            with pool.Fori(0, (BLOCKS - 4) // 3) as i:
                for u in range(3):
                    pool.wait_ge(gathered[u], i * 16 + 16)
                    pool.wait_ge(rows_filled, i * 3 + (u + 1))
                    gather(i * 3 + (u + 3), u)
            pool.wait_ge(gathered[0], 16 * ((BLOCKS - 1) // 3))
            pool.wait_ge(rows_filled, BLOCKS - 3)
            gather(BLOCKS - 1, 0)

            for u in range(3):
                pool.wait_ge(y_stored[u], 16 * len(range(u, BLOCKS, 3)))
            with pool.Fori(0, TILES // 2) as i:
                c.enter(i, 2)
                c.mark()
                for u in range(2):
                    pool.wait_ge(out_ready, i * 2)
                    pool.wait_ge(ya_loaded[u], i * 16)
                    pool.wait_ge(yb_loaded[u], i * 16)
                    for choice, dst, loaded in ((0, y_a, ya_loaded), (1, y_b, yb_loaded)):
                        pool.tensor_copy(slot_tile[:, 2 * u + choice:2 * u + choice + 1],
                                         slot_i[:, ds(i * 2 + (u + choice * TILES), 1)]).then_inc(slot_copied, 1)
                        wait_apart((slot_copied, i * 4 + (2 * u + choice + 1)))
                        pool.indirect_dma_start(dst[:, u, :], None, y_dram,
                                                bass.IndirectOffsetOnAxis(slot_tile[:, 2 * u + choice:2 * u + choice + 1], 0)).then_inc(loaded[u], 16)
                for u in range(2):
                    pool.wait_ge(f_sumsq, i * 2 + (u + 1))
                    rms(rstd[:, u:u + 1], meansq[:, u:u + 1], sumsq[:, u:u + 1], 1).then_inc(f_rstd, 1)
            c.leave(TILES // 2)

        @block.scalar
        def _(act):
            def square_tile(i, u):
                act.wait_ge(x_loaded[u], i * 16 + 16)
                act.activation(junk[:, u, :], x_in[:, u, :], ACT.Square, scale=D ** -0.5, accum_out=sumsq[:, u:u + 1]).then_inc(sumsq_ready[u], 1)

            def evac_low(i, u, dst):
                act.wait_ge(x_transposed[u], i + 1)
                act.activation(dst, cols(2 * u, 512, 4), ACT.Copy).then_inc(xT_low[u], 1)

            with act.Fori(0, TILES // 2) as i:
                for u in range(2):
                    square_tile(i, u)
                for u in range(2):
                    evac_low(i, u, xT[:, 0:4, ds((i * 2 + u) * P, P)])
            for u in range(2):
                square_tile(TILES // 2, u)
            for u in range(2):
                evac_low(TILES // 2, u, memT[:, 0:4, u * P:(u + 1) * P])

            act.wait_ge(small_loaded, 16 * 6)
            for n, job in enumerate(JOBS):
                if n == GATES_BEFORE:
                    for m, (h, s) in enumerate(GATE_JOBS):
                        u = m % 2
                        act.wait_ge(gate_min[u], m // 2 + 1)
                        if m >= 2:
                            act.wait_ge(gate_summed[u], m // 2)
                        act.activation(log_term[u], psum[2 + u][:, :], ACT.Abs, bias=b_gate[:, h:h + 1]).then_inc(gate_log[u], 1)
                        act.wait_ge(gate_log[u], m // 2 * 3 + 1)
                        act.activation(log_term[u], log_term[u], ACT.Exp, scale=-1.0).then_inc(gate_log[u], 1)
                        act.wait_ge(gate_log[u], m // 2 * 3 + 2)
                        act.activation(log_term[u], log_term[u], ACT.Ln, bias=1.0).then_inc(gate_log[u], 1)
                if n % 2 == 0:
                    act.wait_ge(job_filled[n % 4], n // 4 + 1)
                    dst, src, scale = job_result(job, n)
                    act.activation(dst, src, ACT.Copy, scale=scale).then_inc(job_drained[n % 4], 1)

            for u in range(2):
                act.wait_ge(gate_summed[u], len(GATE_JOBS) // 2)
            for b in (1, 3):
                act.wait_ge(job_drained[b], len(range(b, len(JOBS), 4)))
            with act.Fori(0, TILES) as t:
                bt = bT[:, :, ds(t * P, P)]

                def level_exp(f):
                    act.wait_ge(arg_ready, t * 8 + f)
                    act.activation(fac[:, f % 3, :], fac[:, f % 3, :], ACT.Exp, scale=GATE_SCALE).then_inc(exp_ready, 1)

                act.wait_ge(arg_ready, t * 8 + 1)
                act.activation(fac[:, 0, :], fac[:, 0, :], ACT.Exp, scale=GATE_SCALE).then_inc(exp_ready, 1)
                act.wait_ge(fac_used[1], t * 3)
                act.activation(fac[:, 1, :].rearrange("p (h t) -> p h t", h=HEADS), bt, ACT.Exp, scale=GATE_SCALE).then_inc(exp_ready, 1)
                act.wait_ge(drained[5], t * 3)
                act.activation(decay_all.unsqueeze(2), bt[:, :, P - 1:P], ACT.Exp, scale=GATE_SCALE).then_inc(decay_ready, 1)
                act.wait_ge(filled[6], t * 4 + 1)
                act.wait_ge(filled[5], t * 3)
                act.activation(k_decayedT[:, :, :], heads_of(6), ACT.Copy).then_inc(drained[6], 1)
                for f in (2, 3, 4):
                    level_exp(f)
                act.wait_ge(negmax_ready, t + 1)
                act.wait_ge(probs_ready, t)
                act.wait_ge(filled[5], t * 3)
                for h in range(MHEADS):
                    ins = act.activation(probs[:, h, :], cols(4 + h // 2, 512, 2)[:, h % 2, :], ACT.Exp,
                                         bias=neg_max[:, h:h + 1], scale=M_SCALE, accum_out=row_sum[:, h:h + 1])
                    if h % 2:
                        ins.then_inc(drained[4 + h // 2], 1)
                for f in range(5, 9):
                    level_exp(f)
                g_t = vg[:, ds(t, 1), MIX:2 * MIX].rearrange("p a (h d) -> p (a h) d", h=HEADS)
                act.wait_ge(mix_ready, t)
                act.activation(gate[:, :, :], g_t, ACT.Tanh, scale=0.5).then_inc(tanh_ready, 1)
                act.wait_ge(o_sumsq_ready, t)
                for b in (2, 3):
                    act.wait_ge(filled[b], t * 2 + 1)
                    ins = act.activation(o_sq[:, 2 * (b - 2):2 * (b - 1), :], cols(b, 2 * DV, 2), ACT.Square, scale=DV ** -0.5)
                ins.then_inc(o_sq_ready, 1)
                act.wait_ge(filled[5], t * 3 + 3)
                act.wait_ge(filled[6], t * 4)
                act.activation(probsT[:, 2:4, :, :].rearrange("p h m t -> p (h m) t"), heads_of(5), ACT.Copy).then_inc(drained[5], 1)
                act.wait_ge(filled[6], t * 4 + 3)
                act.wait_ge(filled[3], t * 2)
                act.activation(catT[:, 0:4, :], heads_of(6), ACT.Copy).then_inc(drained[6], 1)
                act.wait_ge(drained[2], t * 2 + 2)
                act.wait_ge(drained[3], t * 2 + 2)
                act.activation(probs[:, :, :].rearrange("p h m -> p (h m)"), h_tile, ACT.Square, scale=D ** -0.5, accum_out=h_sumsq).then_inc(h_sumsq_ready, 1)
                act.wait_ge(filled[6], t * 4 + 4)
                act.activation(uT[:, 0:4, :], heads_of(6), ACT.Copy).then_inc(drained[6], 1)

            act.wait_ge(exp_arg, 1)
            act.activation(g_exp, g_exp, ACT.Exp).then_inc(exp_done, 1)
            act.wait_ge(exp_arg, 2)
            act.activation(w_sec, w_sec, ACT.Exp).then_inc(exp_done, 1)

            def evac_rows(j, u):
                act.wait_ge(rows_filled, j + 1)
                act.activation(rowsT[:, u, 0:4, :], heads_of(0), ACT.Copy).then_inc(rowsT_low, 1)

            def gate_and_y(j, i, u):
                act.wait_ge(up_filled, j + 1)
                act.activation(silu[:, u, :], psum[2][:, 0:FF], ACT.Silu).then_inc(silu_ready, 1)

            def evac_y(j, i, u):
                act.wait_ge(down_filled, j + 1)
                act.wait_ge(y_stored[u], i * 16)
                act.activation(y_rows[:, u, 0:512], psum[4][:, :], ACT.Copy).then_inc(y_low, 1)

            def moe_act(j, i, u, last=False):
                gate_and_y(j, i, u)
                if not last:
                    evac_rows(j + 1, (u + 1) % 3)
                evac_y(j, i, u)

            evac_rows(0, 0)
            with act.Fori(0, (BLOCKS - 1) // 3) as i:
                for u in range(3):
                    moe_act(i * 3 + u, i, u)
            moe_act(BLOCKS - 1, (BLOCKS - 1) // 3, 0, last=True)

            with act.Fori(0, TILES // 2) as i:
                for u in range(2):
                    act.wait_ge(sum_ready, i * 4 + (2 * u + 2))
                    act.activation(f_junk[:, u, :], h_in[:, u, :], ACT.Square, scale=D ** -0.5, accum_out=sumsq[:, u:u + 1]).then_inc(f_sumsq, 1)

        @block.vector
        def _(dve):
            c = Chain(dve, dve_step)

            def wait_apart(*waits):
                for s, v in waits:
                    dve.wait_ge(s, v)
                dve.memset(spare[:, 1:2], 0.0)

            iota_work = acts[:, 16384:16384 + 3 * P].bitcast(i32)
            mask_work = acts[:, 16384 + 3 * P:16384 + 5 * P]
            dve.wait_ge(masks_built, 1)
            c.link(dve.tensor_tensor(mask_work[:, 0:P], iota_work[:, 0:P], iota_work[:, P:2 * P], ALU.is_gt))
            c.link(dve.tensor_tensor(iota_work[:, 2 * P:3 * P], iota_work[:, 0:P], iota_work[:, P:2 * P], ALU.bitwise_xor))
            for lvl in range(LEVELS):
                c.link(dve.scalar_tensor_tensor(masks[:, lvl, :], iota_work[:, 2 * P:3 * P], float(P >> lvl), mask_work[:, 0:P], ALU.is_lt, ALU.mult))
            c.link(dve.tensor_scalar(masks[:, LEVELS, :], iota_work[:, 2 * P:3 * P], 0.0, None, ALU.is_equal))
            dve.memset(scoresT[:, :, :], 0.0)
            dve.memset(state[:, :, :], 0.0).then_inc(state_zero, 1)

            dve.wait_ge(gains_loaded, 32)

            def norm_tile(i, u, gain):
                dve.wait_ge(rstd_ready[u], i + 1)
                dve.wait_ge(x_loaded[u], i * 16 + 16)
                dve.wait_ge(x_transposed[u], i)
                dve.scalar_tensor_tensor(x_norm[:, u, :], x_in[:, u, :], rstd[:, u:u + 1], gain, ALU.mult, ALU.mult).then_inc(norm_ready[u], 1)

            def evac_high(i, u, dst):
                dve.wait_ge(x_transposed[u], i + 1)
                dve.tensor_copy(dst, cols(2 * u + 1, 512, 4)).then_inc(xT_high[u], 1)

            with dve.Fori(0, TILES // 2) as i:
                for u in range(2):
                    norm_tile(i, u, mix_gain)
                for u in range(2):
                    evac_high(i, u, xT[:, 4:8, ds((i * 2 + u) * P, P)])
            for u in range(2):
                norm_tile(TILES // 2, u, mem_gain)
            for u in range(2):
                evac_high(TILES // 2, u, memT[:, 4:8, u * P:(u + 1) * P])

            dve.wait_ge(small_loaded, 16 * 6)
            for n, job in enumerate(JOBS):
                if n == GATES_BEFORE:
                    for m, (h, s) in enumerate(GATE_JOBS):
                        u = m % 2
                        dve.wait_ge(gate_filled[u], m // 2 + 1)
                        if m >= 2:
                            dve.wait_ge(gate_summed[u], m // 2)
                        dve.tensor_scalar(min_term[u], psum[2 + u][:, :], b_gate[:, h:h + 1], 0.0, ALU.add, ALU.min).then_inc(gate_min[u], 1)
                        dve.wait_ge(gate_min[u], m // 2 + 1)
                        dve.wait_ge(gate_log[u], m // 2 * 3 + 3)
                        for q in range(4):
                            part = slice(q * P, (q + 1) * P)
                            ins = dve.tensor_tensor_scan(bT[:, h, s * 512 + q * P:s * 512 + (q + 1) * P], min_term[u][:, part],
                                                         log_term[u][:, part], 0.0, ALU.add, ALU.subtract)
                        ins.then_inc(gate_summed[u], 1)
                if n % 2 == 1:
                    dve.wait_ge(job_filled[n % 4], n // 4 + 1)
                    dst, src, scale = job_result(job, n)
                    dve.tensor_scalar(dst, src, scale, None, ALU.mult).then_inc(job_drained[n % 4], 1)

            dve.wait_ge(state_zero, 1)
            for b in (0, 2):
                dve.wait_ge(job_drained[b], len(range(b, len(JOBS), 4)))
            dve.wait_ge(ffn_gain_loaded, 16)
            with dve.Fori(0, TILES) as t:
                c.enter(t, 3)
                c.mark()
                tok = ds(t * P, P)
                kt, qt = kT[:, :, tok], qT[:, :, tok]

                def level(lvl):
                    f, s = lvl + 2, (P // 2) >> lvl
                    dve.wait_ge(exp_ready, t * 9 + (f + 1))
                    dve.wait_ge(filled[lvl % 2], t * 4 + lvl // 2)
                    fh = fac[:, f % 3, :].rearrange("p (h b a s) -> p h b a s", h=HEADS, a=2, s=s)
                    oh = qk[:, lvl % 2, :, :].rearrange("p h (b a s) -> p h b a s", a=2, s=s)
                    kh = kt.rearrange("p h (b a s) -> p h b a s", a=2, s=s)
                    qh = qt.rearrange("p h (b a s) -> p h b a s", a=2, s=s)
                    dve.tensor_tensor(oh[:, :, :, 0, :], kh[:, :, :, 0, :], fh[:, :, :, 0, :], ALU.mult)
                    dve.tensor_tensor(oh[:, :, :, 1, :], qh[:, :, :, 1, :], fh[:, :, :, 1, :], ALU.mult).then_inc(fac_used[f % 3], 1)

                def keep(lvl):
                    wait_apart((filled[lvl % 2], t * 4 + (lvl // 2 + 1)),
                               (filled[3], t * 2) if lvl == 0 else (drained[(lvl - 1) % 2], t * 4 + ((lvl - 1) // 2 + 1)))
                    mask = masks[:, lvl:lvl + 1, :].to_broadcast([P, HEADS, P])
                    dve.copy_predicated(scoresT[:, :, :], mask, heads_of(lvl % 2)).then_inc(drained[lvl % 2], 1)

                dve.wait_ge(exp_ready, t * 9 + 1)
                dve.wait_ge(filled[6], t * 4)
                dve.tensor_tensor(k_decayed[:, :, :], kt, fac[:, 0, :].rearrange("p (h t) -> p h t", h=HEADS), ALU.mult).then_inc(fac_used[0], 1)
                dve.wait_ge(exp_ready, t * 9 + 2)
                dve.wait_ge(filled[3], t * 2)
                dve.tensor_tensor(q_decayed[:, :, :], qt, fac[:, 1, :].rearrange("p (h t) -> p h t", h=HEADS), ALU.mult).then_inc(fac_used[1], 1)
                dve.wait_ge(filled[5], t * 3)
                dve.tensor_scalar(mq_tile[:, :, :], mqT[:, :, tok], 1.0, None, ALU.mult).then_inc(mq_ready, 1)
                level(0)
                level(1)
                dve.wait_ge(drained[5], t * 3)
                for b in (4, 5):
                    dve.wait_ge(filled[b], t * 3 + 1)
                    c.link(dve.tensor_reduce(neg_max[:, 2 * (b - 4):2 * (b - 3)], cols(b, 512, 2), AX.X, ALU.max, negate=True))
                dve.tensor_scalar(neg_max, neg_max, M_SCALE, None, ALU.mult).then_inc(negmax_ready, 1)
                keep(0)
                level(2)
                keep(1)
                level(3)
                keep(2)
                level(4)
                keep(3)
                dve.wait_ge(drained[4], t * 3 + 1)
                dve.wait_ge(drained[5], t * 3 + 1)
                c.link(dve.reciprocal(row_inv, row_sum))
                dve.tensor_tensor(probs[:, :, :], probs[:, :, :], row_inv.unsqueeze(2).to_broadcast([P, MHEADS, N_MEM]), ALU.mult).then_inc(probs_ready, 1)
                level(5)
                keep(4)
                level(6)
                keep(5)
                dve.wait_ge(filled[1], t * 4 + 3)
                dve.tensor_scalar(qk[:, 1, :, :], kt, 1.0, None, ALU.mult).then_inc(kd_ready, 1)
                keep(6)
                keep(7)
                dve.wait_ge(filled[4], t * 3 + 2)
                dve.wait_ge(filled[5], t * 3 + 2)
                dve.wait_ge(filled[3], t * 2 + 1)
                dve.wait_ge(decay_ready, t + 1)
                for h in range(HEADS):
                    ins = dve.scalar_tensor_tensor(state[:, h, :], state[:, h, :], decay_all[:, h:h + 1],
                                                   cols(4 + h // 2, 2 * DV, 2)[:, h % 2, :], ALU.mult, ALU.add)
                    if h % 2:
                        ins.then_inc(drained[4 + h // 2], 1)
                dve.wait_ge(o_sq_ready, t + 1)
                dve.wait_ge(o_rstd_ready, t)
                dve.tensor_reduce(o_sumsq, o_sq[:, :, :], AX.X, ALU.add).then_inc(o_sumsq_ready, 1)
                dve.wait_ge(filled[4], t * 3 + 3)
                dve.wait_ge(filled[6], t * 4)
                dve.tensor_copy(probsT[:, 0:2, :, :].rearrange("p h m t -> p (h m) t"), heads_of(4)).then_inc(drained[4], 1)
                dve.wait_ge(o_rstd_ready, t + 1)
                dve.wait_ge(filled[7], t * 3)
                for b in (2, 3):
                    dve.tensor_tensor(mix[:, 2 * (b - 2):2 * (b - 1), :], cols(b, 2 * DV, 2),
                                      o_rstd[:, 2 * (b - 2):2 * (b - 1)].unsqueeze(2).to_broadcast([P, 2, DV]), ALU.mult).then_inc(drained[b], 1)
                dve.wait_ge(filled[6], t * 4 + 2)
                dve.wait_ge(filled[3], t * 2)
                dve.tensor_copy(catT[:, 6:8, :], cols(6, 2 * P, 2)).then_inc(drained[6], 1)
                dve.wait_ge(filled[7], t * 3 + 1)
                dve.tensor_copy(catT[:, 4:6, :], cols(7, 2 * P, 2)).then_inc(drained[7], 1)
                dve.wait_ge(x_tile_loaded, t * 16 + 16)
                for b in (2, 3):
                    dve.wait_ge(filled[b], t * 2 + 2)
                    half = slice((b - 2) * 512, (b - 1) * 512)
                    dve.tensor_tensor(h_tile[:, half], h_tile[:, half], psum[b][:, :], ALU.add).then_inc(drained[b], 1)
                dve.wait_ge(drained[3], t * 2 + 2)
                dve.wait_ge(h_rstd_ready, t + 1)
                dve.wait_ge(u_stored, t * 16)
                dve.wait_ge(filled[7], t * 3)
                dve.scalar_tensor_tensor(u_tile, h_tile, h_rstd, ffn_gain, ALU.mult, ALU.mult).then_inc(u_ready, 1)
                dve.wait_ge(filled[7], t * 3 + 2)
                dve.tensor_copy(uT[:, 4:8, :], heads_of(7)).then_inc(drained[7], 1)
                dve.wait_ge(filled[7], t * 3 + 3)
                dve.tensor_tensor(logits[:, ds(t, 1), :].rearrange("p a n -> p (a n)"), psum[7][:, 0:G + E], b_route[:, :], ALU.add).then_inc(drained[7], 1)
            c.leave(TILES)

            dve.wait_ge(ones_built, 1)
            dve.wait_ge(drained[7], TILES * USES[7])
            wide = [P, TILES, G]
            gl, el = logits[:, :, 0:G], logits[:, :, G:G + E].rearrange("p t (g e) -> p t g e", g=G)

            def first_of(hot, values, best):
                c.link(dve.tensor_tensor(equal, values, best.unsqueeze(2).to_broadcast(wide), ALU.is_equal))
                c.link(dve.tensor_copy(seen, equal[:, :, 0]))
                c.link(dve.tensor_copy(hot[:, :, 0], equal[:, :, 0]))
                for n in range(1, 4):
                    c.link(dve.tensor_tensor(hot[:, :, n], equal[:, :, n], seen, ALU.is_gt))
                    if n < 3:
                        c.link(dve.tensor_tensor(seen, seen, equal[:, :, n], ALU.max))

            c.link(dve.tensor_reduce(g_max, gl, AX.X, ALU.max))
            dve.tensor_tensor(g_exp, gl, g_max.unsqueeze(2).to_broadcast(wide), ALU.subtract).then_inc(exp_arg, 1)
            first_of(g_hot, gl, g_max)
            c.link(dve.tensor_tensor(picked, el, g_hot.unsqueeze(3).to_broadcast([P, TILES, G, PER]), ALU.mult))
            c.link(dve.tensor_reduce(e_in, picked.rearrange("p t g e -> p t e g"), AX.X, ALU.add))
            c.link(dve.tensor_reduce(e_top, e_in, AX.X, ALU.max))
            first_of(a_hot, e_in, e_top)
            c.link(dve.scalar_tensor_tensor(e_rest, a_hot, -3.0e38, e_in, ALU.mult, ALU.add))
            c.link(dve.tensor_reduce(e_second, e_rest, AX.X, ALU.max))
            first_of(b_hot, e_rest, e_second)
            dve.tensor_tensor(w_sec, e_second, e_top, ALU.subtract).then_inc(exp_arg, 1)
            dve.wait_ge(exp_done, 2)
            c.link(dve.tensor_reduce(g_prob, g_exp, AX.X, ALU.add))
            c.link(dve.tensor_scalar(w_first, w_sec, 1.0, None, ALU.add))
            c.link(dve.tensor_tensor(w_first, w_first, g_prob, ALU.mult))
            c.link(dve.reciprocal(weight[:, 0, :], w_first))
            c.link(dve.tensor_tensor(weight[:, 1, :], weight[:, 0, :], w_sec, ALU.mult))
            for full, hot in ((a_all, a_hot), (b_all, b_hot)):
                c.link(dve.tensor_tensor(full, g_hot.unsqueeze(3).to_broadcast([P, TILES, G, PER]),
                                         hot.unsqueeze(2).to_broadcast([P, TILES, G, PER]), ALU.mult))
            a_te, b_te = (v.rearrange("p t g e -> p t (g e)") for v in (a_all, b_all))
            dve.tensor_tensor(member, a_te, b_te, ALU.add).then_inc(member_ready, 1)
            c.link(dve.memset(carry[:, 0, :], 0.0))
            dve.wait_ge(rank_filled, 1)
            ranks, totals = cols(0, TE, TILES), cols(1, TE, TILES)
            for t in range(TILES):
                c.link(dve.tensor_tensor(carry[:, t + 1, :], carry[:, t, :], totals[:, t, :], ALU.add))
            c.link(dve.tensor_tensor(rank, ranks, carry[:, 0:TILES, :], ALU.add))
            count = carry[:, TILES, :]
            c.link(dve.tensor_scalar(extra, count, float(P), None, ALU.is_gt))
            for m in range(2, T // P):
                c.link(dve.scalar_tensor_tensor(extra, count, float(P * m), extra, ALU.is_gt, ALU.add))
            c.link(dve.memset(one_minus, 1.0))
            c.link(dve.tensor_tensor_scan(extra_upto, one_minus, extra, 0.0, ALU.mult, ALU.add))
            c.link(dve.tensor_tensor(code_high, extra_upto, extra, ALU.subtract))
            c.link(dve.tensor_scalar(code_high, code_high, float(P), float(P * EXPERTS - P), ALU.mult, ALU.add))
            c.link(dve.tensor_tensor(code_low, expert_base, code_high, ALU.subtract))
            all_te = [P, TILES, E]
            c.link(dve.tensor_scalar(code, rank, float(P), None, ALU.is_lt))
            c.link(dve.tensor_tensor(code, code, code_low.unsqueeze(1).to_broadcast(all_te), ALU.mult))
            c.link(dve.tensor_tensor(code, code, code_high.unsqueeze(1).to_broadcast(all_te), ALU.add))
            c.link(dve.tensor_tensor(code, code, rank, ALU.add))
            for n, full in enumerate((a_te, b_te)):
                c.link(dve.tensor_tensor(prod, code, full, ALU.mult))
                c.link(dve.tensor_reduce(slot_f[:, n, :], prod, AX.X, ALU.add))
            flat = slot_f.rearrange("p a b -> p (a b)")
            c.link(dve.tensor_copy(slot_i, flat))
            c.link(dve.tensor_scalar(row_i, slot_i, P - 1, None, ALU.bitwise_and))
            c.link(dve.tensor_scalar(block_i, slot_i, 7, None, ALU.logical_shift_right))
            c.link(dve.tensor_copy(row_f.rearrange("p a b -> p (a b)"), row_i))
            c.link(dve.tensor_copy(block_f.rearrange("p a b -> p (a b)"), block_i))
            c.link(dve.tensor_tensor(upto_cmp, block_iota[:, 0:EXTRA].unsqueeze(2).to_broadcast([P, EXTRA, E]),
                                     extra_upto.unsqueeze(1).to_broadcast([P, EXTRA, E]), ALU.is_ge))
            c.link(dve.tensor_copy(expert_f[:, 0:E], block_iota[:, 0:E]))
            c.link(dve.tensor_reduce(expert_f[:, E:BLOCKS], upto_cmp, AX.X, ALU.add))
            c.link(dve.tensor_scalar(expert_f, expert_f, float(E - 1), None, ALU.min))
            c.link(dve.tensor_copy(expert_table, expert_f))
            for n in range(2 * TILES):
                u = n % 2
                if n >= 2:
                    dve.wait_ge(hot_used, n - 1)
                choice, t = n // TILES, n % TILES
                c.link(dve.tensor_scalar(row_hot[u], row_iota, row_f[:, choice, t:t + 1], None, ALU.is_equal))
                dve.tensor_scalar(block_hot[u], block_iota, block_f[:, choice, t:t + 1], token_id[:, t:t + 1],
                                  ALU.is_equal, ALU.mult).then_inc(hot_ready, 1)
            dve.wait_ge(table_filled, 1)
            dve.tensor_copy(token_table, psum[2][:, 0:BLOCKS]).then_inc(tables_ready, 1)

            def evac_rows(j, u):
                dve.wait_ge(rows_filled, j + 1)
                dve.tensor_copy(rowsT[:, u, 4:8, :], heads_of(1)).then_inc(rowsT_high, 1)

            def moe_dve(j, i, u, last=False):
                dve.wait_ge(silu_ready, j + 1)
                dve.tensor_tensor(hid[:, u, :], psum[2][:, FF:2 * FF], silu[:, u, :], ALU.mult).then_inc(hid_ready, 1)
                if not last:
                    evac_rows(j + 1, (u + 1) % 3)
                dve.wait_ge(hidT_filled, j + 1)
                dve.tensor_copy(hidT[:, u, :, :], cols(3, KF * P, KF)).then_inc(hidT_ready, 1)
                dve.wait_ge(down_filled, j + 1)
                dve.wait_ge(y_stored[u], i * 16)
                dve.tensor_copy(y_rows[:, u, 512:1024], psum[5][:, :]).then_inc(y_high, 1)

            evac_rows(0, 0)
            with dve.Fori(0, (BLOCKS - 1) // 3) as i:
                for u in range(3):
                    moe_dve(i * 3 + u, i, u)
            moe_dve(BLOCKS - 1, (BLOCKS - 1) // 3, 0, last=True)

            dve.wait_ge(final_gain_loaded, 16)
            with dve.Fori(0, TILES // 2) as i:
                for u in range(2):
                    t = i * 2 + u
                    dve.wait_ge(ya_loaded[u], i * 16 + 16)
                    dve.wait_ge(h_loaded[u], i * 16 + 16)
                    dve.scalar_tensor_tensor(h_in[:, u, :], y_a[:, u, :], weight[:, 0, ds(t, 1)], h_in[:, u, :], ALU.mult, ALU.add).then_inc(sum_ready, 1)
                    dve.wait_ge(sum_ready, i * 4 + (2 * u + 1))
                    dve.wait_ge(yb_loaded[u], i * 16 + 16)
                    dve.scalar_tensor_tensor(h_in[:, u, :], y_b[:, u, :], weight[:, 1, ds(t, 1)], h_in[:, u, :], ALU.mult, ALU.add).then_inc(sum_ready, 1)
                for u in range(2):
                    dve.wait_ge(f_rstd, i * 2 + (u + 1))
                    dve.wait_ge(sum_ready, i * 4 + (2 * u + 2))
                    dve.wait_ge(out_stored[u], i * 16)
                    dve.scalar_tensor_tensor(o_out[:, u, :], h_in[:, u, :], rstd[:, u:u + 1], final_gain, ALU.mult, ALU.mult).then_inc(out_ready, 1)

        @block.tensor
        def _(pe):
            pe.wait_ge(ident_built, 1)

            def turn(dst, src, inc=None):
                ins = pe.transpose(dst, src, ident[:, :])
                if inc is not None:
                    ins.then_inc(inc, 1)

            def transpose_tile(i, u):
                pe.wait_ge(norm_ready[u], i + 1)
                pe.wait_ge(xT_low[u], i)
                pe.wait_ge(xT_high[u], i)
                for k in range(KD):
                    turn(psum[2 * u + k // 4][:, (k % 4) * P:(k % 4 + 1) * P], x_norm[:, u, k * P:(k + 1) * P],
                         x_transposed[u] if k == KD - 1 else None)

            with pe.Fori(0, TILES // 2) as i:
                for u in range(2):
                    transpose_tile(i, u)
            for u in range(2):
                transpose_tile(TILES // 2, u)
            for u in range(2):
                pe.wait_ge(xT_low[u], TILES // 2 + 1)
                pe.wait_ge(xT_high[u], TILES // 2 + 1)

            chunk = -1
            for n, (c, kind, g, s) in enumerate(JOBS):
                if n == GATES_BEFORE:
                    pe.wait_ge(small_loaded, 16 * 6)
                    pe.wait_ge(job_drained[0], 2)
                    pe.wait_ge(job_drained[1], 2)
                    for m, (h, sh) in enumerate(GATE_JOBS):
                        u = m % 2
                        if m >= 2:
                            pe.wait_ge(gate_min[u], m // 2)
                            pe.wait_ge(gate_log[u], m // 2 * 3)
                        pe.matmul(psum[2 + u][:, :], w_gate[:, h * P:(h + 1) * P], rT[:, sh * 512:sh * 512 + 512],
                                  start=True, stop=True).then_inc(gate_filled[u], 1)
                if c != chunk:
                    chunk = c
                    pe.wait_ge(chunk_loaded[c % 2], 16 * (c // 2 + 1))
                if n >= 4:
                    pe.wait_ge(job_drained[n % 4], n // 4)
                w = ring[:, c % 2, :, :]
                bank = psum[4 + n % 4]
                half = slice(s * 512, s * 512 + 512)
                for k in range(KD):
                    if kind == "mem_k":
                        o, a, b = bank[:, 0:N_MEM], w[:, k, g * P:(g + 1) * P], memT[:, k, :]
                    elif kind == "mem_v":
                        o, a, b = bank[:, 0:MEMW], memT[:, k, g * P:(g + 1) * P], w[:, k, MEMW:2 * MEMW]
                    elif kind == "rank":
                        o, a, b = bank[0:RANK, :], w[:, k, 0:RANK], xT[:, k, half]
                    elif kind == "mem_q":
                        o, a, b = bank[:, :], w[:, k, RANK + g * P:RANK + (g + 1) * P], xT[:, k, half]
                    elif kind in ("k", "q"):
                        o, a, b = bank[:, :], w[:, k, g * P:(g + 1) * P], xT[:, k, half]
                    else:
                        o, a, b = bank[:, :], xT[:, k, s * P:(s + 1) * P], w[:, k, :]
                    ins = pe.matmul(o, a, b, start=(k == 0), stop=(k == KD - 1))
                ins.then_inc(job_filled[n % 4], 1)

            for b in range(4):
                pe.wait_ge(job_drained[b], len(range(b, len(JOBS), 4)))
            for u in range(2):
                pe.wait_ge(gate_summed[u], len(GATE_JOBS) // 2)
            for u in range(2):
                pe.wait_ge(chunk_loaded[u], 16 * len(range(u, len(CHUNKS), 2)))
            pe.wait_ge(state_zero, 1)
            with pe.Fori(0, TILES) as t:
                def use(bank, k):
                    pe.wait_ge(drained[bank], t * USES[bank] + k)

                v_t = vg[:, ds(t, 1), 0:MIX].rearrange("p a (h d) -> p (a h) d", h=HEADS)
                pe.wait_ge(fac_used[0], t * 3 + 1)
                use(6, 0)
                for h in range(HEADS):
                    turn(heads_of(6)[:, h, :], k_decayed[:, h, :], filled[6] if h == HEADS - 1 else None)
                pe.wait_ge(mq_ready, t + 1)
                for b in (4, 5):
                    use(b, 0)
                    for e in range(2):
                        part = slice((b - 4) * MHD, (b - 3) * MHD)
                        ins = pe.matmul(cols(b, 512, 2)[:, e, :], mq_tile[part, e, :], mem_kT[part, e, :], start=True, stop=True)
                    ins.then_inc(filled[b], 1)
                for lvl in range(LEVELS + 1):
                    b = lvl % 2
                    if lvl < LEVELS:
                        f = lvl + 2
                        pe.wait_ge(fac_used[f % 3], t * 3 + (f // 3 + 1))
                    else:
                        pe.wait_ge(kd_ready, t + 1)
                    use(b, lvl // 2)
                    for h in range(HEADS):
                        moving = qk[:, b, h, :] if lvl < LEVELS else qT[:, h, ds(t * P, P)]
                        ins = pe.matmul(heads_of(b)[:, h, :], qk[:, b, h, :], moving, start=True, stop=True)
                    ins.then_inc(filled[b], 1)
                pe.wait_ge(drained[6], t * 4 + 1)
                for b in (4, 5):
                    use(b, 1)
                    for e in range(2):
                        h = 2 * (b - 4) + e
                        ins = pe.matmul(cols(b, 2 * DV, 2)[:, e, :], k_decayedT[:, h, :], v_t[:, h, :], start=True, stop=True)
                    ins.then_inc(filled[b], 1)
                for b in (0, 1):
                    pe.wait_ge(drained[b], t * 4 + 4)
                pe.wait_ge(fac_used[1], t * 3 + 1)
                pe.wait_ge(drained[5], t * 3)
                for b in (2, 3):
                    use(b, 0)
                    for e in range(2):
                        h = 2 * (b - 2) + e
                        o = cols(b, 2 * DV, 2)[:, e, :]
                        pe.matmul(o, scoresT[:, h, :], v_t[:, h, :], start=True, stop=False)
                        ins = pe.matmul(o, q_decayed[:, h, :], state[:, h, :], start=False, stop=True)
                    ins.then_inc(filled[b], 1)
                pe.wait_ge(probs_ready, t + 1)
                for b in (4, 5):
                    use(b, 2)
                    for n in range(4):
                        h, m = 2 * (b - 4) + n // 2, n % 2
                        turn(heads_of(b)[:, n, :], probs[:, h, m * P:(m + 1) * P], filled[b] if n == 3 else None)
                pe.wait_ge(drained[4], t * 3 + 3)
                pe.wait_ge(drained[5], t * 3 + 3)
                use(6, 1)
                for place in range(MHEADS):
                    h = 2 * (place % 2) + place // 2
                    o = psum[6][(h % 2) * MHD:(h % 2 + 1) * MHD, (h // 2) * P:(h // 2 + 1) * P]
                    for m in range(MTILES):
                        ins = pe.matmul(o, mem_v[:, m, h * MHD:(h + 1) * MHD], probsT[:, place, m, :], start=(m == 0), stop=(m == MTILES - 1))
                ins.then_inc(filled[6], 1)
                pe.wait_ge(mix_ready, t + 1)
                mix_flat = mix[:, :, :].rearrange("p h d -> p (h d)")
                use(6, 2)
                for k in range(4):
                    turn(heads_of(6)[:, k, :], mix_flat[:, k * P:(k + 1) * P], filled[6] if k == 3 else None)
                use(7, 0)
                for k in (4, 5):
                    turn(heads_of(7)[:, k - 4, :], mix_flat[:, k * P:(k + 1) * P], filled[7] if k == 5 else None)
                pe.wait_ge(drained[6], t * 4 + 3)
                pe.wait_ge(drained[7], t * 3 + 1)
                for b in (2, 3):
                    use(b, 1)
                    for k in range(KD):
                        ins = pe.matmul(psum[b][:, :], catT[:, k, :], w_out_half[b - 2][:, k, :], start=(k == 0), stop=(k == KD - 1))
                    ins.then_inc(filled[b], 1)
                pe.wait_ge(u_ready, t + 1)
                use(6, 3)
                for k in range(4):
                    turn(heads_of(6)[:, k, :], u_tile[:, k * P:(k + 1) * P], filled[6] if k == 3 else None)
                use(7, 1)
                for k in range(4, 8):
                    turn(heads_of(7)[:, k - 4, :], u_tile[:, k * P:(k + 1) * P], filled[7] if k == 7 else None)
                pe.wait_ge(drained[6], t * 4 + 4)
                use(7, 2)
                for k in range(KD):
                    ins = pe.matmul(psum[7][:, 0:G + E], uT[:, k, :], w_route[:, k, :], start=(k == 0), stop=(k == KD - 1))
                ins.then_inc(filled[7], 1)

            pe.wait_ge(member_ready, 1)
            pe.wait_ge(drained[0], TILES * USES[0])
            pe.wait_ge(drained[1], TILES * USES[1])
            flat = member.rearrange("p t e -> p (t e)")
            pe.matmul(psum[0][:, 0:TE], tri, flat, start=True, stop=True)
            pe.matmul(psum[1][:, 0:TE], ones, flat, start=True, stop=True).then_inc(rank_filled, 1)
            for n in range(2 * TILES):
                pe.wait_ge(hot_ready, n + 1)
                ins = pe.matmul(psum[2][:, 0:BLOCKS], row_hot[n % 2], block_hot[n % 2], start=(n == 0), stop=(n == 2 * TILES - 1))
                ins.then_inc(hot_used if n < 2 * TILES - 1 else table_filled, 1)
            pe.wait_ge(tables_ready, 1)

            def rows_transposed(j, i, u):
                pe.wait_ge(gathered[u], i * 16 + 16)
                pe.wait_ge(rowsT_low, j)
                pe.wait_ge(rowsT_high, j)
                for k in range(KD):
                    turn(psum[k // 4][:, (k % 4) * P:(k % 4 + 1) * P], rows[:, u, k * P:(k + 1) * P], rows_filled if k == KD - 1 else None)

            def moe_pe(j, i, u, last=False):
                pe.wait_ge(w_loaded[u], i * 32 + 32)
                pe.wait_ge(rowsT_low, j + 1)
                pe.wait_ge(rowsT_high, j + 1)
                pe.wait_ge(hid_ready, j)
                for k in range(KD):
                    ins = pe.matmul(psum[2][:, 0:2 * FF], rowsT[:, u, k, :], up_w[u][:, k, :], start=(k == 0), stop=(k == KD - 1))
                ins.then_inc(up_filled, 1)
                if not last:
                    rows_transposed(j + 1, i + (1 if u == 2 else 0), (u + 1) % 3)
                pe.wait_ge(hid_ready, j + 1)
                pe.wait_ge(hidT_ready, j)
                for k in range(KF):
                    turn(psum[3][:, k * P:(k + 1) * P], hid[:, u, k * P:(k + 1) * P], hidT_filled if k == KF - 1 else None)
                pe.wait_ge(hidT_ready, j + 1)
                pe.wait_ge(y_low, j)
                pe.wait_ge(y_high, j)
                for n in range(2):
                    for k in range(KF):
                        ins = pe.matmul(psum[4 + n][:, :], hidT[:, u, k, :], down_w[u][:, k, n * 512:(n + 1) * 512], start=(k == 0), stop=(k == KF - 1))
                ins.then_inc(down_filled, 1)

            rows_transposed(0, 0, 0)
            with pe.Fori(0, (BLOCKS - 1) // 3) as i:
                for u in range(3):
                    moe_pe(i * 3 + u, i, u)
            moe_pe(BLOCKS - 1, (BLOCKS - 1) // 3, 0, last=True)


INS = ["x", "mem", "mix_norm", "ffn_norm", "mem_norm", "final_norm", "gla_w_in", "gla_w_gate_up",
       "gla_b_gate", "gla_out_norm", "w_mem_kv", "w_out", "w_group", "b_group", "w_router", "b_router",
       "w_up", "w_down"]


def kernel(**inputs):
    import numpy as np
    import concourse.bacc as bacc
    from concourse import mybir as mb
    from concourse.bass_utils import run_bass_kernel_spmd

    nc = bacc.Bacc("TRN2", target_bir_lowering=False, num_devices=1)
    arrays, args = {}, []
    for name in INS:
        a = np.ascontiguousarray(inputs[name])
        arrays[f"in_{name}"] = a
        args.append(nc.dram_tensor(f"in_{name}", a.shape, mb.dt.from_np(a.dtype), kind="ExternalInput").ap())
    shape = tuple(inputs["x"].shape)
    args.append(nc.dram_tensor("out_rows", shape, mb.dt.float32, kind="ExternalOutput").ap())
    hybrid_layer(nc, *args)
    r = run_bass_kernel_spmd(nc, [arrays], core_ids=[0])
    return r.results[0]["out_rows"]
```

```python
from contextlib import ExitStack

import concourse.bass as bass
from concourse import mybir

P = 128


class Chain:

    def __init__(self, eng, sem):
        self.eng, self.sem, self.base, self.n, self.turn, self.per = eng, sem, 0, 0, 0, 0

    def link(self, ins):
        ins.then_inc(self.sem, 1)
        self.n += 1
        self.eng.wait_ge(self.sem, self.turn * self.per + (self.base + self.n))

    def enter(self, turn, per):
        self.turn, self.per = turn, per

    def leave(self, turns):
        assert self.n - self.start == self.per, (self.n - self.start, self.per)
        self.base += self.per * (turns - 1)
        self.turn = 0

    def mark(self):
        self.start = self.n


def hybrid_layer(nc, x, mem, mix_norm, ffn_norm, mem_norm, final_norm, gla_w_in, gla_w_gate_up,
                 gla_b_gate, gla_out_norm, w_mem_kv, w_out, w_group, b_group, w_router, b_router,
                 w_up, w_down, out):
    f32, f16, f32r = mybir.dt.float32, mybir.dt.float16, mybir.dt.float32r
    i32, u8 = mybir.dt.int32, mybir.dt.uint8
    ALU, ACT, AX = mybir.AluOpType, mybir.ActivationFunctionType, mybir.AxisListType
    ds = bass.ds

    T, D = x.shape[1], x.shape[2]
    N_MEM = mem.shape[1]
    TILES, KD = T // P, D // P
    HEADS = 4
    KEY = gla_w_gate_up.shape[2]
    RANK = gla_w_gate_up.shape[1]
    DV = gla_out_norm.shape[1]
    MIX = HEADS * DV
    DK = KEY // HEADS
    MEMW = w_mem_kv.shape[2] // 2
    MHEADS = 4
    MHD = MEMW // MHEADS
    MTILES = N_MEM // P
    GROUPS = w_group.shape[2]
    EXPERTS = w_router.shape[2]
    PER = EXPERTS // GROUPS
    FF = w_down.shape[2]
    KF = FF // P
    EPS = 1e-6
    GATE_SCALE = 1.0 / 16.0
    Q_SCALE = DK ** -0.5
    M_SCALE = MHD ** -0.5
    LEVELS = 7
    CHOICES = 2
    PAIRS = ((T * CHOICES + EXPERTS * (P - 1)) // P + 1) // 2
    BLOCKS = 2 * PAIRS
    COLS = BLOCKS + 2
    EXTRA = COLS - EXPERTS
    assert DK == P and KD == 8 and T % 512 == 0 and D == 1024

    w_in = gla_w_in[0].rearrange("(k p) n -> p k n", p=P)
    w_kv = w_mem_kv[0].rearrange("(k p) n -> p k n", p=P)
    w_o = w_out[0].rearrange("(k p) n -> p k n", p=P)
    up_rows = w_up[0].rearrange("e (k p) n -> e p k n", p=P)
    down_rows = w_down[0].rearrange("e (k p) n -> e p k n", p=P)
    h_dram = nc.dram_tensor("h_rows", [T, D], f32, kind="Internal").ap()
    u_dram = nc.dram_tensor("u_rows", [T, D], f32, kind="Internal").ap()
    y_dram = nc.dram_tensor("y_rows", [BLOCKS * P, D], f32, kind="Internal").ap()

    with ExitStack() as ctx:
        def sb(name, shape, dt=f32):
            return ctx.enter_context(nc.sbuf_tensor(name, shape, dt))

        def sem(name):
            return ctx.enter_context(nc.semaphore(name))

        def sems(name, n):
            return [sem(f"{name}{i}") for i in range(n)]

        def later(name, base, at, shape):
            return nc.alloc_sbuf_tensor_at(name, shape, f32r, offset=base + 4 * at)

        region_a_base = (nc.sbuf_base + 31) // 32 * 32
        region_a = sb("region_a", [P, KD * T])
        ring_base = (nc.sbuf_base + 31) // 32 * 32
        ring = sb("weight_ring", [P, 2, KD, 512])
        acts_base = (nc.sbuf_base + 31) // 32 * 32
        acts = sb("activations", [P, 24576])
        mqT_base = (nc.sbuf_base + 31) // 32 * 32
        mqT = sb("mqT", [P, 2, T])
        fac = sb("fac", [P, 3, 512])
        qk = sb("qk", [P, 2, HEADS, P])
        scoresT = sb("scoresT", [P, HEADS, P])
        q_decayed = sb("q_decayed", [P, HEADS, P])
        k_decayed = sb("k_decayed", [P, HEADS, P])
        k_decayedT = sb("k_decayedT", [P, HEADS, P])
        mq_tile = sb("mq_tile", [P, 2, P])
        state = sb("state", [P, HEADS, DV])
        mix = sb("mix", [P, HEADS, DV])
        gate = sb("gate", [P, HEADS, DV])
        out_gain = sb("out_gain", [P, 1, DV])
        mem_kT = sb("mem_kT", [P, 2, N_MEM])
        mem_v = sb("mem_v", [P, MTILES, MEMW])
        masks = sb("masks", [P, LEVELS + 1, P], u8)
        ident = sb("ident", [P, P])
        w_route = sb("w_route", [P, KD, GROUPS + EXPERTS])
        b_route = sb("b_route", [P, GROUPS + EXPERTS])
        logits = sb("logits", [P, TILES, GROUPS + EXPERTS])
        b_gate = sb("b_gate", [P, HEADS])
        stat = sb("stat", [P, 48])
        minus_half = sb("minus_half", [P, 4])
        eps = sb("eps", [P, 4])
        spare = sb("spare", [P, 2])
        sumsq, meansq, rstd = stat[:, 0:2], stat[:, 2:4], stat[:, 4:6]
        neg_max, row_sum, row_inv = stat[:, 8:12], stat[:, 12:16], stat[:, 16:20]
        o_sumsq, o_meansq, o_rstd = stat[:, 20:24], stat[:, 24:28], stat[:, 28:32]
        h_sumsq, h_meansq, h_rstd = stat[:, 32:33], stat[:, 33:34], stat[:, 34:35]
        decay_all = stat[:, 36:40]

        xT = region_a[:, :].rearrange("p (k t) -> p k t", k=KD)
        qT = acts[:, 0:4096].rearrange("p (h t) -> p h t", h=HEADS)
        kT = acts[:, 4096:8192].rearrange("p (h t) -> p h t", h=HEADS)
        vg = acts[:, 8192:20480].rearrange("p (t n) -> p t n", t=TILES)
        bT = acts[:, 20480:24576].rearrange("p (h t) -> p h t", h=HEADS)
        x_in = acts[:, 8192:10240].rearrange("p (u n) -> p u n", u=2)
        x_norm = acts[:, 10240:12288].rearrange("p (u n) -> p u n", u=2)
        junk = acts[:, 12288:14336].rearrange("p (u n) -> p u n", u=2)
        mix_gain = acts[:, 14336:15360]
        mem_gain = acts[:, 15360:16384]
        memT = acts[:, 20480:22528].rearrange("p (k t) -> p k t", k=KD)
        rT = fac[0:RANK, 0:2, :].rearrange("p u t -> p (u t)")
        w_gate = fac[0:RANK, 2, :]
        log_term = [qk[:, u, :, :].rearrange("p h t -> p (h t)") for u in range(2)]
        min_term = [q_decayed[:, :, :].rearrange("p h t -> p (h t)"),
                    k_decayed[:, :, :].rearrange("p h t -> p (h t)")]
        h_tile, u_tile = region_a[:, 0:1024], region_a[:, 1024:2048]
        uT = region_a[:, 2048:3072].rearrange("p (k t) -> p k t", k=KD)
        catT = region_a[:, 3072:4096].rearrange("p (k t) -> p k t", k=KD)
        probs = region_a[:, 4096:5120].rearrange("p (h m) -> p h m", h=MHEADS)
        probsT = region_a[:, 5120:6144].rearrange("p (h m t) -> p h m t", h=MHEADS, m=MTILES)
        ffn_gain = region_a[:, 6144:7168]
        zeros = region_a[:, 7936:8192]
        o_sq = region_a[:, 7168:7168 + MIX].rearrange("p (h d) -> p h d", h=HEADS)

        psum = [ctx.enter_context(nc.psum_tensor(f"bank{b}", [P, 512], f32)) for b in range(8)]

        def heads_of(bank):
            return psum[bank][:, :].rearrange("p (h t) -> p h t", h=HEADS)

        def cols(bank, n, parts):
            return psum[bank][:, 0:n].rearrange("p (a b) -> p a b", a=parts)

        small_loaded, gains_loaded = sem("small_loaded"), sem("gains_loaded")
        out_gain_loaded, ffn_gain_loaded = sem("out_gain_loaded"), sem("ffn_gain_loaded")
        pool_step, dve_step = sem("pool_step"), sem("dve_step")
        ident_built, half_built, state_zero = sem("ident_built"), sem("half_built"), sem("state_zero")
        masks_built = sem("masks_built")
        x_loaded, sumsq_ready, rstd_ready = sems("x_loaded", 2), sems("sumsq_ready", 2), sems("rstd_ready", 2)
        norm_ready, x_transposed = sems("norm_ready", 2), sems("x_transposed", 2)
        xT_low, xT_high = sems("xT_low", 2), sems("xT_high", 2)
        chunk_loaded = sems("chunk_loaded", 2)
        job_filled, job_drained = sems("job_filled", 4), sems("job_drained", 4)
        gate_filled, gate_log, gate_min = sems("gate_filled", 2), sems("gate_log", 2), sems("gate_min", 2)
        gate_summed = sems("gate_summed", 2)
        filled, drained = sems("bank_filled", 8), sems("bank_drained", 8)
        arg_ready, exp_ready, fac_used = sem("arg_ready"), sem("exp_ready"), sems("fac_used", 3)
        kd_ready, mq_ready, decay_ready = sem("kd_ready"), sem("mq_ready"), sem("decay_ready")
        negmax_ready, probs_ready = sem("negmax_ready"), sem("probs_ready")
        tanh_ready, o_sq_ready, o_sumsq_ready = sem("tanh_ready"), sem("o_sq_ready"), sem("o_sumsq_ready")
        o_rstd_ready, mix_ready = sem("o_rstd_ready"), sem("mix_ready")
        x_tile_loaded, h_sumsq_ready, h_rstd_ready = sem("x_tile_loaded"), sem("h_sumsq_ready"), sem("h_rstd_ready")
        u_ready, h_stored, u_stored = sem("u_ready"), sem("h_stored"), sem("u_stored")
        zeros_built, y_cleared = sem("zeros_built"), sem("y_cleared")
        exp_arg, exp_done, ones_built = sem("exp_arg"), sem("exp_done"), sem("ones_built")
        member_ready, rank_filled, hot_ready = sem("member_ready"), sem("rank_filled"), sem("hot_ready")
        hot_used, table_filled, tables_ready = sem("hot_used"), sem("table_filled"), sem("tables_ready")
        raw_loaded, part_high = sems("raw_loaded", 3), sems("part_high", 3)
        part_low_dve, part_low_pool, part_used = sems("part_low_dve", 3), sems("part_low_pool", 3), sems("part_used", 3)
        y_stored, gathered = sems("y_stored", 2), sems("gathered", 2)
        idx_ready, rows_filled = sem("idx_ready"), sems("rows_filled", 2)
        rowsT_high, rowsT_low = sems("rowsT_high", 2), sem("rowsT_low")
        silu_ready, hid_ready, hidT_filled = sem("silu_ready"), sem("hid_ready"), sem("hidT_filled")
        hidT_high, hidT_low, y_left, y_right = sem("hidT_high"), sem("hidT_low"), sem("y_left"), sem("y_right")
        final_gain_loaded = sem("final_gain_loaded")
        ya_loaded, yb_loaded, h_loaded = sems("ya_loaded", 2), sems("yb_loaded", 2), sems("h_loaded", 2)
        slot_copied = sem("slot_copied")
        sum_ready, f_sumsq, f_rstd = sem("sum_ready"), sem("f_sumsq"), sem("f_rstd")
        out_ready, out_stored = sem("out_ready"), sems("out_stored", 2)

        CHUNKS = [(w_kv, 0, 512), (w_in, 2 * KEY + 2 * MIX, RANK + MEMW), (w_in, KEY, 512), (w_in, 0, 512),
                  (w_in, 2 * KEY, 512), (w_in, 2 * KEY + 512, 512), (w_in, 2 * KEY + 1024, 512),
                  (w_o, 0, 512), (w_o, 512, 512)]
        JOBS = ([(0, "mem_k", g, 0) for g in range(2)] + [(0, "mem_v", m, 0) for m in range(MTILES)]
                + [(1, "rank", 0, s) for s in range(2)] + [(1, "mem_q", g, s) for g in range(2) for s in range(2)]
                + [(2, "k", h, s) for h in range(HEADS) for s in range(2)]
                + [(3, "q", h, s) for h in range(HEADS) for s in range(2)]
                + [(4 + n, "vg", n, t) for n in range(3) for t in range(TILES)])
        GATES_BEFORE = next(n for n, j in enumerate(JOBS) if j[1] == "q")
        GATE_JOBS = [(h, s) for h in range(HEADS) for s in range(2)]

        def last_job(chunk):
            return max(n for n, j in enumerate(JOBS) if j[0] == chunk)

        w_out_half = [ring[:, 1, :, :], ring[:, 0, :, :]]

        USES = [4, 4, 3, 3, 3, 3, 2, 3]

        rt = region_a

        def small(at, *dims):
            n = 1
            for d in dims:
                n *= d
            v = rt[:, at:at + n]
            if len(dims) == 2:
                return v.rearrange("p (a b) -> p a b", a=dims[0])
            if len(dims) == 3:
                return v.rearrange("p (a b c) -> p a b c", a=dims[0], b=dims[1])
            return v

        PIECE = KD // 2 * 2 * FF
        assert PIECE == KF * D and 3 * PIECE <= 6144
        POOL_SHARE = 512
        ring_flat = ring[:, :, :, :].rearrange("p u k n -> p (u k n)")
        raw = [ring_flat[:, p * PIECE:(p + 1) * PIECE] for p in range(3)]
        parts = later("weight_parts", acts_base, 0, [P, 2, 3, 2, PIECE])
        rowsT = [later("rowsT_parts0", ring_base, 3 * PIECE, [P, 2, KD, P]),
                 later("rowsT_parts1", region_a_base, 4224, [P, 2, KD, P])]
        hidT = later("hidT_parts", mqT_base, 0, [P, 2, 2, KF, P])
        rows = [fac[:, 0:2, :].rearrange("p a n -> p (a n)"), mqT[:, 1, :]]
        y_rows = [region_a[:, 6272:6272 + D], qk[:, :, :, :].rearrange("p a h t -> p (a h t)")]
        silu = [mix[:, :, :].rearrange("p h d -> p (h d)")[:, u * FF:(u + 1) * FF] for u in range(2)]
        hid = [gate[:, :, :].rearrange("p h d -> p (h d)")[:, u * FF:(u + 1) * FF] for u in range(2)]
        final_gain = region_a[:, 3200:4224]
        y_a = acts[:, 0:2 * D].rearrange("p (u n) -> p u n", u=2)
        y_b = acts[:, 2 * D:4 * D].rearrange("p (u n) -> p u n", u=2)
        h_in = acts[:, 4 * D:6 * D].rearrange("p (u n) -> p u n", u=2)
        o_out = acts[:, 6 * D:8 * D].rearrange("p (u n) -> p u n", u=2)
        f_junk = acts[:, 8 * D:10 * D].rearrange("p (u n) -> p u n", u=2)

        G, E, TG, TE = GROUPS, EXPERTS, TILES * GROUPS, TILES * EXPERTS
        g_max, e_top, e_second = small(0, TILES), small(8, TILES), small(16, TILES)
        g_prob, w_first, w_sec, seen = small(24, TILES), small(32, TILES), small(40, TILES), small(48, TILES)
        g_exp, g_hot = small(64, TILES, G), small(96, TILES, G)
        e_in, e_rest = small(128, TILES, PER), small(160, TILES, PER)
        a_hot, b_hot, equal = small(192, TILES, PER), small(224, TILES, PER), small(256, TILES, PER)
        picked = small(320, TILES, G, PER)
        a_all, b_all = small(448, TILES, G, PER), small(576, TILES, G, PER)
        member = small(704, TILES, E)
        carry = small(832, TILES + 1, E)
        rank, code, prod = small(1024, TILES, E), small(1152, TILES, E), small(1280, TILES, E)
        extra, extra_upto, code_low, code_high = small(1408, E), small(1424, E), small(1440, E), small(1456, E)
        slot_f, row_f, block_f = small(1488, 2, TILES), small(1504, 2, TILES), small(1520, 2, TILES)
        token_id = small(1536, TILES)
        weight = small(1552, 2, TILES)
        upto_cmp = small(4224, EXTRA, E)
        block_iota, row_iota = small(1856, COLS), small(1920, P)
        tri = small(2048, P)
        ones = small(2176, P)
        expert_f = small(2304, COLS)
        one_minus = small(2368, E)
        expert_base = small(2384, E)
        ints = rt[:, 2560:3200].bitcast(i32)
        slot_i, row_i, block_i = ints[:, 0:16], ints[:, 16:32], ints[:, 32:48]
        token_table = ints[:, 64:64 + COLS]
        expert_table = ints[:, 128:128 + COLS]
        extra_pairs = ints[:, 200:200 + E]
        iota_i = ints[:, 256:256 + P]
        idx_tile = ints[:, 400:402]
        slot_tile = ints[:, 410:414]
        halves = rt[:, 3200:3200 + 1024].bitcast(f16)
        row_hot = [halves[:, u * P:(u + 1) * P] for u in range(2)]
        block_hot = [halves[:, 512 + u * 64:512 + u * 64 + COLS] for u in range(2)]

        def job_result(job, n):
            _, kind, g, s = job
            bank = psum[4 + n % 4]
            half = slice(s * 512, s * 512 + 512)
            if kind == "mem_k":
                return mem_kT[:, g, :], bank[:, 0:N_MEM], 1.0
            if kind == "mem_v":
                return mem_v[:, g, :], bank[:, 0:MEMW], 1.0
            if kind == "rank":
                return rT[:, half], bank[0:RANK, :], 1.0
            if kind == "mem_q":
                return mqT[:, g, half], bank[:, :], 1.0
            if kind == "k":
                return kT[:, g, half], bank[:, :], 1.0
            if kind == "q":
                return qT[:, g, half], bank[:, :], Q_SCALE
            return vg[:, s, g * 512:(g + 1) * 512], bank[:, :], 1.0

        def at_tile(t):
            return slice(t * P, t * P + P) if isinstance(t, int) else ds(t * P, P)

        def one_tile(t):
            return slice(t, t + 1) if isinstance(t, int) else ds(t, 1)

        def hold(eng, sem, value):
            if not (isinstance(value, int) and value <= 0):
                eng.wait_ge(sem, value)

        def is_zero(v):
            return isinstance(v, int) and v == 0

        def ahead(i, u):
            return (i + u, 1 - u)

        def behind(i, u):
            return (i - (1 - u), 1 - u)

        def number(i, u):
            return i * 2 + u

        FIXED = EXPERTS // 2

        def all_pairs(eng, step):
            for u in range(2):
                step(0, u)
            with eng.Fori(1, FIXED) as i:
                for u in range(2):
                    step(i, u)
            extra = eng.value_load(extra_pairs[0:1, E - 1:E], min_val=0, max_val=PAIRS - FIXED)
            with eng.Fori(0, PAIRS - FIXED) as g:
                with eng.If(extra > g):
                    for u in range(2):
                        step(g + FIXED, u)
            return extra

        block = ctx.enter_context(nc.Block())

        @block.sync
        def _(sp):
            sp.dma_start(mix_gain, mix_norm[0:1, :].partition_broadcast(P).rearrange("p a n -> p (a n)")).then_inc(gains_loaded, 16)
            sp.dma_start(mem_gain, mem_norm[0:1, :].partition_broadcast(P).rearrange("p a n -> p (a n)")).then_inc(gains_loaded, 16)

            def chunk(c):
                src, at, n = CHUNKS[c]
                if c >= 2:
                    j = last_job(c - 2)
                    sp.wait_ge(job_filled[j % 4], j // 4 + 1)
                sp.dma_start(ring[:, c % 2, :, 0:n], src[:, :, at:at + n]).then_inc(chunk_loaded[c % 2], 16)

            with sp.Fori(0, TILES // 2) as i:
                for u in range(2):
                    sp.wait_ge(norm_ready[u], i)
                    sp.dma_start(x_in[:, u, :], x[0, ds((i * 2 + u) * P, P), :]).then_inc(x_loaded[u], 16)
            for u in range(2):
                sp.wait_ge(norm_ready[u], TILES // 2)
                sp.dma_start(x_in[:, u, :], mem[0, u * P:(u + 1) * P, :]).then_inc(x_loaded[u], 16)
            for c in range(len(CHUNKS)):
                chunk(c)

            sp.wait_ge(job_filled[(len(JOBS) - 1) % 4], (len(JOBS) - 1) // 4 + 1)
            sp.dma_start(ffn_gain, ffn_norm[0:1, :].partition_broadcast(P).rearrange("p a n -> p (a n)")).then_inc(ffn_gain_loaded, 16)
            sp.wait_ge(zeros_built, 1)
            CLEAR = (BLOCKS - EXPERTS) * P // TILES
            assert CLEAR % P == 0
            with sp.Fori(0, TILES) as t:
                rows_of_y = y_dram[ds(t * CLEAR + EXPERTS * P, CLEAR), :].rearrange("(p b) (a n) -> p (b a) n", p=P, n=256)
                sp.dma_start(rows_of_y, zeros.unsqueeze(1).to_broadcast([P, CLEAR // P * (D // 256), 256])).then_inc(y_cleared, 16)
                sp.wait_ge(h_stored, t * 16)
                sp.wait_ge(u_ready, t)
                sp.dma_start(h_tile, x[0, ds(t * P, P), :]).then_inc(x_tile_loaded, 16)
                sp.wait_ge(drained[3], t * 3 + 3)
                sp.dma_start(h_dram[ds(t * P, P), :], h_tile).then_inc(h_stored, 16)
                sp.wait_ge(u_ready, t + 1)
                sp.dma_start(u_dram[ds(t * P, P), :], u_tile).then_inc(u_stored, 16)

            def load_piece(i, u, p):
                j = number(i, u)
                static = isinstance(j, int) and j < EXPERTS
                if not static:
                    sp.wait_ge(tables_ready, 1)
                e = j if static else sp.value_load(expert_table[0:1, ds(j, 1)], min_val=0, max_val=EXPERTS - 1)
                hold(sp, part_low_dve[p], j)
                hold(sp, part_low_pool[p], j)
                one = slice(e, e + 1) if static else ds(e, 1)
                if p < 2:
                    src = up_rows[one, :, p * KD // 2:(p + 1) * KD // 2, :]
                else:
                    src = down_rows[one, :, :, :]
                width = src.shape[-1]
                sp.dma_start(raw[p].rearrange("p (k n) -> p k n", n=width), src.rearrange("e p k n -> p (e k) n")).then_inc(raw_loaded[p], 16)

            def store_y(i, u):
                j = number(i, u)
                sp.wait_ge(y_left, j + 1)
                sp.wait_ge(y_right, j + 1)
                sp.dma_start(y_dram[ds(j * P, P) if not isinstance(j, int) else slice(j * P, (j + 1) * P), :], y_rows[u]).then_inc(y_stored[u], 16)

            def step_sp(i, u):
                for p in range(2):
                    load_piece(*ahead(i, u), p)
                load_piece(i, u, 2)
                if not is_zero(i):
                    store_y(i - 1, u)

            sp.wait_ge(y_cleared, 16 * TILES)
            sp.wait_ge(filled[3], TILES * USES[3])
            for p in range(2):
                load_piece(0, 0, p)
            more = all_pairs(sp, step_sp)
            last = more + (FIXED - 1)
            for u in range(2):
                store_y(last, u)

            for u in range(2):
                sp.wait_ge(y_stored[u], more * 16 + 16 * FIXED)
            sp.dma_start(final_gain, final_norm.rearrange("(a n) -> a n", a=1).partition_broadcast(P).rearrange("p a n -> p (a n)")).then_inc(final_gain_loaded, 16)
            with sp.Fori(0, TILES // 2) as i:
                for u in range(2):
                    sp.wait_ge(out_ready, i * 2)
                    sp.dma_start(h_in[:, u, :], h_dram[ds((i * 2 + u) * P, P), :]).then_inc(h_loaded[u], 16)
                for u in range(2):
                    sp.wait_ge(out_ready, i * 2 + (u + 1))
                    sp.dma_start(out[0, ds((i * 2 + u) * P, P), :], o_out[:, u, :]).then_inc(out_stored[u], 16)
            for u in range(2):
                sp.wait_ge(out_stored[u], 16 * (TILES // 2))

        @block.gpsimd
        def _(pool):
            c = Chain(pool, pool_step)
            pool.dma_start(b_gate[:, :], gla_b_gate[0].rearrange("(h p) -> p h", p=P), allow_slow_non_contiguous=True).then_inc(small_loaded, 16)
            pool.dma_start(w_gate, gla_w_gate_up[0]).then_inc(small_loaded, 16)
            pool.dma_start(out_gain[:, :, :], gla_out_norm[0:1, :].partition_broadcast(P)).then_inc(out_gain_loaded, 16)
            pool.dma_start(w_route[:, :, 0:G], w_group[0].rearrange("(k p) n -> p k n", p=P), allow_slow_non_contiguous=True).then_inc(small_loaded, 16)
            pool.dma_start(w_route[:, :, G:G + E], w_router[0].rearrange("(k p) n -> p k n", p=P), allow_slow_non_contiguous=True).then_inc(small_loaded, 16)
            pool.dma_start(b_route[:, 0:G], b_group[0:1, :].partition_broadcast(P).rearrange("p a n -> p (a n)")).then_inc(small_loaded, 16)
            pool.dma_start(b_route[:, G:G + E], b_router[0:1, :].partition_broadcast(P).rearrange("p a n -> p (a n)")).then_inc(small_loaded, 16)
            mask_rows = acts[:, 16384:16384 + 3 * P].bitcast(i32)
            pool.iota(mask_rows[:, 0:P], [[1, P]], base=0, channel_multiplier=0)
            pool.iota(mask_rows[:, P:2 * P], [[0, P]], base=0, channel_multiplier=1).then_inc(masks_built, 1)
            pool.memset(eps[:, :], EPS)
            pool.memset(minus_half[:, :], -0.5).then_inc(half_built, 1)
            c.link(pool.memset(ident[:, :], 0.0))
            pool.affine_select(out=ident[:, :], in_=ident[:, :], compare_op=ALU.not_equal, fill=1.0, base=0,
                               pattern=[[-1, P]], channel_multiplier=1).then_inc(ident_built, 1)
            pool.wait_ge(half_built, 1)

            def wait_apart(*waits):
                for s, v in waits:
                    pool.wait_ge(s, v)
                pool.tensor_tensor(spare[:, 0:1], minus_half[:, 0:1], minus_half[:, 0:1], ALU.mult)

            def rms(dst, mean, src, width):
                c.link(pool.tensor_tensor(mean, src, eps[:, 0:width], ALU.add))
                return pool.tensor_tensor(dst, mean, minus_half[:, 0:width], ALU.pow)

            def tile_norm(i, u):
                pool.wait_ge(sumsq_ready[u], i + 1)
                rms(rstd[:, u:u + 1], meansq[:, u:u + 1], sumsq[:, u:u + 1], 1).then_inc(rstd_ready[u], 1)

            with pool.Fori(0, TILES // 2) as i:
                c.enter(i, 2)
                c.mark()
                for u in range(2):
                    tile_norm(i, u)
            c.leave(TILES // 2)
            for u in range(2):
                tile_norm(TILES // 2, u)

            for u in range(2):
                pool.wait_ge(gate_summed[u], len(GATE_JOBS) // 2)
            pool.wait_ge(out_gain_loaded, 16)
            c.link(pool.tensor_scalar(out_gain[:, :, :], out_gain[:, :, :], 0.5, None, ALU.mult))
            for b in range(4):
                pool.wait_ge(job_drained[b], len(range(b, len(JOBS), 4)))

            pool.memset(zeros, 0.0).then_inc(zeros_built, 1)

            def exponent(t, f):
                bt = bT[:, :, at_tile(t)]
                hold(pool, fac_used[f % 3], t * 3 + f // 3)
                if f == 0:
                    f0 = fac[:, 0, :].rearrange("p (h t) -> p h t", h=HEADS)
                    pool.tensor_tensor(f0, bt[:, :, P - 1:P].to_broadcast([P, HEADS, P]), bt, ALU.subtract).then_inc(arg_ready, 1)
                    return
                s = (P // 2) >> (f - 2)
                fh = fac[:, f % 3, :].rearrange("p (h b a s) -> p h b a s", h=HEADS, a=2, s=s)
                bh = bt.rearrange("p h (b a s) -> p h b a s", a=2, s=s)
                mid = bh[:, :, :, 1, 0:1].to_broadcast([P, HEADS, P // (2 * s), s])
                pool.tensor_tensor(fh[:, :, :, 0, :], mid, bh[:, :, :, 0, :], ALU.subtract)
                pool.tensor_tensor(fh[:, :, :, 1, :], bh[:, :, :, 1, :], mid, ALU.subtract).then_inc(arg_ready, 1)

            def mix_pool(t, s):
                if t is not None:
                    for f in (0, 2, 3):
                        exponent(t, f)
                if s is not None:
                    pool.wait_ge(o_sumsq_ready, s + 1)
                    rms(o_rstd, o_meansq, o_sumsq, 4).then_inc(o_rstd_ready, 1)
                    pool.wait_ge(drained[2], s * 3 + 1)
                    pool.wait_ge(drained[3], s * 3 + 1)
                    pool.tensor_tensor(mix[:, :, :], mix[:, :, :], gate[:, :, :], ALU.mult).then_inc(mix_ready, 1)
                if t is not None:
                    for f in range(4, LEVELS + 2):
                        exponent(t, f)
                    g_t = vg[:, one_tile(t), MIX:2 * MIX].rearrange("p a (h d) -> p (a h) d", h=HEADS)
                    wait_apart((tanh_ready, t + 1))
                    c.link(pool.tensor_tensor(gate[:, :, :], gate[:, :, :], g_t, ALU.mult))
                    wait_apart()
                    c.link(pool.tensor_tensor(gate[:, :, :], gate[:, :, :], g_t, ALU.add))
                    c.link(pool.tensor_tensor(gate[:, :, :], gate[:, :, :], out_gain[:, :, :].to_broadcast([P, HEADS, DV]), ALU.mult))
                if s is not None:
                    pool.wait_ge(h_sumsq_ready, s + 1)
                    rms(h_rstd, h_meansq, h_sumsq, 1).then_inc(h_rstd_ready, 1)

            mix_pool(0, None)
            with pool.Fori(1, TILES) as t:
                c.enter(t - 1, 5)
                c.mark()
                mix_pool(t, t - 1)
            c.leave(TILES - 1)
            mix_pool(None, TILES - 1)

            pool.wait_ge(drained[7], TILES * USES[7])
            pool.wait_ge(u_stored, 16 * TILES)
            pool.wait_ge(h_stored, 16 * TILES)
            c.link(pool.memset(ones, 1.0))
            c.link(pool.affine_select(out=tri, in_=ones, compare_op=ALU.is_gt, fill=0.0, base=0,
                                      pattern=[[1, P]], channel_multiplier=-1))
            c.link(pool.iota(iota_i[:, 0:P], [[1, P]], base=0, channel_multiplier=0))
            c.link(pool.tensor_copy(row_iota, iota_i[:, 0:P]))
            c.link(pool.tensor_copy(block_iota, iota_i[:, 0:COLS]))
            c.link(pool.tensor_scalar(expert_base, iota_i[:, 0:E], float(P), None, ALU.mult))
            c.link(pool.iota(iota_i[:, 0:TILES], [[P, TILES]], base=0, channel_multiplier=1))
            pool.tensor_copy(token_id, iota_i[:, 0:TILES]).then_inc(ones_built, 1)

            pool.wait_ge(tables_ready, 1)

            def gather(i, u):
                j = number(i, u)
                pool.tensor_copy(idx_tile[:, u:u + 1], token_table[:, slice(j, j + 1) if isinstance(j, int) else ds(j, 1)]).then_inc(idx_ready, 1)
                wait_apart((idx_ready, j + 1))
                pool.indirect_dma_start(rows[u], None, u_dram, bass.IndirectOffsetOnAxis(idx_tile[:, u:u + 1], 0)).then_inc(gathered[u], 16)

            def split_low(i, u, p):
                pool.wait_ge(part_high[p], number(i, u) + 1)
                share = slice(PIECE - POOL_SHARE, PIECE)
                pool.tensor_tensor(parts[:, u, p, 1, share], raw[p][:, share], parts[:, u, p, 0, share].bitcast(f32), ALU.subtract).then_inc(part_low_pool[p], 1)

            def step_pool(i, u):
                pool.wait_ge(gathered[u], (i + 1) * 16)
                pool.wait_ge(rows_filled[1], number(i, u) + 1)
                gather(i + 1, u)
                for p in range(2):
                    split_low(*ahead(i, u), p)
                split_low(i, u, 2)

            for u in range(2):
                gather(0, u)
            for p in range(2):
                split_low(0, 0, p)
            more = all_pairs(pool, step_pool)

            for u in range(2):
                pool.wait_ge(y_stored[u], more * 16 + 16 * FIXED)
            for p in range(2):
                pool.wait_ge(part_low_dve[p], more * 2 + (2 * FIXED + 1))
            pool.tensor_tensor(spare[:, 0:1], minus_half[:, 0:1], minus_half[:, 0:1], ALU.mult)
            with pool.Fori(0, TILES // 2) as i:
                c.enter(i, 2)
                c.mark()
                for u in range(2):
                    pool.wait_ge(out_ready, i * 2)
                    pool.wait_ge(ya_loaded[u], i * 16)
                    pool.wait_ge(yb_loaded[u], i * 16)
                    for choice, dst, loaded in ((0, y_a, ya_loaded), (1, y_b, yb_loaded)):
                        pool.tensor_copy(slot_tile[:, 2 * u + choice:2 * u + choice + 1],
                                         slot_i[:, ds(i * 2 + (u + choice * TILES), 1)]).then_inc(slot_copied, 1)
                        wait_apart((slot_copied, i * 4 + (2 * u + choice + 1)))
                        pool.indirect_dma_start(dst[:, u, :], None, y_dram,
                                                bass.IndirectOffsetOnAxis(slot_tile[:, 2 * u + choice:2 * u + choice + 1], 0)).then_inc(loaded[u], 16)
                for u in range(2):
                    pool.wait_ge(f_sumsq, i * 2 + (u + 1))
                    rms(rstd[:, u:u + 1], meansq[:, u:u + 1], sumsq[:, u:u + 1], 1).then_inc(f_rstd, 1)
            c.leave(TILES // 2)

        @block.scalar
        def _(act):
            def square_tile(i, u):
                act.wait_ge(x_loaded[u], i * 16 + 16)
                act.activation(junk[:, u, :], x_in[:, u, :], ACT.Square, scale=D ** -0.5, accum_out=sumsq[:, u:u + 1]).then_inc(sumsq_ready[u], 1)

            def evac_low(i, u, dst):
                act.wait_ge(x_transposed[u], i + 1)
                act.activation(dst, cols(2 * u, 512, 4), ACT.Copy).then_inc(xT_low[u], 1)

            with act.Fori(0, TILES // 2) as i:
                for u in range(2):
                    square_tile(i, u)
                for u in range(2):
                    evac_low(i, u, xT[:, 0:4, ds((i * 2 + u) * P, P)])
            for u in range(2):
                square_tile(TILES // 2, u)
            for u in range(2):
                evac_low(TILES // 2, u, memT[:, 0:4, u * P:(u + 1) * P])

            act.wait_ge(small_loaded, 16 * 6)
            for n, job in enumerate(JOBS):
                if n == GATES_BEFORE:
                    for m, (h, s) in enumerate(GATE_JOBS):
                        u = m % 2
                        act.wait_ge(gate_min[u], m // 2 + 1)
                        if m >= 2:
                            act.wait_ge(gate_summed[u], m // 2)
                        act.activation(log_term[u], psum[2 + u][:, :], ACT.Abs, bias=b_gate[:, h:h + 1]).then_inc(gate_log[u], 1)
                        act.wait_ge(gate_log[u], m // 2 * 3 + 1)
                        act.activation(log_term[u], log_term[u], ACT.Exp, scale=-1.0).then_inc(gate_log[u], 1)
                        act.wait_ge(gate_log[u], m // 2 * 3 + 2)
                        act.activation(log_term[u], log_term[u], ACT.Ln, bias=1.0).then_inc(gate_log[u], 1)
                if n % 2 == 0:
                    act.wait_ge(job_filled[n % 4], n // 4 + 1)
                    dst, src, scale = job_result(job, n)
                    act.activation(dst, src, ACT.Copy, scale=scale).then_inc(job_drained[n % 4], 1)

            for u in range(2):
                act.wait_ge(gate_summed[u], len(GATE_JOBS) // 2)
            for b in (1, 3):
                act.wait_ge(job_drained[b], len(range(b, len(JOBS), 4)))

            def factor(t, f):
                if f == 1:
                    hold(act, fac_used[1], t * 3)
                    act.activation(fac[:, 1, :].rearrange("p (h t) -> p h t", h=HEADS), bT[:, :, at_tile(t)], ACT.Exp,
                                   scale=GATE_SCALE).then_inc(exp_ready, 1)
                else:
                    act.wait_ge(arg_ready, t * 8 + max(f, 1))
                    act.activation(fac[:, f % 3, :], fac[:, f % 3, :], ACT.Exp, scale=GATE_SCALE).then_inc(exp_ready, 1)

            def mix_act(t, s):
                if t is not None:
                    for f in range(4):
                        factor(t, f)
                if s is not None:
                    hold(act, o_sumsq_ready, s)
                    for b in (3, 2):
                        act.wait_ge(filled[b], s * 3 + 1)
                        ins = act.activation(o_sq[:, 2 * (b - 2):2 * (b - 1), :], cols(b, 2 * DV, 2), ACT.Square, scale=DV ** -0.5)
                    ins.then_inc(o_sq_ready, 1)
                if t is not None:
                    act.wait_ge(filled[6], t * 2 + 1)
                    hold(act, filled[5], t * 3)
                    act.activation(k_decayedT[:, :, :], heads_of(6), ACT.Copy).then_inc(drained[6], 1)
                    hold(act, drained[5], t * 3)
                    act.activation(decay_all.unsqueeze(2), bT[:, :, at_tile(t)][:, :, P - 1:P], ACT.Exp, scale=GATE_SCALE).then_inc(decay_ready, 1)
                    factor(t, 4)
                    act.wait_ge(negmax_ready, t + 1)
                    hold(act, probs_ready, t)
                    hold(act, filled[5], t * 3)
                    for n in range(MHEADS):
                        ins = act.activation(probs[:, n, :], cols(4 + n // 2, 512, 2)[:, n % 2, :], ACT.Exp,
                                             bias=neg_max[:, n:n + 1], scale=M_SCALE, accum_out=row_sum[:, n:n + 1])
                        if n % 2:
                            ins.then_inc(drained[4 + n // 2], 1)
                    factor(t, 5)
                if s is not None:
                    act.wait_ge(filled[7], s * 3 + 1)
                    hold(act, filled[3], s * 3)
                    act.activation(catT[:, 0:4, :], heads_of(7), ACT.Copy).then_inc(drained[7], 1)
                if t is not None:
                    for f in range(6, LEVELS + 2):
                        factor(t, f)
                    g_t = vg[:, one_tile(t), MIX:2 * MIX].rearrange("p a (h d) -> p (a h) d", h=HEADS)
                    hold(act, mix_ready, t)
                    act.activation(gate[:, :, :], g_t, ACT.Tanh, scale=0.5).then_inc(tanh_ready, 1)
                    act.wait_ge(filled[5], t * 3 + 2)
                    hold(act, filled[6], t * 2)
                    act.activation(probsT[:, 2:4, :, :].rearrange("p h m t -> p (h m) t"), heads_of(5), ACT.Copy).then_inc(drained[5], 1)
                if s is not None:
                    act.wait_ge(drained[2], s * 3 + 2)
                    act.wait_ge(drained[3], s * 3 + 3)
                    hold(act, u_stored, s * 16)
                    act.activation(u_tile, h_tile, ACT.Square, scale=D ** -0.5, accum_out=h_sumsq).then_inc(h_sumsq_ready, 1)
                    act.wait_ge(filled[7], s * 3 + 2)
                    act.activation(uT[:, 0:4, :], heads_of(7), ACT.Copy).then_inc(drained[7], 1)

            mix_act(0, None)
            with act.Fori(1, TILES) as t:
                mix_act(t, t - 1)
            mix_act(None, TILES - 1)

            act.wait_ge(exp_arg, 1)
            act.activation(g_exp, g_exp, ACT.Exp).then_inc(exp_done, 1)
            act.wait_ge(exp_arg, 2)
            act.activation(w_sec, w_sec, ACT.Exp).then_inc(exp_done, 1)

            def split_high(i, u, p):
                j = number(i, u)
                act.wait_ge(raw_loaded[p], j * 16 + 16)
                hold(act, part_used[p], j - 1)
                act.activation(parts[:, u, p, 0, :], raw[p], ACT.Copy).then_inc(part_high[p], 1)

            def rows_high(i, u):
                for b in range(2):
                    act.wait_ge(rows_filled[b], number(i, u) + 1)
                    act.activation(rowsT[u][:, 0, 4 * b:4 * b + 4, :], heads_of(b), ACT.Copy).then_inc(rowsT_high[b], 1)

            def hidT_split_high(i, u):
                act.wait_ge(hidT_filled, number(i, u) + 1)
                act.activation(hidT[:, u, 0, :, :], cols(3, KF * P, KF), ACT.Copy).then_inc(hidT_high, 1)

            def y_left_half(i, u):
                act.wait_ge(part_used[2], number(i, u) + 1)
                hold(act, y_stored[u], i * 16)
                act.activation(y_rows[u][:, 0:512], psum[4][:, :], ACT.Copy).then_inc(y_left, 1)

            def step_act(i, u):
                if not is_zero(i):
                    y_left_half(i - 1, u)
                for p in range(2):
                    split_high(*ahead(i, u), p)
                split_high(i, u, 2)
                if not is_zero(number(i, u)):
                    hidT_split_high(*behind(i, u))
                rows_high(*ahead(i, u))
                act.wait_ge(part_used[1], number(i, u) + 1)
                act.activation(silu[u], psum[2 + 4 * u][:, 0:FF], ACT.Silu).then_inc(silu_ready, 1)

            for p in range(2):
                split_high(0, 0, p)
            rows_high(0, 0)
            more = all_pairs(act, step_act)
            last = more + (FIXED - 1)
            y_left_half(last, 0)
            hidT_split_high(last, 1)
            y_left_half(last, 1)

            with act.Fori(0, TILES // 2) as i:
                for u in range(2):
                    act.wait_ge(sum_ready, i * 4 + (2 * u + 2))
                    act.activation(f_junk[:, u, :], h_in[:, u, :], ACT.Square, scale=D ** -0.5, accum_out=sumsq[:, u:u + 1]).then_inc(f_sumsq, 1)

        @block.vector
        def _(dve):
            c = Chain(dve, dve_step)

            def wait_apart(*waits):
                for s, v in waits:
                    hold(dve, s, v)
                dve.memset(spare[:, 1:2], 0.0)

            iota_work = acts[:, 16384:16384 + 3 * P].bitcast(i32)
            mask_work = acts[:, 16384 + 3 * P:16384 + 5 * P]
            dve.wait_ge(masks_built, 1)
            c.link(dve.tensor_tensor(mask_work[:, 0:P], iota_work[:, 0:P], iota_work[:, P:2 * P], ALU.is_gt))
            c.link(dve.tensor_tensor(iota_work[:, 2 * P:3 * P], iota_work[:, 0:P], iota_work[:, P:2 * P], ALU.bitwise_xor))
            for lvl in range(LEVELS):
                c.link(dve.scalar_tensor_tensor(masks[:, lvl, :], iota_work[:, 2 * P:3 * P], float(P >> lvl), mask_work[:, 0:P], ALU.is_lt, ALU.mult))
            c.link(dve.tensor_scalar(masks[:, LEVELS, :], iota_work[:, 2 * P:3 * P], 0.0, None, ALU.is_equal))
            dve.memset(scoresT[:, :, :], 0.0)
            dve.memset(state[:, :, :], 0.0).then_inc(state_zero, 1)

            dve.wait_ge(gains_loaded, 32)

            def norm_tile(i, u, gain):
                dve.wait_ge(rstd_ready[u], i + 1)
                dve.wait_ge(x_loaded[u], i * 16 + 16)
                dve.wait_ge(x_transposed[u], i)
                dve.scalar_tensor_tensor(x_norm[:, u, :], x_in[:, u, :], rstd[:, u:u + 1], gain, ALU.mult, ALU.mult).then_inc(norm_ready[u], 1)

            def evac_high(i, u, dst):
                dve.wait_ge(x_transposed[u], i + 1)
                dve.tensor_copy(dst, cols(2 * u + 1, 512, 4)).then_inc(xT_high[u], 1)

            with dve.Fori(0, TILES // 2) as i:
                for u in range(2):
                    norm_tile(i, u, mix_gain)
                for u in range(2):
                    evac_high(i, u, xT[:, 4:8, ds((i * 2 + u) * P, P)])
            for u in range(2):
                norm_tile(TILES // 2, u, mem_gain)
            for u in range(2):
                evac_high(TILES // 2, u, memT[:, 4:8, u * P:(u + 1) * P])

            dve.wait_ge(small_loaded, 16 * 6)
            for n, job in enumerate(JOBS):
                if n == GATES_BEFORE:
                    for m, (h, s) in enumerate(GATE_JOBS):
                        u = m % 2
                        dve.wait_ge(gate_filled[u], m // 2 + 1)
                        if m >= 2:
                            dve.wait_ge(gate_summed[u], m // 2)
                        dve.tensor_scalar(min_term[u], psum[2 + u][:, :], b_gate[:, h:h + 1], 0.0, ALU.add, ALU.min).then_inc(gate_min[u], 1)
                        dve.wait_ge(gate_min[u], m // 2 + 1)
                        dve.wait_ge(gate_log[u], m // 2 * 3 + 3)
                        for q in range(4):
                            part = slice(q * P, (q + 1) * P)
                            ins = dve.tensor_tensor_scan(bT[:, h, s * 512 + q * P:s * 512 + (q + 1) * P], min_term[u][:, part],
                                                         log_term[u][:, part], 0.0, ALU.add, ALU.subtract)
                        ins.then_inc(gate_summed[u], 1)
                if n % 2 == 1:
                    dve.wait_ge(job_filled[n % 4], n // 4 + 1)
                    dst, src, scale = job_result(job, n)
                    dve.tensor_scalar(dst, src, scale, None, ALU.mult).then_inc(job_drained[n % 4], 1)

            dve.wait_ge(state_zero, 1)
            for b in (0, 2):
                dve.wait_ge(job_drained[b], len(range(b, len(JOBS), 4)))
            dve.wait_ge(ffn_gain_loaded, 16)

            def heads_done(t):
                return 0 if isinstance(t, int) and t == 0 else (t - 1) * 3 + 1

            def level(t, lvl):
                f, s = lvl + 2, (P // 2) >> lvl
                dve.wait_ge(exp_ready, t * 9 + (f + 1))
                hold(dve, filled[lvl % 2], t * 4 + lvl // 2)
                fh = fac[:, f % 3, :].rearrange("p (h b a s) -> p h b a s", h=HEADS, a=2, s=s)
                oh = qk[:, lvl % 2, :, :].rearrange("p h (b a s) -> p h b a s", a=2, s=s)
                kh = kT[:, :, at_tile(t)].rearrange("p h (b a s) -> p h b a s", a=2, s=s)
                qh = qT[:, :, at_tile(t)].rearrange("p h (b a s) -> p h b a s", a=2, s=s)
                dve.tensor_tensor(oh[:, :, :, 0, :], kh[:, :, :, 0, :], fh[:, :, :, 0, :], ALU.mult)
                dve.tensor_tensor(oh[:, :, :, 1, :], qh[:, :, :, 1, :], fh[:, :, :, 1, :], ALU.mult).then_inc(fac_used[f % 3], 1)

            def keep(t, lvl):
                before = (filled[2], heads_done(t)) if lvl == 0 else (drained[(lvl - 1) % 2], t * 4 + ((lvl - 1) // 2 + 1))
                wait_apart((filled[lvl % 2], t * 4 + (lvl // 2 + 1)), before)
                mask = masks[:, lvl:lvl + 1, :].to_broadcast([P, HEADS, P])
                dve.copy_predicated(scoresT[:, :, :], mask, heads_of(lvl % 2)).then_inc(drained[lvl % 2], 1)

            def mix_dve(t, s):
                fac_heads = [fac[:, f, :].rearrange("p (h t) -> p h t", h=HEADS) for f in range(2)]
                if t is not None:
                    kt, qt = kT[:, :, at_tile(t)], qT[:, :, at_tile(t)]
                    dve.wait_ge(exp_ready, t * 9 + 1)
                    hold(dve, filled[6], t * 2)
                    dve.tensor_tensor(k_decayed[:, :, :], kt, fac_heads[0], ALU.mult).then_inc(fac_used[0], 1)
                    hold(dve, filled[5], t * 3)
                    dve.tensor_scalar(mq_tile[:, :, :], mqT[:, :, at_tile(t)], 1.0, None, ALU.mult).then_inc(mq_ready, 1)
                    level(t, 0)
                    level(t, 1)
                if s is not None:
                    for b in (4, 5):
                        dve.wait_ge(filled[b], s * 3 + 3)
                    for b in (2, 3):
                        dve.wait_ge(filled[b], s * 3 + 1)
                    dve.wait_ge(decay_ready, s + 1)
                    for h in range(HEADS):
                        ins = dve.scalar_tensor_tensor(state[:, h, :], state[:, h, :], decay_all[:, h:h + 1],
                                                       cols(4 + h // 2, 2 * DV, 2)[:, h % 2, :], ALU.mult, ALU.add)
                        if h % 2:
                            ins.then_inc(drained[4 + h // 2], 1)
                    dve.wait_ge(o_sq_ready, s + 1)
                    hold(dve, o_rstd_ready, s)
                    dve.tensor_reduce(o_sumsq, o_sq[:, :, :], AX.X, ALU.add).then_inc(o_sumsq_ready, 1)
                if t is not None:
                    dve.wait_ge(exp_ready, t * 9 + 2)
                    hold(dve, filled[2], heads_done(t))
                    dve.tensor_tensor(q_decayed[:, :, :], qt, fac_heads[1], ALU.mult).then_inc(fac_used[1], 1)
                if s is not None:
                    dve.wait_ge(o_rstd_ready, s + 1)
                    hold(dve, filled[3], s * 3)
                    for b in (3, 2):
                        dve.tensor_tensor(mix[:, 2 * (b - 2):2 * (b - 1), :], cols(b, 2 * DV, 2),
                                          o_rstd[:, 2 * (b - 2):2 * (b - 1)].unsqueeze(2).to_broadcast([P, 2, DV]), ALU.mult).then_inc(drained[b], 1)
                if t is not None:
                    hold(dve, drained[5], t * 3)
                    for b in (4, 5):
                        dve.wait_ge(filled[b], t * 3 + 1)
                        c.link(dve.tensor_reduce(neg_max[:, 2 * (b - 4):2 * (b - 3)], cols(b, 512, 2), AX.X, ALU.max, negate=True))
                    dve.tensor_scalar(neg_max, neg_max, M_SCALE, None, ALU.mult).then_inc(negmax_ready, 1)
                    keep(t, 0)
                    level(t, 2)
                if s is not None:
                    dve.wait_ge(filled[3], s * 3 + 2)
                    dve.tensor_copy(catT[:, 4:6, :], cols(3, 2 * P, 2)).then_inc(drained[3], 1)
                if t is not None:
                    keep(t, 1)
                    level(t, 3)
                    keep(t, 2)
                    level(t, 4)
                    dve.wait_ge(drained[4], t * 3 + 1)
                    dve.wait_ge(drained[5], t * 3 + 1)
                    c.link(dve.reciprocal(row_inv, row_sum))
                    dve.tensor_tensor(probs[:, :, :], probs[:, :, :], row_inv.unsqueeze(2).to_broadcast([P, MHEADS, N_MEM]), ALU.mult).then_inc(probs_ready, 1)
                    keep(t, 3)
                    level(t, 5)
                    keep(t, 4)
                    level(t, 6)
                    keep(t, 5)
                    dve.wait_ge(filled[1], t * 4 + 3)
                    dve.tensor_scalar(qk[:, 1, :, :], kt, 1.0, None, ALU.mult).then_inc(kd_ready, 1)
                    dve.wait_ge(filled[4], t * 3 + 2)
                    hold(dve, filled[6], t * 2)
                    dve.tensor_copy(probsT[:, 0:2, :, :].rearrange("p h m t -> p (h m) t"), heads_of(4)).then_inc(drained[4], 1)
                    keep(t, 6)
                    keep(t, 7)
                if s is not None:
                    dve.wait_ge(x_tile_loaded, s * 16 + 16)
                    for b in (2, 3):
                        dve.wait_ge(filled[b], s * 3 + b)
                        half = slice((b - 2) * 512, (b - 1) * 512)
                        dve.tensor_tensor(h_tile[:, half], h_tile[:, half], psum[b][:, :], ALU.add).then_inc(drained[b], 1)
                if t is not None:
                    dve.wait_ge(filled[6], t * 2 + 2)
                    hold(dve, filled[3], t * 3)
                    dve.tensor_copy(catT[:, 6:8, :], cols(6, 2 * P, 2)).then_inc(drained[6], 1)
                if s is not None:
                    dve.wait_ge(drained[2], s * 3 + 2)
                    dve.wait_ge(drained[3], s * 3 + 3)
                    dve.wait_ge(h_rstd_ready, s + 1)
                    hold(dve, u_stored, s * 16)
                    dve.scalar_tensor_tensor(u_tile, h_tile, h_rstd, ffn_gain, ALU.mult, ALU.mult).then_inc(u_ready, 1)
                    dve.wait_ge(filled[2], s * 3 + 3)
                    dve.tensor_copy(uT[:, 4:8, :], heads_of(2)).then_inc(drained[2], 1)
                    dve.wait_ge(filled[7], s * 3 + 3)
                    dve.tensor_tensor(logits[:, one_tile(s), :].rearrange("p a n -> p (a n)"), psum[7][:, 0:G + E], b_route[:, :], ALU.add).then_inc(drained[7], 1)

            mix_dve(0, None)
            with dve.Fori(1, TILES) as t:
                c.enter(t - 1, 3)
                c.mark()
                mix_dve(t, t - 1)
            c.leave(TILES - 1)
            mix_dve(None, TILES - 1)

            dve.wait_ge(ones_built, 1)
            dve.wait_ge(drained[7], TILES * USES[7])
            wide = [P, TILES, G]
            gl, el = logits[:, :, 0:G], logits[:, :, G:G + E].rearrange("p t (g e) -> p t g e", g=G)

            def first_of(hot, values, best):
                c.link(dve.tensor_tensor(equal, values, best.unsqueeze(2).to_broadcast(wide), ALU.is_equal))
                c.link(dve.tensor_copy(seen, equal[:, :, 0]))
                c.link(dve.tensor_copy(hot[:, :, 0], equal[:, :, 0]))
                for n in range(1, 4):
                    c.link(dve.tensor_tensor(hot[:, :, n], equal[:, :, n], seen, ALU.is_gt))
                    if n < 3:
                        c.link(dve.tensor_tensor(seen, seen, equal[:, :, n], ALU.max))

            c.link(dve.tensor_reduce(g_max, gl, AX.X, ALU.max))
            dve.tensor_tensor(g_exp, gl, g_max.unsqueeze(2).to_broadcast(wide), ALU.subtract).then_inc(exp_arg, 1)
            first_of(g_hot, gl, g_max)
            c.link(dve.tensor_tensor(picked, el, g_hot.unsqueeze(3).to_broadcast([P, TILES, G, PER]), ALU.mult))
            c.link(dve.tensor_reduce(e_in, picked.rearrange("p t g e -> p t e g"), AX.X, ALU.add))
            c.link(dve.tensor_reduce(e_top, e_in, AX.X, ALU.max))
            first_of(a_hot, e_in, e_top)
            c.link(dve.scalar_tensor_tensor(e_rest, a_hot, -3.0e38, e_in, ALU.mult, ALU.add))
            c.link(dve.tensor_reduce(e_second, e_rest, AX.X, ALU.max))
            first_of(b_hot, e_rest, e_second)
            dve.tensor_tensor(w_sec, e_second, e_top, ALU.subtract).then_inc(exp_arg, 1)
            dve.wait_ge(exp_done, 2)
            c.link(dve.tensor_reduce(g_prob, g_exp, AX.X, ALU.add))
            c.link(dve.tensor_scalar(w_first, w_sec, 1.0, None, ALU.add))
            c.link(dve.tensor_tensor(w_first, w_first, g_prob, ALU.mult))
            c.link(dve.reciprocal(weight[:, 0, :], w_first))
            c.link(dve.tensor_tensor(weight[:, 1, :], weight[:, 0, :], w_sec, ALU.mult))
            for full, hot in ((a_all, a_hot), (b_all, b_hot)):
                c.link(dve.tensor_tensor(full, g_hot.unsqueeze(3).to_broadcast([P, TILES, G, PER]),
                                         hot.unsqueeze(2).to_broadcast([P, TILES, G, PER]), ALU.mult))
            a_te, b_te = (v.rearrange("p t g e -> p t (g e)") for v in (a_all, b_all))
            dve.tensor_tensor(member, a_te, b_te, ALU.add).then_inc(member_ready, 1)
            c.link(dve.memset(carry[:, 0, :], 0.0))
            dve.wait_ge(rank_filled, 1)
            ranks, totals = cols(0, TE, TILES), cols(1, TE, TILES)
            for t in range(TILES):
                c.link(dve.tensor_tensor(carry[:, t + 1, :], carry[:, t, :], totals[:, t, :], ALU.add))
            c.link(dve.tensor_tensor(rank, ranks, carry[:, 0:TILES, :], ALU.add))
            count = carry[:, TILES, :]
            c.link(dve.tensor_scalar(extra, count, float(P), None, ALU.is_gt))
            for m in range(2, T // P):
                c.link(dve.scalar_tensor_tensor(extra, count, float(P * m), extra, ALU.is_gt, ALU.add))
            c.link(dve.memset(one_minus, 1.0))
            c.link(dve.tensor_tensor_scan(extra_upto, one_minus, extra, 0.0, ALU.mult, ALU.add))
            c.link(dve.tensor_tensor(code_high, extra_upto, extra, ALU.subtract))
            c.link(dve.tensor_scalar(code_high, code_high, float(P), float(P * EXPERTS - P), ALU.mult, ALU.add))
            c.link(dve.tensor_tensor(code_low, expert_base, code_high, ALU.subtract))
            all_te = [P, TILES, E]
            c.link(dve.tensor_scalar(code, rank, float(P), None, ALU.is_lt))
            c.link(dve.tensor_tensor(code, code, code_low.unsqueeze(1).to_broadcast(all_te), ALU.mult))
            c.link(dve.tensor_tensor(code, code, code_high.unsqueeze(1).to_broadcast(all_te), ALU.add))
            c.link(dve.tensor_tensor(code, code, rank, ALU.add))
            for n, full in enumerate((a_te, b_te)):
                c.link(dve.tensor_tensor(prod, code, full, ALU.mult))
                c.link(dve.tensor_reduce(slot_f[:, n, :], prod, AX.X, ALU.add))
            flat = slot_f.rearrange("p a b -> p (a b)")
            c.link(dve.tensor_copy(slot_i, flat))
            c.link(dve.tensor_scalar(row_i, slot_i, P - 1, None, ALU.bitwise_and))
            c.link(dve.tensor_scalar(block_i, slot_i, 7, None, ALU.logical_shift_right))
            c.link(dve.tensor_copy(row_f.rearrange("p a b -> p (a b)"), row_i))
            c.link(dve.tensor_copy(block_f.rearrange("p a b -> p (a b)"), block_i))
            c.link(dve.tensor_tensor(upto_cmp, block_iota[:, 0:EXTRA].unsqueeze(2).to_broadcast([P, EXTRA, E]),
                                     extra_upto.unsqueeze(1).to_broadcast([P, EXTRA, E]), ALU.is_ge))
            c.link(dve.tensor_copy(expert_f[:, 0:E], block_iota[:, 0:E]))
            c.link(dve.tensor_reduce(expert_f[:, E:COLS], upto_cmp, AX.X, ALU.add))
            c.link(dve.tensor_scalar(expert_f, expert_f, float(E - 1), None, ALU.min))
            c.link(dve.tensor_copy(expert_table, expert_f))
            c.link(dve.tensor_scalar(code_low, extra_upto, 1.0, None, ALU.add))
            c.link(dve.tensor_copy(extra_pairs, code_low))
            c.link(dve.tensor_scalar(extra_pairs, extra_pairs, 1, None, ALU.logical_shift_right))
            for n in range(2 * TILES):
                u = n % 2
                if n >= 2:
                    dve.wait_ge(hot_used, n - 1)
                choice, t = n // TILES, n % TILES
                c.link(dve.tensor_scalar(row_hot[u], row_iota, row_f[:, choice, t:t + 1], None, ALU.is_equal))
                dve.tensor_scalar(block_hot[u], block_iota, block_f[:, choice, t:t + 1], token_id[:, t:t + 1],
                                  ALU.is_equal, ALU.mult).then_inc(hot_ready, 1)
            dve.wait_ge(table_filled, 1)
            dve.tensor_copy(token_table, psum[2][:, 0:COLS]).then_inc(tables_ready, 1)

            def split_low(i, u, p):
                dve.wait_ge(part_high[p], number(i, u) + 1)
                share = slice(0, PIECE - POOL_SHARE)
                dve.tensor_tensor(parts[:, u, p, 1, share], raw[p][:, share], parts[:, u, p, 0, share].bitcast(f32), ALU.subtract).then_inc(part_low_dve[p], 1)

            def rows_low(i, u):
                for b in range(2):
                    dve.wait_ge(rowsT_high[b], number(i, u) + 1)
                    ins = dve.tensor_tensor(rowsT[u][:, 1, 4 * b:4 * b + 4, :], heads_of(b), rowsT[u][:, 0, 4 * b:4 * b + 4, :].bitcast(f32), ALU.subtract)
                ins.then_inc(rowsT_low, 1)

            def hidT_split_low(i, u):
                dve.wait_ge(hidT_high, number(i, u) + 1)
                dve.tensor_tensor(hidT[:, u, 1, :, :], cols(3, KF * P, KF), hidT[:, u, 0, :, :].bitcast(f32), ALU.subtract).then_inc(hidT_low, 1)

            def y_right_half(i, u):
                dve.wait_ge(part_used[2], number(i, u) + 1)
                hold(dve, y_stored[u], i * 16)
                dve.tensor_copy(y_rows[u][:, 512:1024], psum[5][:, :]).then_inc(y_right, 1)

            def step_dve(i, u):
                if not is_zero(i):
                    y_right_half(i - 1, u)
                for p in range(2):
                    split_low(*ahead(i, u), p)
                split_low(i, u, 2)
                if not is_zero(number(i, u)):
                    hidT_split_low(*behind(i, u))
                rows_low(*ahead(i, u))
                dve.wait_ge(silu_ready, number(i, u) + 1)
                dve.tensor_tensor(hid[u], psum[2 + 4 * u][:, FF:2 * FF], silu[u], ALU.mult).then_inc(hid_ready, 1)

            for p in range(2):
                split_low(0, 0, p)
            rows_low(0, 0)
            more = all_pairs(dve, step_dve)
            last = more + (FIXED - 1)
            y_right_half(last, 0)
            hidT_split_low(last, 1)
            y_right_half(last, 1)

            dve.wait_ge(final_gain_loaded, 16)
            with dve.Fori(0, TILES // 2) as i:
                for u in range(2):
                    t = i * 2 + u
                    dve.wait_ge(ya_loaded[u], i * 16 + 16)
                    dve.wait_ge(h_loaded[u], i * 16 + 16)
                    dve.scalar_tensor_tensor(h_in[:, u, :], y_a[:, u, :], weight[:, 0, ds(t, 1)], h_in[:, u, :], ALU.mult, ALU.add).then_inc(sum_ready, 1)
                    dve.wait_ge(sum_ready, i * 4 + (2 * u + 1))
                    dve.wait_ge(yb_loaded[u], i * 16 + 16)
                    dve.scalar_tensor_tensor(h_in[:, u, :], y_b[:, u, :], weight[:, 1, ds(t, 1)], h_in[:, u, :], ALU.mult, ALU.add).then_inc(sum_ready, 1)
                for u in range(2):
                    dve.wait_ge(f_rstd, i * 2 + (u + 1))
                    dve.wait_ge(sum_ready, i * 4 + (2 * u + 2))
                    dve.wait_ge(out_stored[u], i * 16)
                    dve.scalar_tensor_tensor(o_out[:, u, :], h_in[:, u, :], rstd[:, u:u + 1], final_gain, ALU.mult, ALU.mult).then_inc(out_ready, 1)

        @block.tensor
        def _(pe):
            pe.wait_ge(ident_built, 1)

            def turn(dst, src, inc=None):
                ins = pe.transpose(dst, src, ident[:, :])
                if inc is not None:
                    ins.then_inc(inc, 1)

            def transpose_tile(i, u):
                pe.wait_ge(norm_ready[u], i + 1)
                pe.wait_ge(xT_low[u], i)
                pe.wait_ge(xT_high[u], i)
                for k in range(KD):
                    turn(psum[2 * u + k // 4][:, (k % 4) * P:(k % 4 + 1) * P], x_norm[:, u, k * P:(k + 1) * P],
                         x_transposed[u] if k == KD - 1 else None)

            with pe.Fori(0, TILES // 2) as i:
                for u in range(2):
                    transpose_tile(i, u)
            for u in range(2):
                transpose_tile(TILES // 2, u)
            for u in range(2):
                pe.wait_ge(xT_low[u], TILES // 2 + 1)
                pe.wait_ge(xT_high[u], TILES // 2 + 1)

            chunk = -1
            for n, (c, kind, g, s) in enumerate(JOBS):
                if n == GATES_BEFORE:
                    pe.wait_ge(small_loaded, 16 * 6)
                    pe.wait_ge(job_drained[0], 2)
                    pe.wait_ge(job_drained[1], 2)
                    for m, (h, sh) in enumerate(GATE_JOBS):
                        u = m % 2
                        if m >= 2:
                            pe.wait_ge(gate_min[u], m // 2)
                            pe.wait_ge(gate_log[u], m // 2 * 3)
                        pe.matmul(psum[2 + u][:, :], w_gate[:, h * P:(h + 1) * P], rT[:, sh * 512:sh * 512 + 512],
                                  start=True, stop=True).then_inc(gate_filled[u], 1)
                if c != chunk:
                    chunk = c
                    pe.wait_ge(chunk_loaded[c % 2], 16 * (c // 2 + 1))
                if n >= 4:
                    pe.wait_ge(job_drained[n % 4], n // 4)
                w = ring[:, c % 2, :, :]
                bank = psum[4 + n % 4]
                half = slice(s * 512, s * 512 + 512)
                for k in range(KD):
                    if kind == "mem_k":
                        o, a, b = bank[:, 0:N_MEM], w[:, k, g * P:(g + 1) * P], memT[:, k, :]
                    elif kind == "mem_v":
                        o, a, b = bank[:, 0:MEMW], memT[:, k, g * P:(g + 1) * P], w[:, k, MEMW:2 * MEMW]
                    elif kind == "rank":
                        o, a, b = bank[0:RANK, :], w[:, k, 0:RANK], xT[:, k, half]
                    elif kind == "mem_q":
                        o, a, b = bank[:, :], w[:, k, RANK + g * P:RANK + (g + 1) * P], xT[:, k, half]
                    elif kind in ("k", "q"):
                        o, a, b = bank[:, :], w[:, k, g * P:(g + 1) * P], xT[:, k, half]
                    else:
                        o, a, b = bank[:, :], xT[:, k, s * P:(s + 1) * P], w[:, k, :]
                    ins = pe.matmul(o, a, b, start=(k == 0), stop=(k == KD - 1))
                ins.then_inc(job_filled[n % 4], 1)

            for b in range(4):
                pe.wait_ge(job_drained[b], len(range(b, len(JOBS), 4)))
            for u in range(2):
                pe.wait_ge(gate_summed[u], len(GATE_JOBS) // 2)
            for u in range(2):
                pe.wait_ge(chunk_loaded[u], 16 * len(range(u, len(CHUNKS), 2)))
            pe.wait_ge(state_zero, 1)

            def use(bank, tile, k):
                hold(pe, drained[bank], tile * USES[bank] + k)

            def out_projection(s):
                pe.wait_ge(drained[7], s * 3 + 1)
                pe.wait_ge(drained[3], s * 3 + 2)
                pe.wait_ge(drained[6], s * 2 + 2)
                use(2, s, 1)
                for b in (2, 3):
                    for k in range(KD):
                        ins = pe.matmul(psum[b][:, :], catT[:, k, :], w_out_half[b - 2][:, k, :], start=(k == 0), stop=(k == KD - 1))
                        if k == KD - 1:
                            ins.then_inc(filled[b], 1)
                        yield

            def mix_pe(t, s):
                mix_flat = mix[:, :, :].rearrange("p h d -> p (h d)")
                if t is not None:
                    v_t = vg[:, one_tile(t), 0:MIX].rearrange("p a (h d) -> p (a h) d", h=HEADS)
                    pe.wait_ge(fac_used[0], t * 3 + 1)
                    use(6, t, 0)
                    for h in range(HEADS):
                        turn(heads_of(6)[:, h, :], k_decayed[:, h, :], filled[6] if h == HEADS - 1 else None)
                    pe.wait_ge(mq_ready, t + 1)
                    for b in (4, 5):
                        use(b, t, 0)
                        part = slice((b - 4) * MHD, (b - 3) * MHD)
                        for e in range(2):
                            ins = pe.matmul(cols(b, 512, 2)[:, e, :], mq_tile[part, e, :], mem_kT[part, e, :], start=True, stop=True)
                        ins.then_inc(filled[b], 1)
                if t is not None:
                    chunk_scores(t, 0)
                    chunk_scores(t, 1)
                if s is not None:
                    pe.wait_ge(mix_ready, s + 1)
                    use(7, s, 0)
                    for k in range(4):
                        turn(heads_of(7)[:, k, :], mix_flat[:, k * P:(k + 1) * P], filled[7] if k == 3 else None)
                    use(3, s, 1)
                    for k in (4, 5):
                        turn(heads_of(3)[:, k - 4, :], mix_flat[:, k * P:(k + 1) * P], filled[3] if k == 5 else None)
                    pieces = out_projection(s)
                for lvl in range(2, LEVELS + 1):
                    if t is not None:
                        chunk_scores(t, lvl)
                        if lvl == 5:
                            pe.wait_ge(probs_ready, t + 1)
                            for b in (4, 5):
                                use(b, t, 1)
                                for n in range(4):
                                    place, m = 2 * (b - 4) + n // 2, n % 2
                                    turn(heads_of(b)[:, n, :], probs[:, place, m * P:(m + 1) * P], filled[b] if n == 3 else None)
                    if s is not None:
                        for _ in range(4 if lvl < 4 else 2):
                            next(pieces, None)
                if t is not None:
                    pe.wait_ge(drained[4], t * 3 + 2)
                    pe.wait_ge(drained[5], t * 3 + 2)
                    use(6, t, 1)
                    for place in range(MHEADS):
                        h = 2 * (place % 2) + place // 2
                        o = psum[6][(h % 2) * MHD:(h % 2 + 1) * MHD, (h // 2) * P:(h // 2 + 1) * P]
                        for m in range(MTILES):
                            ins = pe.matmul(o, mem_v[:, m, h * MHD:(h + 1) * MHD], probsT[:, place, m, :], start=(m == 0), stop=(m == MTILES - 1))
                    ins.then_inc(filled[6], 1)
                    for b in (4, 5):
                        for e in range(2):
                            h = 2 * (b - 4) + e
                            ins = pe.matmul(cols(b, 2 * DV, 2)[:, e, :], k_decayedT[:, h, :], v_t[:, h, :], start=True, stop=True)
                        ins.then_inc(filled[b], 1)
                if s is not None:
                    pe.wait_ge(u_ready, s + 1)
                    use(7, s, 1)
                    for k in range(4):
                        turn(heads_of(7)[:, k, :], u_tile[:, k * P:(k + 1) * P], filled[7] if k == 3 else None)
                    use(2, s, 2)
                    for k in range(4, 8):
                        turn(heads_of(2)[:, k - 4, :], u_tile[:, k * P:(k + 1) * P], filled[2] if k == 7 else None)
                if t is not None:
                    for b in (0, 1):
                        pe.wait_ge(drained[b], t * 4 + 4)
                    pe.wait_ge(fac_used[1], t * 3 + 1)
                    hold(pe, drained[5], t * 3)
                    for b in (3, 2):
                        use(b, t, 0)
                        for e in range(2):
                            h = 2 * (b - 2) + e
                            o = cols(b, 2 * DV, 2)[:, e, :]
                            pe.matmul(o, scoresT[:, h, :], v_t[:, h, :], start=True, stop=False)
                            ins = pe.matmul(o, q_decayed[:, h, :], state[:, h, :], start=False, stop=True)
                        ins.then_inc(filled[b], 1)
                if s is not None:
                    pe.wait_ge(drained[7], s * 3 + 2)
                    pe.wait_ge(drained[2], s * 3 + 3)
                    for k in range(KD):
                        ins = pe.matmul(psum[7][:, 0:G + E], uT[:, k, :], w_route[:, k, :], start=(k == 0), stop=(k == KD - 1))
                    ins.then_inc(filled[7], 1)

            def chunk_scores(t, lvl):
                b = lvl % 2
                if lvl < LEVELS:
                    f = lvl + 2
                    pe.wait_ge(fac_used[f % 3], t * 3 + (f // 3 + 1))
                else:
                    pe.wait_ge(kd_ready, t + 1)
                use(b, t, lvl // 2)
                for h in range(HEADS):
                    moving = qk[:, b, h, :] if lvl < LEVELS else qT[:, h, at_tile(t)]
                    ins = pe.matmul(heads_of(b)[:, h, :], qk[:, b, h, :], moving, start=True, stop=True)
                ins.then_inc(filled[b], 1)

            mix_pe(0, None)
            with pe.Fori(1, TILES) as t:
                mix_pe(t, t - 1)
            mix_pe(None, TILES - 1)

            pe.wait_ge(member_ready, 1)
            pe.wait_ge(drained[0], TILES * USES[0])
            pe.wait_ge(drained[1], TILES * USES[1])
            flat = member.rearrange("p t e -> p (t e)")
            pe.matmul(psum[0][:, 0:TE], tri, flat, start=True, stop=True)
            pe.matmul(psum[1][:, 0:TE], ones, flat, start=True, stop=True).then_inc(rank_filled, 1)
            for n in range(2 * TILES):
                pe.wait_ge(hot_ready, n + 1)
                ins = pe.matmul(psum[2][:, 0:COLS], row_hot[n % 2], block_hot[n % 2], start=(n == 0), stop=(n == 2 * TILES - 1))
                ins.then_inc(hot_used if n < 2 * TILES - 1 else table_filled, 1)
            pe.wait_ge(tables_ready, 1)

            def rows_transposed(i, u):
                pe.wait_ge(gathered[u], i * 16 + 16)
                hold(pe, rowsT_low, number(i, u))
                for b in range(2):
                    for k in range(4 * b, 4 * b + 4):
                        turn(heads_of(b)[:, k - 4 * b, :], rows[u][:, k * P:(k + 1) * P], rows_filled[b] if k == 4 * b + 3 else None)

            def weights_split(i, u, p):
                pe.wait_ge(part_low_dve[p], number(i, u) + 1)
                pe.wait_ge(part_low_pool[p], number(i, u) + 1)

            PASSES = ((0, 0), (0, 1), (1, 0))

            def up_product(i, u):
                pe.wait_ge(rowsT_low, number(i, u) + 1)
                hold(pe, hid_ready, number(i, u) - 1)
                for p in range(2):
                    weights_split(i, u, p)
                    for k in range(KD // 2):
                        for a, b in PASSES:
                            ins = pe.matmul(psum[2 + 4 * u][:, :], rowsT[u][:, a, p * KD // 2 + k, :],
                                            parts[:, u, p, b, k * 2 * FF:(k + 1) * 2 * FF],
                                            start=(p == 0 and k == 0 and a + b == 0), stop=(p == 1 and k == KD // 2 - 1 and a == 1))
                    ins.then_inc(part_used[p], 1)

            def hid_transposed(i, u):
                pe.wait_ge(hid_ready, number(i, u) + 1)
                hold(pe, hidT_low, number(i, u))
                for k in range(KF):
                    turn(psum[3][:, k * P:(k + 1) * P], hid[u][:, k * P:(k + 1) * P], hidT_filled if k == KF - 1 else None)

            def down_product(i, u):
                pe.wait_ge(hidT_low, number(i, u) + 1)
                hold(pe, y_left, number(i, u))
                hold(pe, y_right, number(i, u))
                weights_split(i, u, 2)
                for n in range(2):
                    for k in range(KF):
                        for a, b in PASSES:
                            ins = pe.matmul(psum[4 + n][:, :], hidT[:, u, a, k, :], parts[:, u, 2, b, k * D + n * 512:k * D + n * 512 + 512],
                                            start=(k == 0 and a + b == 0), stop=(k == KF - 1 and a == 1))
                ins.then_inc(part_used[2], 1)

            def step_pe(i, u):
                up_product(i, u)
                if not is_zero(number(i, u)):
                    hid_transposed(*behind(i, u))
                rows_transposed(*ahead(i, u))
                if not is_zero(number(i, u)):
                    down_product(*behind(i, u))

            rows_transposed(0, 0)
            more = all_pairs(pe, step_pe)
            last = more + (FIXED - 1)
            hid_transposed(last, 1)
            down_product(last, 1)


INS = ["x", "mem", "mix_norm", "ffn_norm", "mem_norm", "final_norm", "gla_w_in", "gla_w_gate_up",
       "gla_b_gate", "gla_out_norm", "w_mem_kv", "w_out", "w_group", "b_group", "w_router", "b_router",
       "w_up", "w_down"]


def kernel(**inputs):
    import numpy as np
    import concourse.bacc as bacc
    from concourse import mybir as mb
    from concourse.bass_utils import run_bass_kernel_spmd

    nc = bacc.Bacc("TRN2", target_bir_lowering=False, num_devices=1)
    arrays, args = {}, []
    for name in INS:
        a = np.ascontiguousarray(inputs[name])
        arrays[f"in_{name}"] = a
        args.append(nc.dram_tensor(f"in_{name}", a.shape, mb.dt.from_np(a.dtype), kind="ExternalInput").ap())
    shape = tuple(inputs["x"].shape)
    args.append(nc.dram_tensor("out_rows", shape, mb.dt.float32, kind="ExternalOutput").ap())
    hybrid_layer(nc, *args)
    r = run_bass_kernel_spmd(nc, [arrays], core_ids=[0])
    return r.results[0]["out_rows"]
```

```python
from contextlib import ExitStack

import concourse.bass as bass
from concourse import mybir

P = 128


class Chain:

    def __init__(self, eng, sem):
        self.eng, self.sem, self.base, self.n, self.turn, self.per = eng, sem, 0, 0, 0, 0

    def link(self, ins):
        ins.then_inc(self.sem, 1)
        self.n += 1
        self.eng.wait_ge(self.sem, self.turn * self.per + (self.base + self.n))

    def enter(self, turn, per):
        self.turn, self.per = turn, per

    def leave(self, turns):
        assert self.n - self.start == self.per, (self.n - self.start, self.per)
        self.base += self.per * (turns - 1)
        self.turn = 0

    def mark(self):
        self.start = self.n


def hybrid_layer(nc, x, mem, mix_norm, ffn_norm, mem_norm, final_norm, gla_w_in, gla_w_gate_up,
                 gla_b_gate, gla_out_norm, w_mem_kv, w_out, w_group, b_group, w_router, b_router,
                 w_up, w_down, out):
    f32, f16, f32r = mybir.dt.float32, mybir.dt.float16, mybir.dt.float32r
    i32, u8 = mybir.dt.int32, mybir.dt.uint8
    ALU, ACT, AX = mybir.AluOpType, mybir.ActivationFunctionType, mybir.AxisListType
    ds = bass.ds

    T, D = x.shape[1], x.shape[2]
    N_MEM = mem.shape[1]
    TILES, KD = T // P, D // P
    HEADS = 4
    KEY = gla_w_gate_up.shape[2]
    RANK = gla_w_gate_up.shape[1]
    DV = gla_out_norm.shape[1]
    MIX = HEADS * DV
    DK = KEY // HEADS
    MEMW = w_mem_kv.shape[2] // 2
    MHEADS = 4
    MHD = MEMW // MHEADS
    MTILES = N_MEM // P
    GROUPS = w_group.shape[2]
    EXPERTS = w_router.shape[2]
    PER = EXPERTS // GROUPS
    FF = w_down.shape[2]
    KF = FF // P
    EPS = 1e-6
    GATE_SCALE = 1.0 / 16.0
    Q_SCALE = DK ** -0.5
    M_SCALE = MHD ** -0.5
    LEVELS = 7
    CHOICES = 2
    PAIRS = ((T * CHOICES + EXPERTS * (P - 1)) // P + 1) // 2
    BLOCKS = 2 * PAIRS
    COLS = BLOCKS + 2
    assert DK == P and KD == 8 and T % 512 == 0 and D == 1024

    w_in = gla_w_in[0].rearrange("(k p) n -> p k n", p=P)
    w_kv = w_mem_kv[0].rearrange("(k p) n -> p k n", p=P)
    w_o = w_out[0].rearrange("(k p) n -> p k n", p=P)
    up_rows = w_up[0].rearrange("e (k p) n -> e p k n", p=P)
    down_rows = w_down[0].rearrange("e (k p) n -> e p k n", p=P)
    h_dram = nc.dram_tensor("h_rows", [T, D], f32, kind="Internal").ap()
    u_dram = nc.dram_tensor("u_rows", [T, D], f32, kind="Internal").ap()
    y_dram = nc.dram_tensor("y_rows", [BLOCKS * P, D], f32, kind="Internal").ap()

    with ExitStack() as ctx:
        def sb(name, shape, dt=f32):
            return ctx.enter_context(nc.sbuf_tensor(name, shape, dt))

        def sem(name):
            return ctx.enter_context(nc.semaphore(name))

        def sems(name, n):
            return [sem(f"{name}{i}") for i in range(n)]

        def later(name, base, at, shape):
            return nc.alloc_sbuf_tensor_at(name, shape, f32r, offset=base + 4 * at)

        region_a_base = (nc.sbuf_base + 31) // 32 * 32
        region_a = sb("region_a", [P, KD * T])
        ring_base = (nc.sbuf_base + 31) // 32 * 32
        ring = sb("weight_ring", [P, 2, KD, 512])
        acts_base = (nc.sbuf_base + 31) // 32 * 32
        acts = sb("activations", [P, 24576])
        mqT_base = (nc.sbuf_base + 31) // 32 * 32
        mqT = sb("mqT", [P, 2, T])
        work_base = (nc.sbuf_base + 31) // 32 * 32
        work = sb("work", [P, 6912])
        fac = work[:, 0:1536].rearrange("p (a n) -> p a n", a=3)
        qk = work[:, 1536:2560].rearrange("p (u h t) -> p u h t", u=2, h=HEADS)
        scoresT, q_decayed, k_decayed, k_decayedT = (work[:, 2560 + n * 512:3072 + n * 512].rearrange("p (h t) -> p h t", h=HEADS) for n in range(4))
        state, mix, gate = (work[:, 4608 + n * MIX:4608 + (n + 1) * MIX].rearrange("p (h d) -> p h d", h=HEADS) for n in range(3))
        mq_tile = sb("mq_tile", [P, 2, P])
        out_gain = sb("out_gain", [P, 1, DV])
        mem_kT = sb("mem_kT", [P, 2, N_MEM])
        mem_v = sb("mem_v", [P, MTILES, MEMW])
        masks = sb("masks", [P, LEVELS + 1, P], u8)
        ident = sb("ident", [P, P])
        w_route = sb("w_route", [P, KD, GROUPS + EXPERTS])
        b_route = sb("b_route", [P, GROUPS + EXPERTS])
        logits = sb("logits", [P, TILES, GROUPS + EXPERTS])
        b_gate = sb("b_gate", [P, HEADS])
        stat = sb("stat", [P, 48])
        minus_half = sb("minus_half", [P, 4])
        eps = sb("eps", [P, 4])
        spare = sb("spare", [P, 4])
        consts = sb("route_consts", [P, 576])
        sumsq, meansq, rstd = stat[:, 0:4], stat[:, 4:8], stat[:, 40:44]
        neg_max, row_sum, row_inv = stat[:, 8:12], stat[:, 12:16], stat[:, 16:20]
        o_sumsq, o_meansq, o_rstd = stat[:, 20:24], stat[:, 24:28], stat[:, 28:32]
        h_sumsq, h_meansq, h_rstd = stat[:, 32:33], stat[:, 33:34], stat[:, 34:35]
        decay_all = stat[:, 36:40]

        HK, UNIT = KD // 2, 256
        assert ring_base == region_a_base + 4 * KD * T
        xT = later("xT_parts", region_a_base, 0, [P, 2, KD, T])
        memT = later("memT_parts", acts_base, 20480, [P, 2, KD, N_MEM])
        pieces = later("weight_pieces", work_base, 0, [P, 2, 2, HK, UNIT])
        raw_pieces = work[:, 4096:4096 + 2 * HK * UNIT].rearrange("p (u k n) -> p u k n", u=2, k=HK)
        qT = acts[:, 0:4096].rearrange("p (h t) -> p h t", h=HEADS)
        kT = acts[:, 4096:8192].rearrange("p (h t) -> p h t", h=HEADS)
        vg = acts[:, 8192:20480].rearrange("p (t n) -> p t n", t=TILES)
        bT = acts[:, 20480:24576].rearrange("p (h t) -> p h t", h=HEADS)
        mix_gain, mem_gain = acts[:, 0:1024], acts[:, 1024:2048]
        x_in = acts[:, 2048:6144].rearrange("p (u n) -> p u n", u=4)
        x_norm = acts[:, 8192:10240].rearrange("p (u n) -> p u n", u=2)
        junk = acts[:, 10240:14336].rearrange("p (u n) -> p u n", u=4)
        rT = acts[0:RANK, 17408:18432]
        w_gate = acts[0:RANK, 18432:18944]
        log_term = [acts[:, 18944 + u * 512:19456 + u * 512] for u in range(2)]
        min_term = [acts[:, 12288 + u * 512:12800 + u * 512] for u in range(2)]
        h_tile, u_tile = region_a[:, 0:1024], region_a[:, 1024:2048]
        uT = region_a[:, 2048:3072].rearrange("p (k t) -> p k t", k=KD)
        catT = region_a[:, 3072:4096].rearrange("p (k t) -> p k t", k=KD)
        probs = region_a[:, 4096:5120].rearrange("p (h m) -> p h m", h=MHEADS)
        probsT = region_a[:, 5120:6144].rearrange("p (h m t) -> p h m t", h=MHEADS, m=MTILES)
        ffn_gain = region_a[:, 6144:7168]
        zeros = region_a[:, 7936:8192]
        o_sq = region_a[:, 7168:7168 + MIX].rearrange("p (h d) -> p h d", h=HEADS)

        psum = [ctx.enter_context(nc.psum_tensor(f"bank{b}", [P, 512], f32)) for b in range(8)]

        def heads_of(bank):
            return psum[bank][:, :].rearrange("p (h t) -> p h t", h=HEADS)

        def cols(bank, n, parts):
            return psum[bank][:, 0:n].rearrange("p (a b) -> p a b", a=parts)

        DEEP = 4

        small_loaded, mix_gain_loaded, mem_gain_loaded = sem("small_loaded"), sem("mix_gain_loaded"), sem("mem_gain_loaded")
        out_gain_loaded, ffn_gain_loaded = sem("out_gain_loaded"), sem("ffn_gain_loaded")
        pool_step, dve_step = sem("pool_step"), sem("dve_step")
        ident_built, half_built, state_zero = sem("ident_built"), sem("half_built"), sem("state_zero")
        masks_built = sem("masks_built")
        x_loaded, sumsq_ready, rstd_ready = sems("x_loaded", 4), sem("sumsq_ready"), sem("rstd_ready")
        norm_ready, x_transposed = sem("norm_ready"), sem("x_transposed")
        xT_low, xT_high = sem("xT_low"), sem("xT_high")
        piece_loaded, piece_high = sems("piece_loaded", 2), sems("piece_high", 2)
        piece_low, first_piece_used = sems("piece_low", 2), sem("first_piece_used")
        w_out_loaded = sem("w_out_loaded")
        job_filled, job_drained = sems("job_filled", 4), sems("job_drained", 4)
        gate_filled, gate_log, gate_min = sems("gate_filled", 2), sems("gate_log", 2), sems("gate_min", 2)
        gate_summed = sems("gate_summed", 2)
        filled, drained = sems("bank_filled", 8), sems("bank_drained", 8)
        arg_ready, exp_ready, fac_used = sem("arg_ready"), sem("exp_ready"), sems("fac_used", 3)
        kd_ready, mq_ready, decay_ready = sem("kd_ready"), sem("mq_ready"), sem("decay_ready")
        negmax_ready, probs_ready = sem("negmax_ready"), sem("probs_ready")
        tanh_ready, o_sq_ready, o_sumsq_ready = sem("tanh_ready"), sem("o_sq_ready"), sem("o_sumsq_ready")
        o_rstd_ready, mix_ready = sem("o_rstd_ready"), sem("mix_ready")
        x_tile_loaded, h_sumsq_ready, h_rstd_ready = sem("x_tile_loaded"), sem("h_sumsq_ready"), sem("h_rstd_ready")
        u_ready, h_stored, u_stored = sem("u_ready"), sem("h_stored"), sem("u_stored")
        zeros_built, y_cleared = sem("zeros_built"), sem("y_cleared")
        exp_arg, exp_done, ones_built = sem("exp_arg"), sem("exp_done"), sem("ones_built")
        member_ready, rank_filled, hot_ready = sem("member_ready"), sem("rank_filled"), sem("hot_ready")
        slots_ready, block_hot_ready, tokens_ready = sem("slots_ready"), sem("block_hot_ready"), sem("tokens_ready")
        hot_used, table_filled, tables_ready = sem("hot_used"), sem("table_filled"), sem("tables_ready")
        raw_loaded, part_high = sems("raw_loaded", 3), sems("part_high", 3)
        part_low_dve, part_low_pool, part_used = sems("part_low_dve", 3), sems("part_low_pool", 3), sems("part_used", 3)
        y_stored, gathered = sems("y_stored", 2), sems("gathered", 2)
        idx_ready, rows_filled = sem("idx_ready"), sems("rows_filled", 2)
        rowsT_high, rowsT_low = sems("rowsT_high", 2), sem("rowsT_low")
        silu_ready, hid_ready, hidT_filled = sem("silu_ready"), sem("hid_ready"), sem("hidT_filled")
        hidT_high, hidT_low, y_left, y_right = sem("hidT_high"), sem("hidT_low"), sem("y_left"), sem("y_right")
        final_gain_loaded = sem("final_gain_loaded")
        ya_loaded, yb_loaded, h_loaded = sems("ya_loaded", DEEP), sems("yb_loaded", DEEP), sems("h_loaded", DEEP)
        slot_copied = sem("slot_copied")
        sum_ready, f_sumsq, f_rstd = sem("sum_ready"), sem("f_sumsq"), sem("f_rstd")
        out_ready, out_stored = sem("out_ready"), sems("out_stored", DEEP)

        UNITS = [("mem_k", w_kv, 0, MEMW), ("mem_v", w_kv, MEMW, MEMW), ("rank", w_in, 2 * KEY + 2 * MIX, P),
                 ("mem_q", w_in, 2 * KEY + 2 * MIX + RANK, MEMW), ("k", w_in, KEY, UNIT), ("k", w_in, KEY + UNIT, UNIT),
                 ("q", w_in, 0, UNIT), ("q", w_in, UNIT, UNIT)]
        FIRST_VG, ALL_UNITS = len(UNITS), len(UNITS) + 2 * MIX // UNIT
        FIRST_K = 4
        assert MEMW == N_MEM == UNIT and T == 1024 and HEADS == 4

        def kind_of(n):
            return UNITS[n][0] if isinstance(n, int) and n < FIRST_VG else "vg"

        def banks_of(n):
            return {"mem_k": (0, 1), "mem_v": (2, 3), "rank": (0, 1)}.get(kind_of(n), (0, 1, 2, 3))

        def fills(n, b):
            if isinstance(n, int):
                return sum(b in banks_of(m) for m in range(n))
            return n - (FIRST_VG - sum(b in banks_of(m) for m in range(FIRST_VG)))

        def next_piece(n, kh):
            return (n, 1) if kh == 0 else (n + 1, 0)

        def gate_at(n, kh):
            m = (n - FIRST_K) * 2 + kh if isinstance(n, int) else -1
            return m if 0 <= m < len(GATE_JOBS) else None

        GATE_JOBS = [(h, s) for h in range(HEADS) for s in range(2)]

        def all_units(eng, unit):
            for n in range(FIRST_VG):
                unit(n)
            with eng.Fori(FIRST_VG, ALL_UNITS - 1) as n:
                unit(n)
            unit(ALL_UNITS - 1)

        def vg_columns(n):
            at = (n - FIRST_VG) * UNIT
            return slice(at, at + UNIT) if isinstance(n, int) else ds(at, UNIT)

        def unit_result(n, b):
            bank, kind = psum[4 + b], kind_of(n)
            g, half = b // 2, slice(b % 2 * 512, b % 2 * 512 + 512)
            if kind == "mem_k":
                return mem_kT[:, b, :], bank[:, 0:N_MEM], 1.0
            if kind == "mem_v":
                return mem_v[:, b - 2, :], bank[:, 0:MEMW], 1.0
            if kind == "rank":
                return rT[:, half], bank[0:RANK, :], 1.0
            if kind == "mem_q":
                return mqT[:, g, half], bank[:, :], 1.0
            if kind == "k":
                return kT[:, (n - FIRST_K) * 2 + g, half], bank[:, :], 1.0
            if kind == "q":
                return qT[:, (n - FIRST_K - 2) * 2 + g, half], bank[:, :], Q_SCALE
            return vg[:, 2 * b:2 * b + 2, vg_columns(n)], cols(4 + b, 512, 2), 1.0

        w_out_half = [ring[:, 0, :, :], ring[:, 1, :, :]]

        USES = [4, 4, 3, 3, 3, 3, 2, 3]

        rt = region_a

        def small(at, *dims):
            n = 1
            for d in dims:
                n *= d
            v = rt[:, at:at + n]
            if len(dims) == 2:
                return v.rearrange("p (a b) -> p a b", a=dims[0])
            if len(dims) == 3:
                return v.rearrange("p (a b c) -> p a b c", a=dims[0], b=dims[1])
            return v

        PIECE = KD // 2 * 2 * FF
        assert PIECE == KF * D and 3 * PIECE <= 6144
        POOL_SHARE = 768
        ring_flat = ring[:, :, :, :].rearrange("p u k n -> p (u k n)")
        raw = [ring_flat[:, p * PIECE:(p + 1) * PIECE] for p in range(3)]
        parts = later("weight_parts", acts_base, 0, [P, 2, 3, 2, PIECE])
        rowsT = [later("rowsT_parts0", ring_base, 3 * PIECE, [P, 2, KD, P]),
                 later("rowsT_parts1", region_a_base, 4224, [P, 2, KD, P])]
        hidT = later("hidT_parts", mqT_base, 0, [P, 2, 2, KF, P])
        rows = [fac[:, 0:2, :].rearrange("p a n -> p (a n)"), mqT[:, 1, :]]
        y_rows = [region_a[:, 6272:6272 + D], qk[:, :, :, :].rearrange("p a h t -> p (a h t)")]
        silu = [mix[:, :, :].rearrange("p h d -> p (h d)")[:, u * FF:(u + 1) * FF] for u in range(2)]
        hid = [gate[:, :, :].rearrange("p h d -> p (h d)")[:, u * FF:(u + 1) * FF] for u in range(2)]
        final_gain = region_a[:, 3200:4224]
        y_a, y_b, h_in, o_out = (acts[:, n * DEEP * D:(n + 1) * DEEP * D].rearrange("p (u n) -> p u n", u=DEEP) for n in range(4))
        f_stat = acts[:, 4 * DEEP * D:4 * DEEP * D + 3 * DEEP]
        f_sum, f_mean, f_inv = (f_stat[:, n * DEEP:(n + 1) * DEEP] for n in range(3))

        G, E, TG, TE = GROUPS, EXPERTS, TILES * GROUPS, TILES * EXPERTS
        g_max, e_top, e_second = small(0, TILES), small(8, TILES), small(16, TILES)
        g_prob, w_first, w_sec, seen = small(24, TILES), small(32, TILES), small(40, TILES), small(48, TILES)
        g_exp, g_hot = small(64, TILES, G), small(96, TILES, G)
        e_in, e_rest = small(128, TILES, PER), small(160, TILES, PER)
        a_hot, b_hot, equal = small(192, TILES, PER), small(224, TILES, PER), small(256, TILES, PER)
        picked = small(320, TILES, G, PER)
        a_all, b_all = small(448, TILES, G, PER), small(576, TILES, G, PER)
        member = small(704, TILES, E)
        carry = small(832, TILES + 1, E)
        rank, code, prod = small(1024, TILES, E), small(1152, TILES, E), small(1280, TILES, E)
        extra, extra_upto, code_low, code_high = small(1408, E), small(1424, E), small(1440, E), small(1456, E)
        slot_f, row_f, block_f = small(1488, 2, TILES), small(1504, 2, TILES), small(1520, 2, TILES)
        ones, tri, row_iota = consts[:, 0:P], consts[:, P:2 * P], consts[:, 2 * P:3 * P]
        iota_i = consts[:, 3 * P:4 * P].bitcast(i32)
        block_iota, token_id = consts[:, 512:512 + COLS], consts[:, 548:548 + TILES]
        expert_base, falling = consts[:, 556:556 + E], consts[:, 572:572 + PER]
        weight = small(1552, 2, TILES)
        upto_cmp = small(4224, COLS, E)
        expert_f = small(2304, COLS + 1)
        plan_f, plan_first = small(2400, COLS - 1), small(2440, COLS - 1)
        one_minus = small(2368, E)
        ints = rt[:, 2560:3200].bitcast(i32)
        slot_i, row_i, block_i = ints[:, 0:16], ints[:, 16:32], ints[:, 32:48]
        token_table = ints[:, 64:64 + COLS]
        plan = ints[:, 128:128 + COLS - 1]
        extra_pairs = ints[:, 200:200 + E]
        idx_tile = ints[:, 400:402]
        slot_tile = ints[:, 410:418]
        halves = rt[:, 3200:3200 + 1024].bitcast(f16)
        row_hot = [halves[:, u * P:(u + 1) * P] for u in range(2)]
        block_hot = [halves[:, 512 + u * 64:512 + u * 64 + COLS] for u in range(2)]

        def at_tile(t):
            return slice(t * P, t * P + P) if isinstance(t, int) else ds(t * P, P)

        def one_tile(t):
            return slice(t, t + 1) if isinstance(t, int) else ds(t, 1)

        def hold(eng, sem, value):
            if not (isinstance(value, int) and value <= 0):
                eng.wait_ge(sem, value)

        XT = TILES + MTILES
        assert TILES % 4 == 0 and MTILES == 2

        def norm_tiles(step):
            def all_tiles(eng):
                for u in range(4):
                    step(0, u)
                with eng.Fori(1, TILES // 4) as g:
                    for u in range(4):
                        step(g, u)
                for u in range(MTILES):
                    step(TILES // 4, u)
            return all_tiles

        def is_mem(g):
            return isinstance(g, int) and g == TILES // 4

        def tile_before(g, u):
            return (g, u - 1) if u > 0 else (g - 1, 3)

        def transposed_tile(g, u):
            if is_mem(g):
                return memT[:, :, :, u * P:(u + 1) * P]
            return xT[:, :, :, at_tile(g * 4 + u)]

        def final_tiles(eng, step):
            for u in range(DEEP):
                step(0, u)
            with eng.Fori(1, TILES // DEEP) as g:
                for u in range(DEEP):
                    step(g, u)

        def is_zero(v):
            return isinstance(v, int) and v == 0

        def ahead(i, u):
            return (i + u, 1 - u)

        def behind(i, u):
            return (i - (1 - u), 1 - u)

        def number(i, u):
            return i * 2 + u

        FIXED = EXPERTS // 2

        def plan_of(eng, i, u):
            j = number(i, u)
            v = eng.value_load(plan[0:1, slice(j, j + 1) if isinstance(j, int) else ds(j, 1)], min_val=0, max_val=4 * EXPERTS - 1)
            return v >> 2, v & 1, (v >> 1) & 1


        def slot_of(p, part, share, e):
            slot = slice(e % 2, e % 2 + 1) if isinstance(e, int) else ds(e & 1, 1)
            return parts[:, slot, p, part, share].rearrange("p a n -> p (a n)")

        def all_pairs(eng, step):
            for u in range(2):
                step(0, u)
            with eng.Fori(1, FIXED) as i:
                for u in range(2):
                    step(i, u)
            extra = eng.value_load(extra_pairs[0:1, E - 1:E], min_val=0, max_val=PAIRS - FIXED)
            with eng.Fori(0, PAIRS - FIXED) as g:
                with eng.If(extra > g):
                    for u in range(2):
                        step(g + FIXED, u)
            return extra

        block = ctx.enter_context(nc.Block())

        @block.sync
        def _(sp):
            def load_tile(g, u):
                n = g * 4 + u
                hold(sp, norm_ready, n - 3)
                src = mem[0, u * P:(u + 1) * P, :] if is_mem(g) else x[0, at_tile(n), :]
                sp.dma_start(x_in[:, u, :], src).then_inc(x_loaded[u], 16)
                if is_zero(g) and u == 0:
                    sp.dma_start(mix_gain, mix_norm[0:1, :].partition_broadcast(P).rearrange("p a n -> p (a n)")).then_inc(mix_gain_loaded, 16)
                if is_zero(g) and u == 3:
                    sp.dma_start(mem_gain, mem_norm[0:1, :].partition_broadcast(P).rearrange("p a n -> p (a n)")).then_inc(mem_gain_loaded, 16)

            def load_unit_piece(n, kh):
                rows_k = slice(kh * HK, (kh + 1) * HK)
                hold(sp, piece_low[kh], n)
                if kind_of(n) != "vg":
                    _, src, at, width = UNITS[n]
                    cols_n = slice(at, at + width)
                else:
                    src, width, at = w_in, UNIT, (n - FIRST_VG) * UNIT + 2 * KEY
                    cols_n = slice(at, at + UNIT) if isinstance(n, int) else ds(at, UNIT)
                sp.dma_start(raw_pieces[:, kh, :, 0:width], src[:, rows_k, cols_n]).then_inc(piece_loaded[kh], 16)

            norm_tiles(load_tile)(sp)

            def load_unit(n):
                for kh in range(2):
                    load_unit_piece(n, kh)

            all_units(sp, load_unit)

            for b in range(4):
                sp.wait_ge(job_filled[b], fills(ALL_UNITS, b))
            sp.dma_start(ffn_gain, ffn_norm[0:1, :].partition_broadcast(P).rearrange("p a n -> p (a n)")).then_inc(ffn_gain_loaded, 16)
            for n in range(2):
                sp.dma_start(ring[:, n, :, :], w_o[:, :, n * 512:(n + 1) * 512]).then_inc(w_out_loaded, 16)
            sp.wait_ge(zeros_built, 1)
            CLEAR = (BLOCKS - EXPERTS) * P // TILES
            assert CLEAR % P == 0

            def tile_traffic(t):
                rows_of_y = y_dram[ds(t * CLEAR + EXPERTS * P, CLEAR) if not isinstance(t, int) else slice(EXPERTS * P, EXPERTS * P + CLEAR), :]
                sp.dma_start(rows_of_y.rearrange("(p b) (a n) -> p (b a) n", p=P, n=256),
                             zeros.unsqueeze(1).to_broadcast([P, CLEAR // P * (D // 256), 256])).then_inc(y_cleared, 16)
                hold(sp, h_stored, t * 16)
                hold(sp, u_ready, t)
                sp.dma_start(h_tile, x[0, at_tile(t), :]).then_inc(x_tile_loaded, 16)
                sp.wait_ge(drained[3], t * 3 + 3)
                sp.dma_start(h_dram[at_tile(t), :], h_tile).then_inc(h_stored, 16)
                sp.wait_ge(u_ready, t + 1)
                sp.dma_start(u_dram[at_tile(t), :], u_tile).then_inc(u_stored, 16)

            tile_traffic(0)
            with sp.Fori(1, TILES) as t:
                tile_traffic(t)

            def load_piece(e, p):
                one = slice(e, e + 1) if isinstance(e, int) else ds(e, 1)
                hold(sp, part_low_dve[p], e)
                hold(sp, part_low_pool[p], e)
                src = up_rows[one, :, p * KD // 2:(p + 1) * KD // 2, :] if p < 2 else down_rows[one, :, :, :]
                width = src.shape[-1]
                sp.dma_start(raw[p].rearrange("p (k n) -> p k n", n=width), src.rearrange("e p k n -> p (e k) n")).then_inc(raw_loaded[p], 16)

            sp.wait_ge(y_cleared, 16 * TILES)
            sp.wait_ge(filled[3], TILES * USES[3])
            for e, p in ((0, 0), (0, 1), (0, 2), (1, 0), (1, 1)):
                load_piece(e, p)
            with sp.Fori(2, EXPERTS) as e:
                for p in range(2):
                    load_piece(e, p)
                load_piece(e - 1, 2)
            load_piece(EXPERTS - 1, 2)
            sp.wait_ge(tables_ready, 1)
            more = sp.value_load(extra_pairs[0:1, E - 1:E], min_val=0, max_val=PAIRS - FIXED)

            for u in range(2):
                sp.wait_ge(y_stored[u], more * 16 + 16 * FIXED)
            sp.wait_ge(tables_ready, 1)
            sp.dma_start(final_gain, final_norm.rearrange("(a n) -> a n", a=1).partition_broadcast(P).rearrange("p a n -> p (a n)")).then_inc(final_gain_loaded, 16)
            def load_h(g, u):
                hold(sp, out_ready, g * DEEP - DEEP + u + 1 if not is_zero(g) else 0)
                t = g * DEEP + u
                sp.dma_start(h_in[:, u, :], h_dram[at_tile(t), :]).then_inc(h_loaded[u], 16)

            def store_out(g, u):
                t = g * DEEP + u
                sp.wait_ge(out_ready, t + 1)
                sp.dma_start(out[0, at_tile(t), :], o_out[:, u, :]).then_inc(out_stored[u], 16)

            for u in range(DEEP):
                load_h(0, u)
            with sp.Fori(1, TILES // DEEP) as g:
                for u in range(DEEP):
                    store_out(g - 1, u)
                    load_h(g, u)
            for u in range(DEEP):
                store_out(TILES // DEEP - 1, u)
            for u in range(DEEP):
                sp.wait_ge(out_stored[u], 16 * (TILES // DEEP))

        @block.gpsimd
        def _(pool):
            c = Chain(pool, pool_step)
            pool.memset(eps[:, :], EPS)
            pool.memset(minus_half[:, :], -0.5).then_inc(half_built, 1)
            c.link(pool.memset(ident[:, :], 0.0))
            pool.affine_select(out=ident[:, :], in_=ident[:, :], compare_op=ALU.not_equal, fill=1.0, base=0,
                               pattern=[[-1, P]], channel_multiplier=1).then_inc(ident_built, 1)
            mask_rows = acts[:, 16384:16384 + 3 * P].bitcast(i32)
            pool.iota(mask_rows[:, 0:P], [[1, P]], base=0, channel_multiplier=0)
            pool.iota(mask_rows[:, P:2 * P], [[0, P]], base=0, channel_multiplier=1).then_inc(masks_built, 1)
            pool.wait_ge(half_built, 1)

            def wait_apart(*waits):
                for s, v in waits:
                    pool.wait_ge(s, v)
                pool.tensor_tensor(spare[:, 0:1], minus_half[:, 0:1], minus_half[:, 0:1], ALU.mult)

            def rms(dst, mean, src, width):
                c.link(pool.tensor_tensor(mean, src, eps[:, 0:width], ALU.add))
                return pool.tensor_tensor(dst, mean, minus_half[:, 0:width], ALU.pow)

            def tile_norm(g, u):
                pool.wait_ge(sumsq_ready, g * 4 + (u + 1))
                rms(rstd[:, u:u + 1], meansq[:, u:u + 1], sumsq[:, u:u + 1], 1).then_inc(rstd_ready, 1)

            for u in range(4):
                tile_norm(0, u)
            with pool.Fori(1, TILES // 4) as g:
                c.enter(g - 1, 4)
                c.mark()
                for u in range(4):
                    tile_norm(g, u)
            c.leave(TILES // 4 - 1)
            for u in range(MTILES):
                tile_norm(TILES // 4, u)
            pool.dma_start(b_gate[:, :], gla_b_gate[0].rearrange("(h p) -> p h", p=P), allow_slow_non_contiguous=True).then_inc(small_loaded, 16)
            pool.dma_start(w_gate, gla_w_gate_up[0]).then_inc(small_loaded, 16)
            pool.dma_start(out_gain[:, :, :], gla_out_norm[0:1, :].partition_broadcast(P)).then_inc(out_gain_loaded, 16)
            pool.dma_start(w_route[:, :, 0:G], w_group[0].rearrange("(k p) n -> p k n", p=P), allow_slow_non_contiguous=True).then_inc(small_loaded, 16)
            pool.dma_start(w_route[:, :, G:G + E], w_router[0].rearrange("(k p) n -> p k n", p=P), allow_slow_non_contiguous=True).then_inc(small_loaded, 16)
            pool.dma_start(b_route[:, 0:G], b_group[0:1, :].partition_broadcast(P).rearrange("p a n -> p (a n)")).then_inc(small_loaded, 16)
            pool.dma_start(b_route[:, G:G + E], b_router[0:1, :].partition_broadcast(P).rearrange("p a n -> p (a n)")).then_inc(small_loaded, 16)

            c.link(pool.memset(ones, 1.0))
            c.link(pool.affine_select(out=tri, in_=ones, compare_op=ALU.is_gt, fill=0.0, base=0,
                                      pattern=[[1, P]], channel_multiplier=-1))
            c.link(pool.iota(iota_i[:, 0:P], [[1, P]], base=0, channel_multiplier=0))
            c.link(pool.tensor_copy(row_iota, iota_i[:, 0:P]))
            c.link(pool.tensor_copy(block_iota, iota_i[:, 0:COLS]))
            c.link(pool.tensor_scalar(expert_base, iota_i[:, 0:E], float(P), None, ALU.mult))
            c.link(pool.tensor_scalar(falling, iota_i[:, 0:PER], -1.0, float(PER), ALU.mult, ALU.add))
            c.link(pool.iota(iota_i[:, 0:TILES], [[P, TILES]], base=0, channel_multiplier=1))
            pool.tensor_copy(token_id, iota_i[:, 0:TILES]).then_inc(ones_built, 1)

            for u in range(2):
                pool.wait_ge(gate_summed[u], len(GATE_JOBS) // 2)
            pool.wait_ge(out_gain_loaded, 16)
            c.link(pool.tensor_scalar(out_gain[:, :, :], out_gain[:, :, :], 0.5, None, ALU.mult))
            for b in range(4):
                pool.wait_ge(job_drained[b], fills(ALL_UNITS, b))

            pool.memset(zeros, 0.0).then_inc(zeros_built, 1)

            def exponent(t, f):
                bt = bT[:, :, at_tile(t)]
                hold(pool, fac_used[f % 3], t * 3 + f // 3)
                if f == 0:
                    f0 = fac[:, 0, :].rearrange("p (h t) -> p h t", h=HEADS)
                    pool.tensor_tensor(f0, bt[:, :, P - 1:P].to_broadcast([P, HEADS, P]), bt, ALU.subtract).then_inc(arg_ready, 1)
                    return
                s = (P // 2) >> (f - 2)
                fh = fac[:, f % 3, :].rearrange("p (h b a s) -> p h b a s", h=HEADS, a=2, s=s)
                bh = bt.rearrange("p h (b a s) -> p h b a s", a=2, s=s)
                mid = bh[:, :, :, 1, 0:1].to_broadcast([P, HEADS, P // (2 * s), s])
                pool.tensor_tensor(fh[:, :, :, 0, :], mid, bh[:, :, :, 0, :], ALU.subtract)
                pool.tensor_tensor(fh[:, :, :, 1, :], bh[:, :, :, 1, :], mid, ALU.subtract).then_inc(arg_ready, 1)

            def mix_pool(t, s, ahead=True):
                if s is not None:
                    pool.wait_ge(o_sumsq_ready, s + 1)
                    rms(o_rstd, o_meansq, o_sumsq, 4).then_inc(o_rstd_ready, 1)
                    pool.wait_ge(drained[2], s * 3 + 1)
                    pool.wait_ge(drained[3], s * 3 + 1)
                    pool.tensor_tensor(mix[:, :, :], mix[:, :, :], gate[:, :, :], ALU.mult).then_inc(mix_ready, 1)
                if t is not None:
                    for f in range(4, LEVELS + 2):
                        exponent(t, f)
                    g_t = vg[:, one_tile(t), MIX:2 * MIX].rearrange("p a (h d) -> p (a h) d", h=HEADS)
                    wait_apart((tanh_ready, t + 1))
                    c.link(pool.tensor_tensor(gate[:, :, :], gate[:, :, :], g_t, ALU.mult))
                    wait_apart()
                    c.link(pool.tensor_tensor(gate[:, :, :], gate[:, :, :], g_t, ALU.add))
                    c.link(pool.tensor_tensor(gate[:, :, :], gate[:, :, :], out_gain[:, :, :].to_broadcast([P, HEADS, DV]), ALU.mult))
                    if ahead:
                        exponent(t + 1, 0)
                        exponent(t + 1, 2)
                if s is not None:
                    pool.wait_ge(h_sumsq_ready, s + 1)
                    rms(h_rstd, h_meansq, h_sumsq, 1).then_inc(h_rstd_ready, 1)
                if t is not None and ahead:
                    exponent(t + 1, 3)

            for f in (0, 2, 3):
                exponent(0, f)
            mix_pool(0, None)
            mix_pool(1, 0)
            with pool.Fori(2, TILES - 1) as t:
                c.enter(t - 2, 5)
                c.mark()
                mix_pool(t, t - 1)
            c.leave(TILES - 3)
            mix_pool(TILES - 1, TILES - 2, ahead=False)
            mix_pool(None, TILES - 1)

            for n in range(2 * TILES):
                pool.wait_ge(slots_ready, 1)
                if n >= 2:
                    pool.wait_ge(hot_used, n - 1)
                choice, t = n // TILES, n % TILES
                pool.tensor_scalar(block_hot[n % 2], block_iota, block_f[:, choice, t:t + 1], token_id[:, t:t + 1],
                                   ALU.is_equal, ALU.mult).then_inc(block_hot_ready, 1)

            pool.wait_ge(tokens_ready, 1)

            def gather(i, u):
                j = number(i, u)
                pool.tensor_copy(idx_tile[:, u:u + 1], token_table[:, slice(j, j + 1) if isinstance(j, int) else ds(j, 1)]).then_inc(idx_ready, 1)
                wait_apart((idx_ready, j + 1))
                pool.indirect_dma_start(rows[u], None, u_dram, bass.IndirectOffsetOnAxis(idx_tile[:, u:u + 1], 0)).then_inc(gathered[u], 16)

            def split_low(e, p):
                share = slice(PIECE - POOL_SHARE, PIECE)
                pool.wait_ge(part_high[p], e + 1)
                pool.tensor_tensor(slot_of(p, 1, share, e), raw[p][:, share], slot_of(p, 0, share, e).bitcast(f32), ALU.subtract).then_inc(part_low_pool[p], 1)

            def step_pool(i, u):
                before, first, next_first = plan_of(pool, i, u)
                e = before + first
                pool.wait_ge(gathered[u], (i + 1) * 16)
                pool.wait_ge(rows_filled[1], number(i, u) + 1)
                gather(i + 1, u)
                with pool.If(next_first > 0):
                    for p in range(2):
                        split_low(e + 1, p)
                if is_zero(number(i, u)):
                    split_low(0, 2)
                else:
                    with pool.If(first > 0):
                        split_low(e, 2)

            for u in range(2):
                gather(0, u)
            pool.wait_ge(tables_ready, 1)
            for p in range(2):
                split_low(0, p)
            more = all_pairs(pool, step_pool)

            for u in range(2):
                pool.wait_ge(y_stored[u], more * 16 + 16 * FIXED)
            pool.tensor_tensor(spare[:, 2:3], minus_half[:, 0:1], minus_half[:, 0:1], ALU.mult)

            def gather_y(g, u):
                t = g * DEEP + u
                if not is_zero(g):
                    pool.wait_ge(sum_ready, t * 2 - (2 * DEEP - 2))
                for choice, dst, loaded in ((0, y_a, ya_loaded), (1, y_b, yb_loaded)):
                    col = t + choice * TILES
                    copy = slot_tile[:, 2 * u + choice:2 * u + choice + 1]
                    pool.tensor_copy(copy, slot_i[:, one_tile(col)]).then_inc(slot_copied, 1)
                    wait_apart((slot_copied, t * 2 + (choice + 1)))
                    pool.indirect_dma_start(dst[:, u, :], None, y_dram, bass.IndirectOffsetOnAxis(copy, 0)).then_inc(loaded[u], 16)

            def norm_of(g, u):
                pool.wait_ge(f_sumsq, g * DEEP + (u + 1))
                rms(f_inv[:, u:u + 1], f_mean[:, u:u + 1], f_sum[:, u:u + 1], 1).then_inc(f_rstd, 1)

            for u in range(DEEP):
                gather_y(0, u)
            with pool.Fori(1, TILES // DEEP) as g:
                c.enter(g - 1, DEEP)
                c.mark()
                for u in range(DEEP):
                    norm_of(g - 1, u)
                    gather_y(g, u)
            c.leave(TILES // DEEP - 1)
            for u in range(DEEP):
                norm_of(TILES // DEEP - 1, u)

        @block.scalar
        def _(act):
            def square_tile(g, u):
                act.wait_ge(x_loaded[u], g * 16 + 16)
                act.activation(junk[:, u, :], x_in[:, u, :], ACT.Square, scale=D ** -0.5, accum_out=sumsq[:, u:u + 1]).then_inc(sumsq_ready, 1)

            def evac_high(g, u):
                n = g * 4 + u
                for b in range(2):
                    act.wait_ge(x_transposed, n * 2 + (b + 1))
                    act.activation(transposed_tile(g, u)[:, 0, 4 * b:4 * b + 4, :], cols(2 * (u % 2) + b, 512, 4), ACT.Copy).then_inc(xT_high, 1)

            def tile_act(g, u):
                square_tile(g, u)
                if not (is_zero(g) and u == 0):
                    evac_high(*tile_before(g, u))

            norm_tiles(tile_act)(act)
            evac_high(TILES // 4, MTILES - 1)

            def width_of(n):
                return UNITS[n][3] if kind_of(n) != "vg" else UNIT

            def split_high(n, kh):
                act.wait_ge(piece_loaded[kh], n * 16 + 16)
                if kh == 0:
                    hold(act, first_piece_used, n)
                elif not is_zero(n):
                    b = banks_of(n - 1)[-1]
                    act.wait_ge(job_filled[b], fills(n, b))
                w = width_of(n)
                act.activation(pieces[:, kh, 0, :, 0:w], raw_pieces[:, kh, :, 0:w], ACT.Copy).then_inc(piece_high[kh], 1)

            def gate_log_term(m):
                u, (h, s) = m % 2, GATE_JOBS[m]
                if m == 0:
                    act.wait_ge(small_loaded, 16 * 6)
                act.wait_ge(gate_min[u], m // 2 + 1)
                if m >= 2:
                    act.wait_ge(gate_summed[u], m // 2)
                act.activation(log_term[u], psum[2 + u][:, :], ACT.Abs, bias=b_gate[:, h:h + 1]).then_inc(gate_log[u], 1)
                act.wait_ge(gate_log[u], m // 2 * 3 + 1)
                act.activation(log_term[u], log_term[u], ACT.Exp, scale=-1.0).then_inc(gate_log[u], 1)
                act.wait_ge(gate_log[u], m // 2 * 3 + 2)
                act.activation(log_term[u], log_term[u], ACT.Ln, bias=1.0).then_inc(gate_log[u], 1)

            def unit_act(n):
                for kh in range(2):
                    if not (isinstance(n, int) and n == ALL_UNITS - 1 and kh == 1):
                        split_high(*next_piece(n, kh))
                    if gate_at(n, kh) is not None:
                        gate_log_term(gate_at(n, kh))
                for b in banks_of(n):
                    if b % 2 == 0:
                        act.wait_ge(job_filled[b], fills(n, b) + 1)
                        dst, src, scale = unit_result(n, b)
                        act.activation(dst, src, ACT.Copy, scale=scale).then_inc(job_drained[b], 1)
                if isinstance(n, int) and n == FIRST_VG - 1:
                    for u in range(2):
                        act.wait_ge(gate_summed[u], len(GATE_JOBS) // 2)

            split_high(0, 0)
            all_units(act, unit_act)

            for u in range(2):
                act.wait_ge(gate_summed[u], len(GATE_JOBS) // 2)
            for b in (1, 3):
                act.wait_ge(job_drained[b], fills(ALL_UNITS, b))

            def factor(t, f):
                if f == 1:
                    hold(act, fac_used[1], t * 3)
                    act.activation(fac[:, 1, :].rearrange("p (h t) -> p h t", h=HEADS), bT[:, :, at_tile(t)], ACT.Exp,
                                   scale=GATE_SCALE).then_inc(exp_ready, 1)
                else:
                    act.wait_ge(arg_ready, t * 8 + max(f, 1))
                    act.activation(fac[:, f % 3, :], fac[:, f % 3, :], ACT.Exp, scale=GATE_SCALE).then_inc(exp_ready, 1)

            def mix_act(t, s, ahead=True):
                if s is not None:
                    hold(act, o_sumsq_ready, s)
                    for b in (3, 2):
                        act.wait_ge(filled[b], s * 3 + 1)
                        ins = act.activation(o_sq[:, 2 * (b - 2):2 * (b - 1), :], cols(b, 2 * DV, 2), ACT.Square, scale=DV ** -0.5)
                    ins.then_inc(o_sq_ready, 1)
                if t is not None:
                    factor(t, 1)
                    act.wait_ge(filled[6], t * 2 + 1)
                    hold(act, filled[5], t * 3)
                    act.activation(k_decayedT[:, :, :], heads_of(6), ACT.Copy).then_inc(drained[6], 1)
                    hold(act, drained[5], t * 3)
                    act.activation(decay_all.unsqueeze(2), bT[:, :, at_tile(t)][:, :, P - 1:P], ACT.Exp, scale=GATE_SCALE).then_inc(decay_ready, 1)
                    factor(t, 4)
                    act.wait_ge(negmax_ready, t + 1)
                    hold(act, probs_ready, t)
                    hold(act, filled[5], t * 3)
                    for n in range(MHEADS):
                        ins = act.activation(probs[:, n, :], cols(4 + n // 2, 512, 2)[:, n % 2, :], ACT.Exp,
                                             bias=neg_max[:, n:n + 1], scale=M_SCALE, accum_out=row_sum[:, n:n + 1])
                        if n % 2:
                            ins.then_inc(drained[4 + n // 2], 1)
                    factor(t, 5)
                if s is not None:
                    act.wait_ge(filled[7], s * 3 + 1)
                    hold(act, filled[3], s * 3)
                    act.activation(catT[:, 0:4, :], heads_of(7), ACT.Copy).then_inc(drained[7], 1)
                if t is not None:
                    for f in range(6, LEVELS + 2):
                        factor(t, f)
                    g_t = vg[:, one_tile(t), MIX:2 * MIX].rearrange("p a (h d) -> p (a h) d", h=HEADS)
                    hold(act, mix_ready, t)
                    act.activation(gate[:, :, :], g_t, ACT.Tanh, scale=0.5).then_inc(tanh_ready, 1)
                    act.wait_ge(filled[5], t * 3 + 2)
                    hold(act, filled[6], t * 2)
                    act.activation(probsT[:, 2:4, :, :].rearrange("p h m t -> p (h m) t"), heads_of(5), ACT.Copy).then_inc(drained[5], 1)
                    if ahead:
                        factor(t + 1, 0)
                        factor(t + 1, 2)
                if s is not None:
                    act.wait_ge(drained[2], s * 3 + 2)
                    act.wait_ge(drained[3], s * 3 + 3)
                    hold(act, u_stored, s * 16)
                    act.activation(u_tile, h_tile, ACT.Square, scale=D ** -0.5, accum_out=h_sumsq).then_inc(h_sumsq_ready, 1)
                    act.wait_ge(filled[7], s * 3 + 2)
                    act.activation(uT[:, 0:4, :], heads_of(7), ACT.Copy).then_inc(drained[7], 1)
                if t is not None and ahead:
                    factor(t + 1, 3)

            for f in (0, 2, 3):
                factor(0, f)
            mix_act(0, None)
            mix_act(1, 0)
            with act.Fori(2, TILES - 1) as t:
                mix_act(t, t - 1)
            mix_act(TILES - 1, TILES - 2, ahead=False)
            mix_act(None, TILES - 1)

            act.wait_ge(exp_arg, 1)
            act.activation(g_exp, g_exp, ACT.Exp).then_inc(exp_done, 1)
            act.wait_ge(exp_arg, 2)
            act.activation(w_sec, w_sec, ACT.Exp).then_inc(exp_done, 1)

            def split_high(e, p, used):
                act.wait_ge(raw_loaded[p], e * 16 + 16)
                hold(act, part_used[p], used)
                act.activation(slot_of(p, 0, slice(0, PIECE), e), raw[p], ACT.Copy).then_inc(part_high[p], 1)

            def rows_high(i, u):
                for b in range(2):
                    act.wait_ge(rows_filled[b], number(i, u) + 1)
                    act.activation(rowsT[u][:, 0, 4 * b:4 * b + 4, :], heads_of(b), ACT.Copy).then_inc(rowsT_high[b], 1)

            def store_y(i, u):
                j = number(i, u)
                act.wait_ge(y_left, j + 1)
                act.wait_ge(y_right, j + 1)
                act.dma_start(y_dram[ds(j * P, P) if not isinstance(j, int) else slice(j * P, (j + 1) * P), :], y_rows[u]).then_inc(y_stored[u], 16)

            def hidT_split_high(i, u):
                act.wait_ge(hidT_filled, number(i, u) + 1)
                act.activation(hidT[:, u, 0, :, :], cols(3, KF * P, KF), ACT.Copy).then_inc(hidT_high, 1)

            def y_left_half(i, u):
                act.wait_ge(part_used[2], number(i, u) + 1)
                hold(act, y_stored[u], i * 16)
                act.activation(y_rows[u][:, 0:512], psum[4][:, :], ACT.Copy).then_inc(y_left, 1)

            def step_act(i, u):
                before, first, next_first = plan_of(act, i, u)
                e = before + first
                j = number(i, u)
                if not is_zero(i):
                    y_left_half(i - 1, u)
                with act.If(next_first > 0):
                    split_high(e + 1, 0, j)
                if not is_zero(j):
                    hidT_split_high(*behind(i, u))
                with act.If(next_first > 0):
                    split_high(e + 1, 1, j)
                rows_high(*ahead(i, u))
                act.wait_ge(part_used[1], j + 1)
                act.activation(silu[u], psum[2 + 4 * u][:, 0:FF], ACT.Silu).then_inc(silu_ready, 1)
                if is_zero(number(i, u)):
                    split_high(0, 2, 0)
                else:
                    with act.If(first > 0):
                        split_high(e, 2, j - 1)
                if not is_zero(i):
                    store_y(i - 1, u)

            for p in range(2):
                split_high(0, p, 0)
            rows_high(0, 0)
            act.wait_ge(tables_ready, 1)
            more = all_pairs(act, step_act)
            last = more + (FIXED - 1)
            y_left_half(last, 0)
            hidT_split_high(last, 1)
            store_y(last, 0)
            y_left_half(last, 1)
            store_y(last, 1)

            def square_sum(g, u):
                act.wait_ge(sum_ready, g * (2 * DEEP) + (2 * u + 2))
                if not is_zero(g):
                    act.wait_ge(out_stored[u], g * 16)
                act.activation(o_out[:, u, :], h_in[:, u, :], ACT.Square, scale=D ** -0.5, accum_out=f_sum[:, u:u + 1]).then_inc(f_sumsq, 1)

            final_tiles(act, square_sum)

        @block.vector
        def _(dve):
            c = Chain(dve, dve_step)

            def wait_apart(*waits):
                for s, v in waits:
                    hold(dve, s, v)
                dve.memset(spare[:, 1:2], 0.0)

            dve.wait_ge(mix_gain_loaded, 16)

            def norm_tile(g, u):
                n = g * 4 + u
                dve.wait_ge(rstd_ready, n + 1)
                dve.wait_ge(x_loaded[u], g * 16 + 16)
                hold(dve, x_transposed, n * 2 - 2)
                gain = mem_gain if is_mem(g) else mix_gain
                if is_mem(g):
                    dve.wait_ge(mem_gain_loaded, 16)
                dve.scalar_tensor_tensor(x_norm[:, u % 2, :], x_in[:, u, :], rstd[:, u:u + 1], gain, ALU.mult, ALU.mult).then_inc(norm_ready, 1)

            def evac_low(g, u):
                n = g * 4 + u
                dst = transposed_tile(g, u)
                for b in range(2):
                    dve.wait_ge(xT_high, n * 2 + (b + 1))
                    part = slice(4 * b, 4 * b + 4)
                    ins = dve.tensor_tensor(dst[:, 1, part, :], cols(2 * (u % 2) + b, 512, 4), dst[:, 0, part, :].bitcast(f32), ALU.subtract)
                ins.then_inc(xT_low, 1)

            def tile_dve(g, u):
                norm_tile(g, u)
                if not (is_zero(g) and u == 0):
                    evac_low(*tile_before(g, u))

            norm_tiles(tile_dve)(dve)
            evac_low(TILES // 4, MTILES - 1)

            def piece_split_low(n, kh):
                dve.wait_ge(piece_high[kh], n + 1)
                w = UNITS[n][3] if kind_of(n) != "vg" else UNIT
                dve.tensor_tensor(pieces[:, kh, 1, :, 0:w], raw_pieces[:, kh, :, 0:w], pieces[:, kh, 0, :, 0:w].bitcast(f32), ALU.subtract).then_inc(piece_low[kh], 1)

            def gate_sum(m):
                u, (h, s) = m % 2, GATE_JOBS[m]
                if m == 0:
                    dve.wait_ge(small_loaded, 16 * 6)
                dve.wait_ge(gate_filled[u], m // 2 + 1)
                if m >= 2:
                    dve.wait_ge(gate_summed[u], m // 2)
                dve.tensor_scalar(min_term[u], psum[2 + u][:, :], b_gate[:, h:h + 1], 0.0, ALU.add, ALU.min).then_inc(gate_min[u], 1)
                dve.wait_ge(gate_min[u], m // 2 + 1)
                dve.wait_ge(gate_log[u], m // 2 * 3 + 3)
                for q in range(4):
                    part = slice(q * P, (q + 1) * P)
                    ins = dve.tensor_tensor_scan(bT[:, h, s * 512 + q * P:s * 512 + (q + 1) * P], min_term[u][:, part],
                                                 log_term[u][:, part], 0.0, ALU.add, ALU.subtract)
                ins.then_inc(gate_summed[u], 1)

            def build_masks():
                iota_work = acts[:, 16384:16384 + 3 * P].bitcast(i32)
                mask_work = acts[:, 16384 + 3 * P:16384 + 5 * P]
                dve.wait_ge(masks_built, 1)
                c.link(dve.tensor_tensor(mask_work[:, 0:P], iota_work[:, 0:P], iota_work[:, P:2 * P], ALU.is_gt))
                c.link(dve.tensor_tensor(iota_work[:, 2 * P:3 * P], iota_work[:, 0:P], iota_work[:, P:2 * P], ALU.bitwise_xor))
                for lvl in range(LEVELS):
                    c.link(dve.scalar_tensor_tensor(masks[:, lvl, :], iota_work[:, 2 * P:3 * P], float(P >> lvl), mask_work[:, 0:P], ALU.is_lt, ALU.mult))
                c.link(dve.tensor_scalar(masks[:, LEVELS, :], iota_work[:, 2 * P:3 * P], 0.0, None, ALU.is_equal))

            def unit_dve(n):
                for kh in range(2):
                    if not (isinstance(n, int) and n == ALL_UNITS - 1 and kh == 1):
                        piece_split_low(*next_piece(n, kh))
                    if gate_at(n, kh) is not None:
                        gate_sum(gate_at(n, kh))
                if isinstance(n, int) and kind_of(n) == "mem_q":
                    build_masks()
                for b in banks_of(n):
                    if b % 2 == 1:
                        dve.wait_ge(job_filled[b], fills(n, b) + 1)
                        dst, src, scale = unit_result(n, b)
                        dve.tensor_scalar(dst, src, scale, None, ALU.mult).then_inc(job_drained[b], 1)

            piece_split_low(0, 0)
            all_units(dve, unit_dve)
            dve.memset(scoresT[:, :, :], 0.0)
            dve.memset(state[:, :, :], 0.0).then_inc(state_zero, 1)

            dve.wait_ge(state_zero, 1)
            for b in (0, 2):
                dve.wait_ge(job_drained[b], fills(ALL_UNITS, b))

            def heads_done(t):
                return 0 if isinstance(t, int) and t == 0 else (t - 1) * 3 + 1

            def level(t, lvl):
                f, s = lvl + 2, (P // 2) >> lvl
                dve.wait_ge(exp_ready, t * 9 + (f + 1 if f > 3 else f))
                hold(dve, filled[lvl % 2], t * 4 + lvl // 2)
                fh = fac[:, f % 3, :].rearrange("p (h b a s) -> p h b a s", h=HEADS, a=2, s=s)
                oh = qk[:, lvl % 2, :, :].rearrange("p h (b a s) -> p h b a s", a=2, s=s)
                kh = kT[:, :, at_tile(t)].rearrange("p h (b a s) -> p h b a s", a=2, s=s)
                qh = qT[:, :, at_tile(t)].rearrange("p h (b a s) -> p h b a s", a=2, s=s)
                dve.tensor_tensor(oh[:, :, :, 0, :], kh[:, :, :, 0, :], fh[:, :, :, 0, :], ALU.mult)
                dve.tensor_tensor(oh[:, :, :, 1, :], qh[:, :, :, 1, :], fh[:, :, :, 1, :], ALU.mult).then_inc(fac_used[f % 3], 1)

            def keep(t, lvl):
                before = (filled[2], heads_done(t)) if lvl == 0 else (drained[(lvl - 1) % 2], t * 4 + ((lvl - 1) // 2 + 1))
                wait_apart((filled[lvl % 2], t * 4 + (lvl // 2 + 1)), before)
                mask = masks[:, lvl:lvl + 1, :].to_broadcast([P, HEADS, P])
                dve.copy_predicated(scoresT[:, :, :], mask, heads_of(lvl % 2)).then_inc(drained[lvl % 2], 1)

            fac_heads = [fac[:, f, :].rearrange("p (h t) -> p h t", h=HEADS) for f in range(2)]

            def start_tile(t):
                dve.wait_ge(exp_ready, t * 9 + 1)
                hold(dve, filled[6], t * 2)
                dve.tensor_tensor(k_decayed[:, :, :], kT[:, :, at_tile(t)], fac_heads[0], ALU.mult).then_inc(fac_used[0], 1)
                hold(dve, filled[5], t * 3 - 1)
                dve.tensor_scalar(mq_tile[:, :, :], mqT[:, :, at_tile(t)], 1.0, None, ALU.mult).then_inc(mq_ready, 1)
                level(t, 0)

            def mix_dve(t, s, ahead=True):
                if t is not None:
                    kt, qt = kT[:, :, at_tile(t)], qT[:, :, at_tile(t)]
                if s is not None:
                    for b in (4, 5):
                        dve.wait_ge(filled[b], s * 3 + 3)
                    for b in (2, 3):
                        dve.wait_ge(filled[b], s * 3 + 1)
                    dve.wait_ge(decay_ready, s + 1)
                    for h in range(HEADS):
                        ins = dve.scalar_tensor_tensor(state[:, h, :], state[:, h, :], decay_all[:, h:h + 1],
                                                       cols(4 + h // 2, 2 * DV, 2)[:, h % 2, :], ALU.mult, ALU.add)
                        if h % 2:
                            ins.then_inc(drained[4 + h // 2], 1)
                    dve.wait_ge(o_sq_ready, s + 1)
                    hold(dve, o_rstd_ready, s)
                    dve.tensor_reduce(o_sumsq, o_sq[:, :, :], AX.X, ALU.add).then_inc(o_sumsq_ready, 1)
                if t is not None:
                    level(t, 1)
                    dve.wait_ge(exp_ready, t * 9 + 4)
                    hold(dve, filled[2], heads_done(t))
                    dve.tensor_tensor(q_decayed[:, :, :], qt, fac_heads[1], ALU.mult).then_inc(fac_used[1], 1)
                if s is not None:
                    dve.wait_ge(o_rstd_ready, s + 1)
                    hold(dve, filled[3], s * 3)
                    for b in (3, 2):
                        dve.tensor_tensor(mix[:, 2 * (b - 2):2 * (b - 1), :], cols(b, 2 * DV, 2),
                                          o_rstd[:, 2 * (b - 2):2 * (b - 1)].unsqueeze(2).to_broadcast([P, 2, DV]), ALU.mult).then_inc(drained[b], 1)
                if t is not None:
                    hold(dve, drained[5], t * 3)
                    for b in (4, 5):
                        dve.wait_ge(filled[b], t * 3 + 1)
                        c.link(dve.tensor_reduce(neg_max[:, 2 * (b - 4):2 * (b - 3)], cols(b, 512, 2), AX.X, ALU.max, negate=True))
                    dve.tensor_scalar(neg_max, neg_max, M_SCALE, None, ALU.mult).then_inc(negmax_ready, 1)
                    keep(t, 0)
                    level(t, 2)
                if s is not None:
                    dve.wait_ge(filled[3], s * 3 + 2)
                    dve.tensor_copy(catT[:, 4:6, :], cols(3, 2 * P, 2)).then_inc(drained[3], 1)
                if t is not None:
                    keep(t, 1)
                    level(t, 3)
                    keep(t, 2)
                    level(t, 4)
                    dve.wait_ge(drained[4], t * 3 + 1)
                    dve.wait_ge(drained[5], t * 3 + 1)
                    c.link(dve.reciprocal(row_inv, row_sum))
                    dve.tensor_tensor(probs[:, :, :], probs[:, :, :], row_inv.unsqueeze(2).to_broadcast([P, MHEADS, N_MEM]), ALU.mult).then_inc(probs_ready, 1)
                    keep(t, 3)
                    level(t, 5)
                    keep(t, 4)
                    level(t, 6)
                    keep(t, 5)
                    dve.wait_ge(filled[1], t * 4 + 3)
                    dve.tensor_scalar(qk[:, 1, :, :], kt, 1.0, None, ALU.mult).then_inc(kd_ready, 1)
                    dve.wait_ge(filled[4], t * 3 + 2)
                    hold(dve, filled[6], t * 2)
                    dve.tensor_copy(probsT[:, 0:2, :, :].rearrange("p h m t -> p (h m) t"), heads_of(4)).then_inc(drained[4], 1)
                    keep(t, 6)
                    keep(t, 7)
                if s is not None:
                    dve.wait_ge(x_tile_loaded, s * 16 + 16)
                    for b in (2, 3):
                        dve.wait_ge(filled[b], s * 3 + b)
                        half = slice((b - 2) * 512, (b - 1) * 512)
                        dve.tensor_tensor(h_tile[:, half], h_tile[:, half], psum[b][:, :], ALU.add).then_inc(drained[b], 1)
                if t is not None:
                    dve.wait_ge(filled[6], t * 2 + 2)
                    hold(dve, filled[3], t * 3)
                    dve.tensor_copy(catT[:, 6:8, :], cols(6, 2 * P, 2)).then_inc(drained[6], 1)
                if s is not None:
                    dve.wait_ge(drained[2], s * 3 + 2)
                    dve.wait_ge(drained[3], s * 3 + 3)
                    dve.wait_ge(h_rstd_ready, s + 1)
                    hold(dve, u_stored, s * 16)
                    dve.scalar_tensor_tensor(u_tile, h_tile, h_rstd, ffn_gain, ALU.mult, ALU.mult).then_inc(u_ready, 1)
                    dve.wait_ge(filled[2], s * 3 + 3)
                    dve.tensor_copy(uT[:, 4:8, :], heads_of(2)).then_inc(drained[2], 1)
                if t is not None and ahead:
                    start_tile(t + 1)
                if s is not None:
                    dve.wait_ge(filled[7], s * 3 + 3)
                    dve.tensor_tensor(logits[:, one_tile(s), :].rearrange("p a n -> p (a n)"), psum[7][:, 0:G + E], b_route[:, :], ALU.add).then_inc(drained[7], 1)

            start_tile(0)
            mix_dve(0, None)
            dve.wait_ge(ffn_gain_loaded, 16)
            mix_dve(1, 0)
            with dve.Fori(2, TILES - 1) as t:
                c.enter(t - 2, 3)
                c.mark()
                mix_dve(t, t - 1)
            c.leave(TILES - 3)
            mix_dve(TILES - 1, TILES - 2, ahead=False)
            mix_dve(None, TILES - 1)

            dve.wait_ge(ones_built, 1)
            dve.wait_ge(u_stored, 16 * TILES)
            dve.wait_ge(h_stored, 16 * TILES)
            dve.wait_ge(drained[7], TILES * USES[7])
            wide = [P, TILES, G]
            gl, el = logits[:, :, 0:G], logits[:, :, G:G + E].rearrange("p t (g e) -> p t g e", g=G)

            def first_of(hot, values, best):
                c.link(dve.tensor_tensor(equal, values, best.unsqueeze(2).to_broadcast(wide), ALU.is_equal))
                c.link(dve.tensor_tensor(equal, equal, falling.unsqueeze(1).to_broadcast(wide), ALU.mult))
                c.link(dve.tensor_reduce(seen, equal, AX.X, ALU.max))
                c.link(dve.tensor_tensor(hot, equal, seen.unsqueeze(2).to_broadcast(wide), ALU.is_equal))

            c.link(dve.tensor_reduce(g_max, gl, AX.X, ALU.max))
            dve.tensor_tensor(g_exp, gl, g_max.unsqueeze(2).to_broadcast(wide), ALU.subtract).then_inc(exp_arg, 1)
            first_of(g_hot, gl, g_max)
            c.link(dve.tensor_tensor(picked, el, g_hot.unsqueeze(3).to_broadcast([P, TILES, G, PER]), ALU.mult))
            c.link(dve.tensor_reduce(e_in, picked.rearrange("p t g e -> p t e g"), AX.X, ALU.add))
            c.link(dve.tensor_reduce(e_top, e_in, AX.X, ALU.max))
            first_of(a_hot, e_in, e_top)
            c.link(dve.scalar_tensor_tensor(e_rest, a_hot, -3.0e38, e_in, ALU.mult, ALU.add))
            c.link(dve.tensor_reduce(e_second, e_rest, AX.X, ALU.max))
            first_of(b_hot, e_rest, e_second)
            dve.tensor_tensor(w_sec, e_second, e_top, ALU.subtract).then_inc(exp_arg, 1)
            dve.wait_ge(exp_done, 2)
            c.link(dve.tensor_reduce(g_prob, g_exp, AX.X, ALU.add))
            c.link(dve.tensor_scalar(w_first, w_sec, 1.0, None, ALU.add))
            c.link(dve.tensor_tensor(w_first, w_first, g_prob, ALU.mult))
            c.link(dve.reciprocal(weight[:, 0, :], w_first))
            c.link(dve.tensor_tensor(weight[:, 1, :], weight[:, 0, :], w_sec, ALU.mult))
            for full, hot in ((a_all, a_hot), (b_all, b_hot)):
                c.link(dve.tensor_tensor(full, g_hot.unsqueeze(3).to_broadcast([P, TILES, G, PER]),
                                         hot.unsqueeze(2).to_broadcast([P, TILES, G, PER]), ALU.mult))
            a_te, b_te = (v.rearrange("p t g e -> p t (g e)") for v in (a_all, b_all))
            dve.tensor_tensor(member, a_te, b_te, ALU.add).then_inc(member_ready, 1)
            c.link(dve.memset(carry[:, 0, :], 0.0))
            dve.wait_ge(rank_filled, 1)
            ranks, totals = cols(0, TE, TILES), cols(1, TE, TILES)
            for t in range(TILES):
                c.link(dve.tensor_tensor(carry[:, t + 1, :], carry[:, t, :], totals[:, t, :], ALU.add))
            c.link(dve.tensor_tensor(rank, ranks, carry[:, 0:TILES, :], ALU.add))
            count = carry[:, TILES, :]
            c.link(dve.tensor_scalar(extra, count, float(P), None, ALU.is_gt))
            for m in range(2, T // P):
                c.link(dve.scalar_tensor_tensor(extra, count, float(P * m), extra, ALU.is_gt, ALU.add))
            c.link(dve.memset(one_minus, 1.0))
            c.link(dve.tensor_tensor_scan(extra_upto, one_minus, extra, 0.0, ALU.mult, ALU.add))
            c.link(dve.tensor_tensor(code_high, extra_upto, extra, ALU.subtract))
            c.link(dve.scalar_tensor_tensor(code_high, code_high, float(P), expert_base, ALU.mult, ALU.add))
            all_te = [P, TILES, E]
            c.link(dve.tensor_tensor(code, rank, code_high.unsqueeze(1).to_broadcast(all_te), ALU.add))
            for n, full in enumerate((a_te, b_te)):
                c.link(dve.tensor_tensor(prod, code, full, ALU.mult))
                c.link(dve.tensor_reduce(slot_f[:, n, :], prod, AX.X, ALU.add))
            flat = slot_f.rearrange("p a b -> p (a b)")
            c.link(dve.tensor_copy(slot_i, flat))
            c.link(dve.tensor_scalar(row_i, slot_i, P - 1, None, ALU.bitwise_and))
            c.link(dve.tensor_scalar(block_i, slot_i, 7, None, ALU.logical_shift_right))
            c.link(dve.tensor_copy(row_f.rearrange("p a b -> p (a b)"), row_i))
            dve.tensor_copy(block_f.rearrange("p a b -> p (a b)"), block_i).then_inc(slots_ready, 1)
            for n in range(2 * TILES):
                u = n % 2
                if n >= 2:
                    dve.wait_ge(hot_used, n - 1)
                choice, t = n // TILES, n % TILES
                dve.tensor_scalar(row_hot[u], row_iota, row_f[:, choice, t:t + 1], None, ALU.is_equal).then_inc(hot_ready, 1)
            dve.wait_ge(table_filled, 1)
            dve.tensor_copy(token_table, psum[2][:, 0:COLS]).then_inc(tokens_ready, 1)
            c.link(dve.scalar_tensor_tensor(code_low, expert_base, 1.0 / P, extra_upto, ALU.mult, ALU.add))
            c.link(dve.tensor_scalar(code_low, code_low, 1.0, None, ALU.add))
            c.link(dve.tensor_tensor(upto_cmp, block_iota.unsqueeze(2).to_broadcast([P, COLS, E]),
                                     code_low.unsqueeze(1).to_broadcast([P, COLS, E]), ALU.is_ge))
            c.link(dve.tensor_reduce(expert_f[:, 1:COLS + 1], upto_cmp, AX.X, ALU.add))
            c.link(dve.tensor_scalar(expert_f[:, 1:COLS + 1], expert_f[:, 1:COLS + 1], float(E - 1), None, ALU.min))
            c.link(dve.memset(expert_f[:, 0:1], 0.0))
            now, after, before = expert_f[:, 1:COLS], expert_f[:, 2:COLS + 1], expert_f[:, 0:COLS - 1]
            c.link(dve.tensor_tensor(plan_f, after, now, ALU.not_equal))
            c.link(dve.scalar_tensor_tensor(plan_f, before, 2.0, plan_f, ALU.mult, ALU.add))
            c.link(dve.tensor_tensor(plan_first, now, before, ALU.not_equal))
            c.link(dve.scalar_tensor_tensor(plan_f, plan_f, 2.0, plan_first, ALU.mult, ALU.add))
            c.link(dve.tensor_copy(plan, plan_f))
            c.link(dve.tensor_scalar(code_low, extra_upto, 1.0, None, ALU.add))
            c.link(dve.tensor_copy(extra_pairs, code_low))
            dve.tensor_scalar(extra_pairs, extra_pairs, 1, None, ALU.logical_shift_right).then_inc(tables_ready, 1)

            def split_low(e, p):
                share = slice(0, PIECE - POOL_SHARE)
                dve.wait_ge(part_high[p], e + 1)
                dve.tensor_tensor(slot_of(p, 1, share, e), raw[p][:, share], slot_of(p, 0, share, e).bitcast(f32), ALU.subtract).then_inc(part_low_dve[p], 1)

            def rows_low(i, u):
                for b in range(2):
                    dve.wait_ge(rowsT_high[b], number(i, u) + 1)
                    ins = dve.tensor_tensor(rowsT[u][:, 1, 4 * b:4 * b + 4, :], heads_of(b), rowsT[u][:, 0, 4 * b:4 * b + 4, :].bitcast(f32), ALU.subtract)
                ins.then_inc(rowsT_low, 1)

            def hidT_split_low(i, u):
                dve.wait_ge(hidT_high, number(i, u) + 1)
                dve.tensor_tensor(hidT[:, u, 1, :, :], cols(3, KF * P, KF), hidT[:, u, 0, :, :].bitcast(f32), ALU.subtract).then_inc(hidT_low, 1)

            def y_right_half(i, u):
                dve.wait_ge(part_used[2], number(i, u) + 1)
                hold(dve, y_stored[u], i * 16)
                dve.tensor_copy(y_rows[u][:, 512:1024], psum[5][:, :]).then_inc(y_right, 1)

            def step_dve(i, u):
                before, first, next_first = plan_of(dve, i, u)
                e = before + first
                if not is_zero(i):
                    y_right_half(i - 1, u)
                with dve.If(next_first > 0):
                    split_low(e + 1, 0)
                if not is_zero(number(i, u)):
                    hidT_split_low(*behind(i, u))
                with dve.If(next_first > 0):
                    split_low(e + 1, 1)
                rows_low(*ahead(i, u))
                dve.wait_ge(silu_ready, number(i, u) + 1)
                dve.tensor_tensor(hid[u], psum[2 + 4 * u][:, FF:2 * FF], silu[u], ALU.mult).then_inc(hid_ready, 1)
                if is_zero(number(i, u)):
                    split_low(0, 2)
                else:
                    with dve.If(first > 0):
                        split_low(e, 2)

            dve.wait_ge(tables_ready, 1)
            for p in range(2):
                split_low(0, p)
            rows_low(0, 0)
            more = all_pairs(dve, step_dve)
            last = more + (FIXED - 1)
            y_right_half(last, 0)
            hidT_split_low(last, 1)
            y_right_half(last, 1)

            dve.wait_ge(final_gain_loaded, 16)

            def sum_tile(g, u):
                t = g * DEEP + u
                for n, (y, loaded) in enumerate(((y_a, ya_loaded), (y_b, yb_loaded))):
                    dve.wait_ge(loaded[u], g * 16 + 16)
                    if n == 0:
                        dve.wait_ge(h_loaded[u], g * 16 + 16)
                    else:
                        dve.wait_ge(sum_ready, g * (2 * DEEP) + (2 * u + 1))
                    dve.scalar_tensor_tensor(h_in[:, u, :], y[:, u, :], weight[:, n, one_tile(t)], h_in[:, u, :], ALU.mult, ALU.add).then_inc(sum_ready, 1)

            def norm_out(g, u):
                dve.wait_ge(f_rstd, g * DEEP + (u + 1))
                dve.wait_ge(sum_ready, g * (2 * DEEP) + (2 * u + 2))
                dve.scalar_tensor_tensor(o_out[:, u, :], h_in[:, u, :], f_inv[:, u:u + 1], final_gain, ALU.mult, ALU.mult).then_inc(out_ready, 1)

            def final_step(g, u):
                sum_tile(g, u)
                if u > 0:
                    norm_out(g, u - 1)
                elif not is_zero(g):
                    norm_out(g - 1, DEEP - 1)

            final_tiles(dve, final_step)
            norm_out(TILES // DEEP - 1, DEEP - 1)

        @block.tensor
        def _(pe):
            pe.wait_ge(ident_built, 1)

            def turn(dst, src, inc=None):
                ins = pe.transpose(dst, src, ident[:, :])
                if inc is not None:
                    ins.then_inc(inc, 1)

            def transpose_tile(g, u):
                n = g * 4 + u
                pe.wait_ge(norm_ready, n + 1)
                hold(pe, xT_low, n - 1)
                for k in range(KD):
                    turn(psum[2 * (u % 2) + k // 4][:, (k % 4) * P:(k % 4 + 1) * P], x_norm[:, u % 2, k * P:(k + 1) * P],
                         x_transposed if k % 4 == 3 else None)

            norm_tiles(transpose_tile)(pe)
            pe.wait_ge(xT_low, XT)

            def gate_logits(m):
                u, (h, s) = m % 2, GATE_JOBS[m]
                if m >= 2:
                    pe.wait_ge(gate_min[u], m // 2)
                    pe.wait_ge(gate_log[u], m // 2 * 3)
                if m == 0:
                    pe.wait_ge(small_loaded, 16 * 6)
                pe.matmul(psum[2 + u][:, :], w_gate[:, h * P:(h + 1) * P], rT[:, s * 512:s * 512 + 512],
                          start=True, stop=True).then_inc(gate_filled[u], 1)

            PASSES = ((0, 0), (0, 1), (1, 0))

            def products(n, kh, b):
                bank, kind = psum[4 + b], kind_of(n)
                g, half = b // 2, slice(b % 2 * 512, b % 2 * 512 + 512)

                def w(c):
                    return lambda part, k: pieces[:, kh, part, k, c]

                def x(c, of=xT):
                    return lambda part, k: of[:, part, kh * HK + k, c]

                if kind == "mem_k":
                    return [(bank[:, 0:N_MEM], w(slice(b * P, (b + 1) * P)), x(slice(0, N_MEM), memT))]
                if kind == "mem_v":
                    return [(bank[:, 0:MEMW], x(slice((b - 2) * P, (b - 1) * P), memT), w(slice(0, MEMW)))]
                if kind == "rank":
                    return [(bank[:, :], w(slice(0, P)), x(half))]
                if kind != "vg":
                    return [(bank[:, :], w(slice(g * P, (g + 1) * P)), x(half))]
                return [(cols(4 + b, 512, 2)[:, e, :], x(slice((2 * b + e) * P, (2 * b + e + 1) * P)), w(slice(0, UNIT))) for e in range(2)]

            def unit_pe(n):
                for kh in range(2):
                    if gate_at(n, kh) is not None:
                        gate_logits(gate_at(n, kh))
                    pe.wait_ge(piece_low[kh], n + 1)
                    for b in banks_of(n):
                        if kh == 0:
                            hold(pe, job_drained[b], fills(n, b))
                        parts_of_bank = products(n, kh, b)
                        for e, (o, stationary, moving) in enumerate(parts_of_bank):
                            for k in range(HK):
                                for a, c in PASSES:
                                    ins = pe.matmul(o, stationary(a, k), moving(c, k), start=(kh == 0 and e == 0 and k == 0 and a + c == 0),
                                                    stop=(kh == 1 and e == len(parts_of_bank) - 1 and k == HK - 1 and a == 1))
                        if kh == 1:
                            ins.then_inc(job_filled[b], 1)
                    if kh == 0:
                        ins.then_inc(first_piece_used, 1)

            all_units(pe, unit_pe)

            for b in range(4):
                pe.wait_ge(job_drained[b], fills(ALL_UNITS, b))
            for u in range(2):
                pe.wait_ge(gate_summed[u], len(GATE_JOBS) // 2)
            pe.wait_ge(state_zero, 1)

            def use(bank, tile, k):
                hold(pe, drained[bank], tile * USES[bank] + k)

            def out_projection(s):
                pe.wait_ge(drained[7], s * 3 + 1)
                pe.wait_ge(drained[3], s * 3 + 2)
                pe.wait_ge(drained[6], s * 2 + 2)
                use(2, s, 1)
                for b in (2, 3):
                    for k in range(KD):
                        ins = pe.matmul(psum[b][:, :], catT[:, k, :], w_out_half[b - 2][:, k, :], start=(k == 0), stop=(k == KD - 1))
                        if k == KD - 1:
                            ins.then_inc(filled[b], 1)
                        yield

            PROJECTION_STEPS = (0, 0, 4, 4, 2, 2, 2, 2)
            assert sum(PROJECTION_STEPS) == 2 * KD

            def mix_pe(t, s):
                mix_flat = mix[:, :, :].rearrange("p h d -> p (h d)")
                if t is not None:
                    v_t = vg[:, one_tile(t), 0:MIX].rearrange("p a (h d) -> p (a h) d", h=HEADS)
                    pe.wait_ge(fac_used[0], t * 3 + 1)
                    use(6, t, 0)
                    for h in range(HEADS):
                        turn(heads_of(6)[:, h, :], k_decayed[:, h, :], filled[6] if h == HEADS - 1 else None)
                    pe.wait_ge(mq_ready, t + 1)
                    for b in (4, 5):
                        use(b, t, 0)
                        part = slice((b - 4) * MHD, (b - 3) * MHD)
                        for e in range(2):
                            ins = pe.matmul(cols(b, 512, 2)[:, e, :], mq_tile[part, e, :], mem_kT[part, e, :], start=True, stop=True)
                        ins.then_inc(filled[b], 1)
                if t is not None:
                    chunk_scores(t, 0)
                    chunk_scores(t, 1)
                if s is not None:
                    pe.wait_ge(mix_ready, s + 1)
                    use(7, s, 0)
                    for k in range(4):
                        turn(heads_of(7)[:, k, :], mix_flat[:, k * P:(k + 1) * P], filled[7] if k == 3 else None)
                    use(3, s, 1)
                    for k in (4, 5):
                        turn(heads_of(3)[:, k - 4, :], mix_flat[:, k * P:(k + 1) * P], filled[3] if k == 5 else None)
                    pieces = out_projection(s)
                for lvl in range(2, LEVELS + 1):
                    if t is not None:
                        chunk_scores(t, lvl)
                        if lvl == 5:
                            pe.wait_ge(probs_ready, t + 1)
                            for b in (4, 5):
                                use(b, t, 1)
                                for n in range(4):
                                    place, m = 2 * (b - 4) + n // 2, n % 2
                                    turn(heads_of(b)[:, n, :], probs[:, place, m * P:(m + 1) * P], filled[b] if n == 3 else None)
                    if s is not None:
                        for _ in range(PROJECTION_STEPS[lvl]):
                            next(pieces, None)
                if t is not None:
                    pe.wait_ge(drained[4], t * 3 + 2)
                    pe.wait_ge(drained[5], t * 3 + 2)
                    use(6, t, 1)
                    for place in range(MHEADS):
                        h = 2 * (place % 2) + place // 2
                        o = psum[6][(h % 2) * MHD:(h % 2 + 1) * MHD, (h // 2) * P:(h // 2 + 1) * P]
                        for m in range(MTILES):
                            ins = pe.matmul(o, mem_v[:, m, h * MHD:(h + 1) * MHD], probsT[:, place, m, :], start=(m == 0), stop=(m == MTILES - 1))
                    ins.then_inc(filled[6], 1)
                    for b in (4, 5):
                        for e in range(2):
                            h = 2 * (b - 4) + e
                            ins = pe.matmul(cols(b, 2 * DV, 2)[:, e, :], k_decayedT[:, h, :], v_t[:, h, :], start=True, stop=True)
                        ins.then_inc(filled[b], 1)
                if s is not None:
                    pe.wait_ge(u_ready, s + 1)
                    use(7, s, 1)
                    for k in range(4):
                        turn(heads_of(7)[:, k, :], u_tile[:, k * P:(k + 1) * P], filled[7] if k == 3 else None)
                    use(2, s, 2)
                    for k in range(4, 8):
                        turn(heads_of(2)[:, k - 4, :], u_tile[:, k * P:(k + 1) * P], filled[2] if k == 7 else None)
                if t is not None:
                    for b in (0, 1):
                        pe.wait_ge(drained[b], t * 4 + 4)
                    pe.wait_ge(fac_used[1], t * 3 + 1)
                    hold(pe, drained[5], t * 3)
                    for b in (3, 2):
                        use(b, t, 0)
                        for e in range(2):
                            h = 2 * (b - 2) + e
                            o = cols(b, 2 * DV, 2)[:, e, :]
                            pe.matmul(o, scoresT[:, h, :], v_t[:, h, :], start=True, stop=False)
                            ins = pe.matmul(o, q_decayed[:, h, :], state[:, h, :], start=False, stop=True)
                        ins.then_inc(filled[b], 1)
                if s is not None:
                    pe.wait_ge(drained[7], s * 3 + 2)
                    pe.wait_ge(drained[2], s * 3 + 3)
                    for k in range(KD):
                        ins = pe.matmul(psum[7][:, 0:G + E], uT[:, k, :], w_route[:, k, :], start=(k == 0), stop=(k == KD - 1))
                    ins.then_inc(filled[7], 1)

            def chunk_scores(t, lvl):
                b = lvl % 2
                if lvl < LEVELS:
                    f = lvl + 2
                    pe.wait_ge(fac_used[f % 3], t * 3 + (f // 3 + 1))
                else:
                    pe.wait_ge(kd_ready, t + 1)
                use(b, t, lvl // 2)
                for h in range(HEADS):
                    moving = qk[:, b, h, :] if lvl < LEVELS else qT[:, h, at_tile(t)]
                    ins = pe.matmul(heads_of(b)[:, h, :], qk[:, b, h, :], moving, start=True, stop=True)
                ins.then_inc(filled[b], 1)

            mix_pe(0, None)
            pe.wait_ge(w_out_loaded, 32)
            mix_pe(1, 0)
            with pe.Fori(2, TILES) as t:
                mix_pe(t, t - 1)
            mix_pe(None, TILES - 1)

            pe.wait_ge(member_ready, 1)
            pe.wait_ge(drained[0], TILES * USES[0])
            pe.wait_ge(drained[1], TILES * USES[1])
            flat = member.rearrange("p t e -> p (t e)")
            pe.matmul(psum[0][:, 0:TE], tri, flat, start=True, stop=True)
            pe.matmul(psum[1][:, 0:TE], ones, flat, start=True, stop=True).then_inc(rank_filled, 1)
            for n in range(2 * TILES):
                pe.wait_ge(hot_ready, n + 1)
                pe.wait_ge(block_hot_ready, n + 1)
                ins = pe.matmul(psum[2][:, 0:COLS], row_hot[n % 2], block_hot[n % 2], start=(n == 0), stop=(n == 2 * TILES - 1))
                ins.then_inc(hot_used if n < 2 * TILES - 1 else table_filled, 1)
            pe.wait_ge(tokens_ready, 1)

            def rows_transposed(i, u):
                pe.wait_ge(gathered[u], i * 16 + 16)
                hold(pe, rowsT_low, number(i, u))
                for b in range(2):
                    for k in range(4 * b, 4 * b + 4):
                        turn(heads_of(b)[:, k - 4 * b, :], rows[u][:, k * P:(k + 1) * P], rows_filled[b] if k == 4 * b + 3 else None)

            def weights_split(e, p):
                pe.wait_ge(part_low_dve[p], e + 1)
                pe.wait_ge(part_low_pool[p], e + 1)

            def up_product(i, u, e, between):
                pe.wait_ge(rowsT_low, number(i, u) + 1)
                hold(pe, hid_ready, number(i, u) - 1)
                for p in range(2):
                    weights_split(e, p)
                    for k in range(KD // 2):
                        for a, b in PASSES:
                            ins = pe.matmul(psum[2 + 4 * u][:, :], rowsT[u][:, a, p * KD // 2 + k, :],
                                            slot_of(p, b, slice(k * 2 * FF, (k + 1) * 2 * FF), e),
                                            start=(p == 0 and k == 0 and a + b == 0), stop=(p == 1 and k == KD // 2 - 1 and a == 1))
                    ins.then_inc(part_used[p], 1)
                    if p == 0:
                        between()

            def hid_transposed(i, u):
                pe.wait_ge(hid_ready, number(i, u) + 1)
                hold(pe, hidT_low, number(i, u))
                for k in range(KF):
                    turn(psum[3][:, k * P:(k + 1) * P], hid[u][:, k * P:(k + 1) * P], hidT_filled if k == KF - 1 else None)

            def down_product(i, u, e):
                pe.wait_ge(hidT_low, number(i, u) + 1)
                hold(pe, y_left, number(i, u))
                hold(pe, y_right, number(i, u))
                weights_split(e, 2)
                for n in range(2):
                    for k in range(KF):
                        for a, b in PASSES:
                            ins = pe.matmul(psum[4 + n][:, :], hidT[:, u, a, k, :], slot_of(2, b, slice(k * D + n * 512, k * D + n * 512 + 512), e),
                                            start=(k == 0 and a + b == 0), stop=(k == KF - 1 and a == 1))
                ins.then_inc(part_used[2], 1)

            def step_pe(i, u):
                before, first, _ = plan_of(pe, i, u)
                if is_zero(number(i, u)):
                    up_product(i, u, 0, lambda: None)
                else:
                    up_product(i, u, before + first, lambda: hid_transposed(*behind(i, u)))
                rows_transposed(*ahead(i, u))
                if not is_zero(number(i, u)):
                    down_product(*behind(i, u), before)

            rows_transposed(0, 0)
            pe.wait_ge(tables_ready, 1)
            more = all_pairs(pe, step_pe)
            last = more + (FIXED - 1)
            hid_transposed(last, 1)
            down_product(last, 1, EXPERTS - 1)


INS = ["x", "mem", "mix_norm", "ffn_norm", "mem_norm", "final_norm", "gla_w_in", "gla_w_gate_up",
       "gla_b_gate", "gla_out_norm", "w_mem_kv", "w_out", "w_group", "b_group", "w_router", "b_router",
       "w_up", "w_down"]


def kernel(**inputs):
    import numpy as np
    import concourse.bacc as bacc
    from concourse import mybir as mb
    from concourse.bass_utils import run_bass_kernel_spmd

    nc = bacc.Bacc("TRN2", target_bir_lowering=False, num_devices=1)
    arrays, args = {}, []
    for name in INS:
        a = np.ascontiguousarray(inputs[name])
        arrays[f"in_{name}"] = a
        args.append(nc.dram_tensor(f"in_{name}", a.shape, mb.dt.from_np(a.dtype), kind="ExternalInput").ap())
    shape = tuple(inputs["x"].shape)
    args.append(nc.dram_tensor("out_rows", shape, mb.dt.float32, kind="ExternalOutput").ap())
    hybrid_layer(nc, *args)
    r = run_bass_kernel_spmd(nc, [arrays], core_ids=[0])
    return r.results[0]["out_rows"]
```
